# Optimizing a Trainium2 kernel written in Bass

```python
import math
import jax, jax.numpy as jnp
from jax import lax
import numpy as np

D_MODEL = 1024
BATCH = 1
SEQ = 1024
DEPTH = 1

HEAD_DIM = 64
CONV_WIDTH = D_MODEL // 2
CONV_K = 3
N_Q_HEADS = (D_MODEL // 2) // HEAD_DIM
N_KV_HEADS = 2
Q_PER_KV = N_Q_HEADS // N_KV_HEADS
ATTN_WIDTH = N_Q_HEADS * HEAD_DIM
KV_WIDTH = N_KV_HEADS * HEAD_DIM
MIX_WIDTH = CONV_WIDTH + ATTN_WIDTH
IN_WIDTH = 3 * CONV_WIDTH + ATTN_WIDTH + 2 * KV_WIDTH
WINDOW = 128
BLOCK = 128
N_BUCKETS = 32
MAX_DISTANCE = 128
N_EXPERTS = 32
TOP_K = 4
D_FF = D_MODEL
SWIGLU_LIMIT = 7.0
SWIGLU_ALPHA = 1.702
MOE_BLOCK = 128
EPS = 1e-5

kernel_name = "hymba_conv_swa_sink_t5_moe_block"

def rms_norm(x, g):
    xf = x.astype(jnp.float32)
    y = xf * lax.rsqrt(jnp.mean(xf * xf, axis=-1, keepdims=True) + EPS)
    return (y * g.astype(jnp.float32)).astype(x.dtype)

def t5_bucket(rel):
    n = jnp.maximum(rel, 0)
    max_exact = N_BUCKETS // 2
    nf = jnp.maximum(n, 1).astype(jnp.float32)
    large = max_exact + (jnp.log(nf / max_exact) / math.log(MAX_DISTANCE / max_exact)
                         * (N_BUCKETS - max_exact)).astype(jnp.int32)
    large = jnp.minimum(large, N_BUCKETS - 1)
    return jnp.where(n < max_exact, n, large)

def causal_short_conv(u, conv_w):
    S = u.shape[1]
    up = jnp.pad(u, ((0, 0), (CONV_K - 1, 0), (0, 0)))
    y = conv_w[CONV_K - 1] * up[:, CONV_K - 1:CONV_K - 1 + S]
    for j in range(CONV_K - 1):
        y = y + conv_w[j] * up[:, j:j + S]
    return y

def sliding_window_attention(q, k, v, sinks, rel_bias):
    B, S = q.shape[0], q.shape[1]
    nb = S // BLOCK
    qb = q.reshape(B, nb, BLOCK, N_KV_HEADS, Q_PER_KV, HEAD_DIM)

    def with_prev(t):
        tb = t.reshape(B, nb, BLOCK, N_KV_HEADS, HEAD_DIM)
        prev = jnp.pad(tb[:, :-1], ((0, 0), (1, 0), (0, 0), (0, 0), (0, 0)))
        return jnp.concatenate([prev, tb], axis=2)

    kw, vw = with_prev(k), with_prev(v)
    scores = jnp.einsum('bnqkgd,bnskd->bnkgqs', qb, kw,
                        preferred_element_type=jnp.float32) * (HEAD_DIM ** -0.5)

    qi = jnp.arange(BLOCK, dtype=jnp.int32)
    kj = jnp.arange(2 * BLOCK, dtype=jnp.int32)
    rel = qi[:, None] + BLOCK - kj[None, :]
    bias = rel_bias.astype(jnp.float32)[t5_bucket(rel)]
    bias = jnp.transpose(bias, (2, 0, 1)).reshape(N_KV_HEADS, Q_PER_KV, BLOCK, 2 * BLOCK)

    in_window = (rel >= 0) & (rel < WINDOW)
    key_pos = jnp.arange(nb, dtype=jnp.int32)[:, None] * BLOCK - BLOCK + kj[None, :]
    mask = in_window[None] & (key_pos >= 0)[:, None, :]

    logits = jnp.where(mask[None, :, None, None], scores + bias[None, None], -jnp.inf)
    sink = sinks.astype(jnp.float32).reshape(1, 1, N_KV_HEADS, Q_PER_KV, 1, 1)
    m = jnp.maximum(jnp.max(logits, axis=-1, keepdims=True), sink)
    p = jnp.exp(logits - m)
    denom = jnp.sum(p, axis=-1, keepdims=True) + jnp.exp(sink - m)
    out = jnp.einsum('bnkgqs,bnskd->bnqkgd', (p / denom).astype(v.dtype), vw)
    return out.reshape(B, S, ATTN_WIDTH)

def clamped_swiglu(hid):
    x_glu, x_lin = hid[..., ::2], hid[..., 1::2]
    x_glu = jnp.minimum(x_glu, SWIGLU_LIMIT)
    x_lin = jnp.clip(x_lin, -SWIGLU_LIMIT, SWIGLU_LIMIT)
    return x_glu * jax.nn.sigmoid(SWIGLU_ALPHA * x_glu) * (x_lin + 1.0)

def moe_ffn(h, w_router, b_router, w1, b1, w2, b2):
    T = h.shape[0]
    logits = jnp.matmul(h, w_router, preferred_element_type=jnp.float32) + b_router.astype(jnp.float32)
    top_vals, top_idx = lax.top_k(logits, TOP_K)
    gates = jax.nn.softmax(top_vals, axis=-1)

    e_flat = top_idx.reshape(-1).astype(jnp.int32)
    tok_flat = jnp.repeat(jnp.arange(T, dtype=jnp.int32), TOP_K)
    g_flat = gates.reshape(-1)
    order = jnp.argsort(e_flat, stable=True)
    e_s, tok_s, g_s = e_flat[order], tok_flat[order], g_flat[order]

    counts = jnp.bincount(e_flat, length=N_EXPERTS).astype(jnp.int32)
    starts = jnp.cumsum(counts) - counts
    padded = (counts + MOE_BLOCK - 1) // MOE_BLOCK * MOE_BLOCK
    pad_ends = jnp.cumsum(padded)
    pad_starts = pad_ends - padded
    dest = pad_starts[e_s] + (jnp.arange(T * TOP_K, dtype=jnp.int32) - starts[e_s])

    n_blocks = -(-(T * TOP_K + N_EXPERTS * MOE_BLOCK) // MOE_BLOCK)
    n_slots = n_blocks * MOE_BLOCK
    slot_tok = jnp.zeros((n_slots,), jnp.int32).at[dest].set(tok_s)
    slot_gate = jnp.zeros((n_slots,), jnp.float32).at[dest].set(g_s)
    block_start = jnp.arange(n_blocks, dtype=jnp.int32) * MOE_BLOCK
    block_expert = jnp.minimum(jnp.searchsorted(pad_ends, block_start, side='right'),
                               N_EXPERTS - 1).astype(jnp.int32)

    def expert_block(args):
        toks, gts, e = args
        xb = h[toks]
        hid = xb @ w1[e] + b1[e]
        yb = clamped_swiglu(hid) @ w2[e] + b2[e]
        return yb * gts[:, None].astype(yb.dtype)

    y_slots = lax.map(expert_block, (slot_tok.reshape(n_blocks, MOE_BLOCK),
                                     slot_gate.reshape(n_blocks, MOE_BLOCK), block_expert))
    y_slots = y_slots.reshape(n_slots, h.shape[-1])
    return jnp.zeros_like(h).at[slot_tok].add(y_slots.astype(h.dtype))

def setup_inputs(seed: int = 0) -> dict:
    key = jax.random.key(seed)
    ks = jax.random.split(key, 20)
    f32 = jnp.float32
    nrm = lambda k, shape, s: jax.random.normal(k, shape, f32) * s
    return {
        "x": nrm(ks[0], (BATCH, SEQ, D_MODEL), 1.0),
        "norm_mix": 1.0 + nrm(ks[1], (DEPTH, D_MODEL), 0.02),
        "w_in": nrm(ks[2], (DEPTH, D_MODEL, IN_WIDTH), D_MODEL ** -0.5),
        "b_in": nrm(ks[3], (DEPTH, IN_WIDTH), 0.02),
        "conv_w": nrm(ks[4], (DEPTH, CONV_K, CONV_WIDTH), CONV_K ** -0.5),
        "q_norm": 1.0 + nrm(ks[5], (DEPTH, HEAD_DIM), 0.02),
        "k_norm": 1.0 + nrm(ks[6], (DEPTH, HEAD_DIM), 0.02),
        "sinks": nrm(ks[7], (DEPTH, N_Q_HEADS), 1.0),
        "rel_bias": nrm(ks[8], (N_BUCKETS, N_Q_HEADS), 0.1),
        "out_norm_conv": 1.0 + nrm(ks[9], (DEPTH, CONV_WIDTH), 0.02),
        "out_norm_attn": 1.0 + nrm(ks[10], (DEPTH, ATTN_WIDTH), 0.02),
        "w_out": nrm(ks[11], (DEPTH, MIX_WIDTH, D_MODEL), MIX_WIDTH ** -0.5),
        "b_out": nrm(ks[12], (DEPTH, D_MODEL), 0.02),
        "norm_ffn": 1.0 + nrm(ks[13], (DEPTH, D_MODEL), 0.02),
        "w_router": nrm(ks[14], (DEPTH, D_MODEL, N_EXPERTS), D_MODEL ** -0.5),
        "b_router": nrm(ks[15], (DEPTH, N_EXPERTS), 0.01),
        "w1": nrm(ks[16], (DEPTH, N_EXPERTS, D_MODEL, 2 * D_FF), D_MODEL ** -0.5),
        "b1": nrm(ks[17], (DEPTH, N_EXPERTS, 2 * D_FF), 0.02),
        "w2": nrm(ks[18], (DEPTH, N_EXPERTS, D_FF, D_MODEL), D_FF ** -0.5),
        "b2": nrm(ks[19], (DEPTH, N_EXPERTS, D_MODEL), 0.02),
    }

def reference(x, norm_mix, w_in, b_in, conv_w, q_norm, k_norm, sinks, rel_bias,
              out_norm_conv, out_norm_attn, w_out, b_out, norm_ffn,
              w_router, b_router, w1, b1, w2, b2):
    B, S, D = x.shape
    cuts = [CONV_WIDTH, 2 * CONV_WIDTH, 3 * CONV_WIDTH, 3 * CONV_WIDTH + ATTN_WIDTH,
            3 * CONV_WIDTH + ATTN_WIDTH + KV_WIDTH]
    for l in range(DEPTH):
        h = rms_norm(x, norm_mix[l])
        proj = h @ w_in[l] + b_in[l]
        b_gate, c_gate, u, q, k, v = jnp.split(proj, cuts, axis=-1)

        y_conv = b_gate * causal_short_conv(c_gate * u, conv_w[l])

        q = rms_norm(q.reshape(B, S, N_Q_HEADS, HEAD_DIM), q_norm[l])
        k = rms_norm(k.reshape(B, S, N_KV_HEADS, HEAD_DIM), k_norm[l])
        v = v.reshape(B, S, N_KV_HEADS, HEAD_DIM)
        y_attn = sliding_window_attention(q, k, v, sinks[l], rel_bias)

        mix = jnp.concatenate([rms_norm(y_conv, out_norm_conv[l]),
                               rms_norm(y_attn, out_norm_attn[l])], axis=-1)
        x = x + mix @ w_out[l] + b_out[l]

        h2 = rms_norm(x, norm_ffn[l]).reshape(B * S, D)
        x = x + moe_ffn(h2, w_router[l], b_router[l], w1[l], b1[l], w2[l], b2[l]).reshape(B, S, D)
    return x


_drawn_inputs = setup_inputs


def setup_inputs(seed=0):
    import zlib

    import numpy as np

    out = dict(_drawn_inputs(seed))
    spreads = {}
    factors = {'sinks': 5.325, 'b1': 6.852, 'b2': 7.921}
    for name, (base, spread) in spreads.items():
        noise = np.random.default_rng([zlib.crc32(name.encode()), seed]).standard_normal(out[name].shape)
        drawn = base * np.exp(spread * noise) if base else spread * noise
        out[name] = __import__('jax').numpy.asarray(drawn.astype(out[name].dtype))
    for name, factor in factors.items():
        out[name] = (out[name] * factor).astype(out[name].dtype)
    return out
```

```python
from contextlib import ExitStack

import numpy as np
import concourse.bass as bass
from concourse import mybir

ALU = mybir.AluOpType
ACT = mybir.ActivationFunctionType
F32 = mybir.dt.float32
BF16 = mybir.dt.bfloat16
I32 = mybir.dt.int32
U32 = mybir.dt.uint32
AX_X = mybir.AxisListType.X

P = 128
D = 1024
S = 1024
NB = S // P
KD = D // P
CW = 512
CC = CW // P
HD = 64
NH = 8
NKV = 2
AW = NH * HD
KVW = NKV * HD
QKV0 = 3 * CW
IN_W = 3 * CW + AW + 2 * KVW
NBUCKET = 32
MAX_DISTANCE = 128
NE = 32
TOP_K = 4
FF = 1024
LIMIT = 7.0
ALPHA = 1.702
EPS = 1e-5
MASKED = -1e30

CAP = 256
SIZES = (64, 80, 96, 112, 128, 144, 160, 176, 192, 208, 256)
PIECES = 12
P1 = 8
PW = 256
REL_W = 384

C_ID, C_TRI, C_IOTA, C_ONES, C_E, C_PART, C_TOK, C_HOT = 0, 128, 256, 512, 640, 672, 673, 689
C_MASK = C_HOT + REL_W
C_FLIP = C_MASK + REL_W
C_W = C_FLIP + P


def constants():
    c = np.zeros((P, C_W), np.float32)
    p = np.arange(P)
    c[:, C_ID:C_ID + P] = np.eye(P)
    c[:, C_TRI:C_TRI + P] = p[:, None] < p[None, :]
    c[:, C_IOTA:C_IOTA + CAP] = np.arange(CAP)
    c[:, C_ONES:C_ONES + P] = 1.0
    c[:, C_E:C_E + NE] = np.arange(NE)
    c[:, C_PART] = p
    tok = p[:, None] + P * np.arange(NB)[None, :]
    c[:, C_TOK:C_TOK + NB] = tok // 32
    c[:, C_TOK + NB:C_TOK + 2 * NB] = tok % 32
    half = NBUCKET // 2
    rel = 255 - np.arange(REL_W)
    n = np.maximum(rel, 1).astype(np.float32)
    large = half + (np.log(n / half) / np.log(MAX_DISTANCE / half) * (NBUCKET - half)).astype(np.int32)
    bucket = np.where(rel < half, np.maximum(rel, 0), np.minimum(large, NBUCKET - 1))
    c[:NBUCKET, C_HOT:C_HOT + REL_W] = bucket[None, :] == np.arange(NBUCKET)[:, None]
    c[:, C_MASK:C_MASK + REL_W] = np.where((rel >= 0) & (rel < P), 0.0, MASKED)[None, :]
    c[:, C_FLIP:C_FLIP + P] = np.eye(P)[::-1]
    return c


class Event:

    def __init__(self, sem, unit=1, credit=0):
        self.sem, self.unit, self.credit = sem, unit, credit

    def of(self, t):
        n = t + (1 + self.credit)
        return n if self.unit == 1 else n * self.unit


class Steps:

    def __init__(self, sem, per):
        self.sem, self.per, self.n = sem, per, 0

    def did(self, ins):
        ins.then_inc(self.sem, 1)
        self.n += 1

    def value(self, t):
        return t * self.per + self.n


def clear_sems(nc, sems):
    numbers = sorted(s.num for s in sems)
    assert numbers == list(range(numbers[0], numbers[-1] + 1))
    nc.all_engine_barrier(sems_to_clear=range(numbers[0], numbers[-1] + 1))


def slot(h):
    return (h % 2) * (NH // 2) + h // 2


def mixer(nc, x_rows, out_rows, h2_rows, rel_rows, norm_mix, w_in, b_in, conv_w, q_norm, k_norm, sinks,
          rel_bias, out_norm_conv, out_norm_attn, w_out, b_out, norm_ffn, w_router, b_router, const,
          cst, picked, gates):
    ident = cst[:, C_ID:C_ID + P]
    with ExitStack() as ctx:
        def sb(name, shape, dt=F32):
            return ctx.enter_context(nc.sbuf_tensor(name, shape, dt))

        def ps(name, shape):
            return ctx.enter_context(nc.psum_tensor(name, shape, F32))

        all_sems = []

        def sem(name):
            all_sems.append(ctx.enter_context(nc.semaphore(name)))
            return all_sems[-1]

        credited = []

        def event(name, unit=1, credit=0):
            e = Event(sem(name), unit, credit)
            if credit:
                credited.append(e)
            return e

        w_in_sb = sb("w_in_sb", [P, KD, IN_W])
        w_out_sb = sb("w_out_sb", [P, KD, D])
        w_router_sb = sb("w_router_sb", [P, KD, NE])
        norm_ffn_row = sb("norm_ffn_row", [P, D])
        vectors = sb("vectors", [P, 42])
        norm_mix_col = vectors[:, 0:8]
        b_in_col = vectors[:, 8:20]
        conv_w_col = vectors[:, 20:32].rearrange("p (j c) -> p j c", j=3)
        conv_g_col = vectors[:, 32:36]
        attn_g_col = vectors[:, 36:40]
        q_norm_col = vectors[:, 40:41]
        k_norm_col = vectors[:, 41:42]
        b_qkv_row = sb("b_qkv_row", [P, AW + 2 * KVW])
        b_out_row = sb("b_out_row", [P, D])
        b_router_row = sb("b_router_row", [P, NE])
        q_scale_col = sb("q_scale_col", [P, 1])
        sink_row = sb("sink_row", [P, NH])
        rel_bias_sb = sb("rel_bias_sb", [NBUCKET, NH])
        rel_bias_slots = sb("rel_bias_slots", [NBUCKET, NH])
        sink_slots = sb("sink_slots", [P, NH])
        minus_half = sb("minus_half", [P, NH + NKV])
        bias_prev = sb("bias_prev", [P, NH, P])
        bias_all = sb("bias_all", [P, NH, 2 * P])

        x_in = sb("x_in", [P, D])
        x_res = sb("x_res", [P, D])
        junk = sb("junk", [P, D])
        xn = sb("xn", [P, D])
        hT = sb("hT", [P, KD, P])
        qk = sb("qk", [P, AW + KVW])
        qk_sq = sb("qk_sq", [P, AW + KVW])
        qn = sb("qn", [P, AW])
        kn = sb("kn", [P, NKV, 2, HD])
        qT = sb("qT", [P, NH // 2, P])
        kT = sb("kT", [P, NKV, 2, P])
        v_keys = sb("v_keys", [P, 2, KVW])
        conv_u = sb("conv_u", [P, 2, P])
        conv_x = sb("conv_x", [P, CC, P + 2])
        conv_t = sb("conv_t", [P, 3, P])
        conv_y = sb("conv_y", [P, CC, P])
        conv_sq = sb("conv_sq", [P, CC, P])
        conv_s = sb("conv_s", [P, CC, P])
        probs = sb("probs", [P, NH, 2 * P])
        pT = sb("pT", [P, 2, 2 * P])
        attn = sb("attn", [P, AW])
        attnT = sb("attnT", [P, CC, P])
        x1 = sb("x1", [P, D])
        h2 = sb("h2", [P, D])
        h2T = sb("h2T", [P, KD, P])
        small = sb("small", [P, 160])
        rel_const = junk[:, 0:2 * REL_W + P]
        vector_rows = xn[0:42, 0:P]
        rel_row = h2T[:].rearrange("p k q -> p (k q)")[0:NH, 0:REL_W]
        best_i = sb("best_i", [P, 8], U32)
        hot = sb("hot", [P, TOP_K, NE])
        hot_g = sb("hot_g", [P, TOP_K, NE])
        used = [0]

        def cols(n):
            used[0] += n
            return small[:, used[0] - n:used[0]]

        ss_x, ms_x, rstd_x = cols(1), cols(1), cols(1)
        ss_qk, ms_qk, rstd_qk = cols(NH + NKV), cols(NH + NKV), cols(NH + NKV)
        top, neg_top, sink_gap, sink_exp = cols(NH), cols(NH), cols(NH), cols(NH)
        row_sum, denom, rdenom = cols(NH), cols(NH), cols(NH)
        ss_ca, ms_ca, rstd_ca = cols(2), cols(2), cols(2)
        ss_f, ms_f, rstd_f = cols(1), cols(1), cols(1)
        best, neg_best, best_f = cols(8), cols(1), cols(8)
        exp4, sum4, rsum4, gate4 = cols(TOP_K), cols(1), cols(1), cols(TOP_K)
        route_sc = sb("route_sc", [P, NE])

        ps_q = ps("ps_q", [P, 512])
        ps_kv = ps("ps_kv", [P, 512])
        ps_c = ps("ps_c", [P, 2, 512])
        ps_s = ps("ps_s", [P, 2048])
        ps_heads = ps_s[:].rearrange("p (h k) -> p h k", h=NH)
        ps_route = ps_s[:, 1024:1024 + NE]

        setup_loaded = sem("setup_loaded")
        qkv_w_loaded = sem("qkv_w_loaded")
        conv_w_loaded = sem("conv_w_loaded")
        out_w_loaded = sem("out_w_loaded")
        cleared = sem("buffers_cleared")
        scale_made = sem("scale_made")
        slots_made = sem("slots_made")
        rel_summed = sem("rel_summed")
        vectors_turned = sem("vectors_turned")
        vectors_ready = sem("vectors_ready")
        rel_made = sem("rel_made")
        rel_stored = sem("rel_stored")
        bias_loaded = sem("bias_loaded")
        bias_turned = sem("bias_turned")
        bias_flipped = sem("bias_flipped")
        x_loaded = event("x_loaded", 16)
        x_squared = event("x_squared")
        x_mean = event("x_mean")
        x_rstd = event("x_rstd")
        x_normed = event("x_normed")
        x_turned = [event("x_turned_a"), event("x_turned_b")]
        hT_ready = [event("hT_ready_a"), event("hT_ready_b")]
        qkv_done = event("qkv_done")
        qk_ready = event("qk_ready")
        v_shifted = event("v_shifted")
        v_ready = event("v_ready")
        qk_squared = event("qk_squared")
        qk_summed = event("qk_summed")
        qk_mean = event("qk_mean")
        qk_rstd = event("qk_rstd")
        qk_normed = event("qk_normed")
        conv_done = [event(f"conv_done{c}") for c in range(CC)]
        u_ready = [event(f"u_ready{c}") for c in range(CC)]
        conv_out = [event(f"conv_out{c}", 1, 1) for c in range(CC)]
        conv_squared = event("conv_squared")
        conv_scaled = event("conv_scaled")
        conv_summed = event("conv_summed")
        qk_turned = event("qk_turned")
        k_shifted = event("k_shifted")
        qT_ready = event("qT_ready")
        scored = event("scored")
        biased = event("biased")
        bias_switched = event("bias_switched", 1, 1)
        neg_ready = event("neg_ready")
        exped = [event(f"exped{h}") for h in range(NH)]
        sink_exped = event("sink_exped")
        p_turned = [event(f"p_turned{h}") for h in range(NH)]
        pT_ready = [event(f"pT_ready{h}") for h in range(NH)]
        av_done = [event(f"av_done{h}", 1, 1) for h in range(NH)]
        attn_ready = event("attn_ready")
        attn_squared = event("attn_squared")
        attn_turned = event("attn_turned")
        attnT_ready = event("attnT_ready")
        ca_mean = event("conv_attn_mean")
        ca_rstd = event("conv_attn_rstd")
        res_loaded = event("res_loaded", 16)
        res_biased = event("res_biased")
        conv_mixed = event("conv_mixed")
        attn_mixed = event("attn_mixed")
        x1_ready = event("x1_ready", 1, 1)
        x1_squared = event("x1_squared")
        f_mean = event("ffn_mean")
        f_rstd = event("ffn_rstd")
        h2_ready = event("h2_ready")
        h2_turned = [event("h2_turned_a"), event("h2_turned_b")]
        h2T_ready = [event("h2T_ready_a"), event("h2T_ready_b")]
        routed = event("routed")
        logits_read = event("logits_read", 1, 1)
        stored = event("rows_stored", 32, 1)
        best_ready = event("best_ready")
        best_exped = event("best_exped")
        vstep = Steps(sem("vector_step"), 30)

        ctx.callback(clear_sems, nc, all_sems)
        block = ctx.enter_context(nc.Block())

        setups = [
            (vector_rows[0:8, :], norm_mix.rearrange("o (k p) -> (o k) p", p=P)),
            (vector_rows[8:20, :], b_in[:, 0:QKV0].rearrange("o (k p) -> (o k) p", p=P)),
            (vector_rows[20:32, :], conv_w.rearrange("o j (c p) -> (o j c) p", p=P)),
            (vector_rows[32:36, :], out_norm_conv.rearrange("o (k p) -> (o k) p", p=P)),
            (vector_rows[36:40, :], out_norm_attn.rearrange("o (k p) -> (o k) p", p=P)),
            (vector_rows[40:41, 0:HD], q_norm),
            (vector_rows[40:41, HD:P], q_norm),
            (vector_rows[41:42, 0:HD], k_norm),
            (vector_rows[41:42, HD:P], k_norm),
            (b_qkv_row[:], b_in[0, QKV0:IN_W].partition_broadcast(P)),
            (sink_row[:], sinks[0].partition_broadcast(P)),
            (rel_bias_sb[:], rel_bias),
            (b_out_row[:], b_out[0].partition_broadcast(P)),
            (norm_ffn_row[:], norm_ffn[0].partition_broadcast(P)),
            (b_router_row[:], b_router[0].partition_broadcast(P)),
            (w_router_sb[:], w_router[0].rearrange("(k p) e -> p k e", p=P)),
        ]
        all_setup = 16 * (2 + len(setups))

        def wait(eng, e, t):
            eng.wait_ge(e.sem, e.of(t))

        @block.sync
        def _(sp):
            w_rows = w_in[0].rearrange("(k p) n -> p k n", p=P)
            sp.dma_start(cst[:], const[:, 0:C_HOT]).then_inc(setup_loaded, 16)
            sp.dma_start(rel_const, const[:, C_HOT:C_W]).then_inc(setup_loaded, 16)
            sp.dma_start(x_in[:], x_rows[0:P, :]).then_inc(x_loaded.sem, 16)
            for dst, src in setups[:12]:
                sp.dma_start(dst, src).then_inc(setup_loaded, 16)
            sp.dma_start(w_in_sb[:, :, QKV0:IN_W], w_rows[:, :, QKV0:IN_W]).then_inc(qkv_w_loaded, 16)
            for dst, src in setups[12:]:
                sp.dma_start(dst, src).then_inc(setup_loaded, 16)
            for c in range(3):
                sp.dma_start(w_in_sb[:, :, c * CW:(c + 1) * CW],
                             w_rows[:, :, c * CW:(c + 1) * CW]).then_inc(conv_w_loaded, 16)
            sp.wait_ge(rel_stored, 16)
            slanted = bass.AP(tensor=rel_rows.tensor, offset=0, ap=[[1, P], [REL_W, NH], [1, 2 * P]])
            sp.dma_start(probs[:], slanted).then_inc(bias_loaded, 16)
            sp.dma_start(w_out_sb[:], w_out[0].rearrange("(k p) n -> p k n", p=P)).then_inc(out_w_loaded, 16)

            def load_block(n, rows):
                wait(sp, x_normed, n)
                sp.dma_start(x_in[:], rows).then_inc(x_loaded.sem, 16)

            def load_residual(t):
                wait(sp, x1_ready, t - 1)
                sp.dma_start(x_res[:], x_rows[bass.ds(t * P, P), :]).then_inc(res_loaded.sem, 16)

            with sp.Fori(0, NB - 1) as t:
                load_block(t, x_rows[bass.ds((t + 1) * P, P), :])
                load_residual(t)
            load_block(NB - 1, x_rows[(NB - 1) * P:NB * P, :])
            load_residual(NB - 1)

        @block.gpsimd
        def _(pool):
            for e in credited:
                pool.sem_inc(e.sem, e.unit * e.credit)
            nc.gpsimd.memset(minus_half[:], -0.5).then_inc(cleared, 1)
            nc.gpsimd.memset(v_keys[:], 0.0).then_inc(cleared, 1)
            nc.gpsimd.memset(kT[:], 0.0).then_inc(cleared, 1)
            nc.gpsimd.memset(conv_x[:], 0.0).then_inc(cleared, 1)
            nc.gpsimd.memset(bias_all[:, :, 0:P], MASKED).then_inc(cleared, 1)
            pool.wait_ge(rel_made, 1)
            pool.dma_start(rel_rows, rel_row).then_inc(rel_stored, 16)
            pool.wait_ge(cleared, 5)

            def rsqrt(mean, t, src, dst, done):
                wait(pool, mean, t)
                nc.gpsimd.tensor_tensor(dst, src, minus_half[:, 0:src.shape[1]], ALU.pow).then_inc(done.sem, 1)

            rsqrt(x_mean, 0, ms_x, rstd_x, x_rstd)
            rsqrt(qk_mean, 0, ms_qk, rstd_qk, qk_rstd)
            pool.wait_ge(setup_loaded, all_setup)
            pool.wait_ge(bias_flipped, 2)
            with pool.Fori(0, NB) as t:
                wait(pool, res_loaded, t)
                nc.gpsimd.tensor_tensor(x_res[:], x_res[:], b_out_row[:], ALU.add).then_inc(res_biased.sem, 1)
                wait(pool, biased, t)
                nc.gpsimd.tensor_tensor(bias_all[:, :, 0:P], bias_prev[:],
                                        cst[:, C_ONES:C_ONES + P].unsqueeze(1).broadcast_to([P, NH, P]),
                                        ALU.mult).then_inc(bias_switched.sem, 1)
                rsqrt(x_mean, t + 1, ms_x, rstd_x, x_rstd)
                rsqrt(ca_mean, t, ms_ca, rstd_ca, ca_rstd)
                rsqrt(f_mean, t, ms_f, rstd_f, f_rstd)
                rsqrt(qk_mean, t + 1, ms_qk, rstd_qk, qk_rstd)

        @block.scalar
        def _(act):
            def prepare(n):
                wait(act, x_loaded, n)
                nc.scalar.activation(junk[:], x_in[:], ACT.Square, accum_out=ss_x).then_inc(x_squared.sem, 1)
                wait(act, x_rstd, n)
                nc.scalar.activation(xn[:], x_in[:], ACT.Copy, scale=rstd_x).then_inc(x_normed.sem, 1)

            def square_qk(n):
                wait(act, qk_ready, n)
                nc.scalar.activation(qk_sq[:], qk[:], ACT.Square).then_inc(qk_squared.sem, 1)

            def add_u_bias(t, c):
                wait(act, conv_done[c], t)
                if c < 2:
                    wait(act, conv_out[c + 2], t - 1)
                else:
                    wait(act, conv_out[c - 2], t)
                nc.scalar.activation(conv_u[:, c % 2, :], ps_c[:, c % 2, 2 * P:3 * P], ACT.Identity,
                                     bias=b_in_col[:, 2 * CC + c:2 * CC + c + 1]).then_inc(u_ready[c].sem, 1)

            act.wait_ge(setup_loaded, all_setup)
            act.wait_ge(vectors_ready, 1)
            nc.scalar.activation(q_scale_col[:], q_norm_col, ACT.Copy, scale=HD ** -0.5).then_inc(scale_made, 1)
            act.wait_ge(bias_turned, 1)
            prepare(0)
            square_qk(0)
            act.wait_ge(scale_made, 1)
            act.wait_ge(cleared, 5)
            with act.Fori(0, NB) as t:
                add_u_bias(t, 0)
                add_u_bias(t, 1)
                wait(act, qk_turned, t)
                nc.scalar.copy(kT[:, :, 0, :], kT[:, :, 1, :]).then_inc(k_shifted.sem, 1)
                wait(act, k_shifted, t)
                nc.scalar.activation(kT[:, :, 1, :], ps_s[:, 512:512 + 2 * P].rearrange("p (v k) -> p v k", v=2),
                                     ACT.Copy, scale=k_norm_col)
                nc.scalar.activation(qT[:].rearrange("p h q -> p (h q)"), ps_s[:, 0:512],
                                     ACT.Copy, scale=q_scale_col[:]).then_inc(qT_ready.sem, 1)
                add_u_bias(t, 2)
                add_u_bias(t, 3)
                wait(act, neg_ready, t)
                for h in range(NH):
                    s = slot(h)
                    nc.scalar.activation(probs[:, s, :], probs[:, s, :], ACT.Exp, bias=neg_top[:, s:s + 1],
                                         accum_out=row_sum[:, s:s + 1]).then_inc(exped[h].sem, 1)
                nc.scalar.activation(sink_exp, sink_gap, ACT.Exp).then_inc(sink_exped.sem, 1)
                wait(act, conv_out[3], t)
                nc.scalar.activation(conv_sq[:], conv_y[:], ACT.Square).then_inc(conv_squared.sem, 1)
                prepare(t + 1)
                wait(act, attn_ready, t)
                nc.scalar.activation(junk[:, 0:AW], attn[:], ACT.Square, accum_out=ss_ca[:, 1:2]).then_inc(attn_squared.sem, 1)
                wait(act, x1_ready, t)
                nc.scalar.activation(junk[:], x1[:], ACT.Square, accum_out=ss_f).then_inc(x1_squared.sem, 1)
                square_qk(t + 1)
                act.dma_start(out_rows[bass.ds(t * P, P), :], x1[:]).then_inc(stored.sem, 16)
                wait(act, h2_ready, t)
                act.dma_start(h2_rows[bass.ds(t * P, P), :], h2[:]).then_inc(stored.sem, 16)
                for i in range(2):
                    wait(act, h2_turned[i], t)
                    nc.scalar.copy(h2T[:, 4 * i:4 * i + 4, :], ps_s[:, 512 * i:512 * i + 512].rearrange(
                        "p (k q) -> p k q", k=4)).then_inc(h2T_ready[i].sem, 1)
                wait(act, best_ready, t)
                nc.scalar.activation(exp4, best[:, 0:TOP_K], ACT.Exp, bias=neg_best,
                                     accum_out=sum4).then_inc(best_exped.sem, 1)
            wait(act, stored, NB - 1)

        @block.vector
        def _(dve):
            def mean(ss, ms, width):
                return nc.vector.tensor_scalar(ms, ss, 1.0 / width, EPS, ALU.mult, ALU.add)

            def x_to_mean(n):
                wait(dve, x_squared, n)
                mean(ss_x, ms_x, D).then_inc(x_mean.sem, 1)

            def read_hT(n, i):
                wait(dve, x_turned[i], n)
                nc.vector.tensor_tensor(hT[:, 4 * i:4 * i + 4, :],
                                        ps_c[:, i, :].rearrange("p (k q) -> p k q", k=4),
                                        norm_mix_col[:, 4 * i:4 * i + 4].unsqueeze(2).broadcast_to([P, 4, P]),
                                        ALU.mult).then_inc(hT_ready[i].sem, 1)

            def read_qkv(n):
                wait(dve, qkv_done, n)
                nc.vector.tensor_tensor(qk[:, 0:AW], ps_q[:], b_qkv_row[:, 0:AW], ALU.add)
                nc.vector.tensor_tensor(qk[:, AW:AW + KVW], ps_kv[:, 0:KVW], b_qkv_row[:, AW:AW + KVW],
                                        ALU.add).then_inc(qk_ready.sem, 1)
                nc.vector.tensor_copy(v_keys[:, 0, :], v_keys[:, 1, :]).then_inc(v_shifted.sem, 1)
                wait(dve, v_shifted, n)
                nc.vector.tensor_tensor(v_keys[:, 1, :], ps_kv[:, KVW:2 * KVW], b_qkv_row[:, AW + KVW:],
                                        ALU.add).then_inc(v_ready.sem, 1)

            def norm_qk(n):
                wait(dve, qk_squared, n)
                nc.vector.tensor_reduce(ss_qk, qk_sq[:].rearrange("p (h d) -> p h d", d=HD), AX_X,
                                        ALU.add).then_inc(qk_summed.sem, 1)
                wait(dve, qk_summed, n)
                mean(ss_qk, ms_qk, HD).then_inc(qk_mean.sem, 1)
                wait(dve, qk_rstd, n)
                nc.vector.tensor_tensor(qn[:].rearrange("p (h d) -> p h d", d=HD),
                                        qk[:, 0:AW].rearrange("p (h d) -> p h d", d=HD),
                                        rstd_qk[:, 0:NH].unsqueeze(2).broadcast_to([P, NH, HD]), ALU.mult)
                for j in range(2):
                    last = nc.vector.tensor_tensor(kn[:, :, j, :],
                                                   qk[:, AW:].rearrange("p (h d) -> p h d", d=HD),
                                                   rstd_qk[:, NH:].unsqueeze(2).broadcast_to([P, NKV, HD]), ALU.mult)
                last.then_inc(qk_normed.sem, 1)

            def convolve(t, c):
                gate_b, gate_c = ps_c[:, c % 2, 0:P], ps_c[:, c % 2, P:2 * P]
                step = vstep.did
                wait(dve, conv_done[c], t)
                wait(dve, u_ready[c], t)
                step(nc.vector.scalar_tensor_tensor(out=conv_x[:, c, 2:], in0=gate_c,
                                                    scalar=b_in_col[:, CC + c:CC + c + 1],
                                                    in1=conv_u[:, c % 2, :], op0=ALU.add, op1=ALU.mult))
                dve.wait_ge(vstep.sem, vstep.value(t))
                step(nc.vector.tensor_scalar(conv_t[:, 0, :], conv_x[:, c, 2:], conv_w_col[:, 2, c:c + 1], None, ALU.mult))
                dve.wait_ge(vstep.sem, vstep.value(t))
                step(nc.vector.scalar_tensor_tensor(out=conv_t[:, 1, :], in0=conv_x[:, c, 1:P + 1],
                                                    scalar=conv_w_col[:, 1, c:c + 1], in1=conv_t[:, 0, :],
                                                    op0=ALU.mult, op1=ALU.add))
                dve.wait_ge(vstep.sem, vstep.value(t))
                step(nc.vector.scalar_tensor_tensor(out=conv_t[:, 2, :], in0=conv_x[:, c, 0:P],
                                                    scalar=conv_w_col[:, 0, c:c + 1], in1=conv_t[:, 1, :],
                                                    op0=ALU.mult, op1=ALU.add))
                dve.wait_ge(vstep.sem, vstep.value(t))
                nc.vector.scalar_tensor_tensor(out=conv_y[:, c, :], in0=gate_b, scalar=b_in_col[:, c:c + 1],
                                               in1=conv_t[:, 2, :], op0=ALU.add,
                                               op1=ALU.mult).then_inc(conv_out[c].sem, 1)

            def then_wait(t, ins):
                vstep.did(ins)
                dve.wait_ge(vstep.sem, vstep.value(t))

            dve.wait_ge(setup_loaded, all_setup)
            nc.vector.tensor_copy(sink_slots[:].rearrange("p (b a) -> p b a", b=2),
                                  sink_row[:].rearrange("p (a b) -> p b a", b=2)).then_inc(slots_made, 1)
            nc.vector.tensor_copy(rel_bias_slots[:].rearrange("p (b a) -> p b a", b=2),
                                  rel_bias_sb[:].rearrange("p (a b) -> p b a", b=2)).then_inc(slots_made, 1)
            dve.wait_ge(rel_summed, 1)
            nc.vector.tensor_tensor(rel_row, ps_s[0:NH, 0:REL_W], rel_const[0:NH, REL_W:2 * REL_W],
                                    ALU.add).then_inc(rel_made, 1)
            dve.wait_ge(vectors_turned, 1)
            nc.vector.tensor_copy(vectors[:], ps_s[:, 512:554]).then_inc(vectors_ready, 1)
            dve.wait_ge(vectors_ready, 1)
            dve.wait_ge(slots_made, 2)
            dve.wait_ge(cleared, 5)
            dve.wait_ge(bias_turned, 1)
            nc.vector.tensor_copy(bias_prev[:], ps_heads[:, :, 0:P]).then_inc(bias_flipped, 1)
            nc.vector.tensor_copy(bias_all[:, :, P:2 * P], ps_heads[:, :, P:2 * P]).then_inc(bias_flipped, 1)
            dve.wait_ge(bias_flipped, 2)
            x_to_mean(0)
            read_hT(0, 0)
            read_hT(0, 1)
            read_qkv(0)
            norm_qk(0)
            with dve.Fori(0, NB) as t:
                vstep.n = 0
                then_wait(t, nc.vector.tensor_copy(conv_x[:, :, 0:2], conv_x[:, :, P:P + 2]))
                convolve(t, 0)
                convolve(t, 1)
                convolve(t, 2)
                wait(dve, scored, t)
                wait(dve, bias_switched, t - 1)
                wait(dve, av_done[NH - 1], t - 1)
                nc.vector.tensor_tensor(probs[:], ps_heads, bias_all[:], ALU.add).then_inc(biased.sem, 1)
                wait(dve, biased, t)
                then_wait(t, nc.vector.tensor_reduce(denom, probs[:], AX_X, ALU.max))
                then_wait(t, nc.vector.tensor_tensor(top, denom, sink_slots[:], ALU.max))
                nc.vector.tensor_tensor(sink_gap, sink_slots[:], top, ALU.subtract)
                nc.vector.tensor_scalar(neg_top, top, -1.0, None, ALU.mult).then_inc(neg_ready.sem, 1)
                convolve(t, 3)
                wait(dve, conv_out[3], t)
                nc.vector.tensor_tensor(conv_s[:], conv_y[:], conv_g_col.unsqueeze(2).broadcast_to([P, CC, P]),
                                        ALU.mult).then_inc(conv_scaled.sem, 1)
                for h in range(NH):
                    wait(dve, p_turned[h], t)
                    if h >= 2:
                        wait(dve, av_done[h - 2], t)
                    nc.vector.tensor_copy(pT[:, h % 2, :], (ps_q, ps_kv)[h % 2][:, 0:2 * P]).then_inc(pT_ready[h].sem, 1)
                wait(dve, sink_exped, t)
                then_wait(t, nc.vector.tensor_tensor(denom, row_sum, sink_exp, ALU.add))
                then_wait(t, nc.vector.reciprocal(rdenom, denom))
                x_to_mean(t + 1)
                wait(dve, av_done[NH - 1], t)
                nc.vector.tensor_tensor(attn[:].rearrange("p (a b d) -> p b a d", b=2, d=HD),
                                        ps_c[:, 0, :].rearrange("p (a b d) -> p b a d", b=2, d=HD),
                                        rdenom.rearrange("p (b a) -> p b a", b=2).unsqueeze(3).broadcast_to(
                                            [P, 2, NH // 2, HD]), ALU.mult).then_inc(attn_ready.sem, 1)
                wait(dve, conv_summed, t)
                nc.vector.tensor_reduce(ss_ca[:, 0:1], ps_kv[:, 2 * P:2 * P + CC], AX_X, ALU.add).then_inc(vstep.sem, 1)
                vstep.n += 1
                wait(dve, attn_turned, t)
                nc.vector.tensor_tensor(attnT[:], ps_c[:, 1, :].rearrange("p (c q) -> p c q", c=CC),
                                        attn_g_col.unsqueeze(2).broadcast_to([P, CC, P]),
                                        ALU.mult).then_inc(attnT_ready.sem, 1)
                dve.wait_ge(vstep.sem, vstep.value(t))
                wait(dve, attn_squared, t)
                mean(ss_ca, ms_ca, CW).then_inc(ca_mean.sem, 1)
                read_hT(t + 1, 0)
                wait(dve, conv_mixed, t)
                wait(dve, ca_rstd, t)
                wait(dve, res_biased, t)
                wait(dve, stored, t - 1)
                then_wait(t, nc.vector.scalar_tensor_tensor(out=x1[:], in0=ps_s[:, 0:D], scalar=rstd_ca[:, 0:1],
                                                            in1=x_res[:], op0=ALU.mult, op1=ALU.add))
                wait(dve, attn_mixed, t)
                nc.vector.scalar_tensor_tensor(out=x1[:], in0=ps_s[:, D:2 * D], scalar=rstd_ca[:, 1:2],
                                               in1=x1[:], op0=ALU.mult, op1=ALU.add).then_inc(x1_ready.sem, 1)
                read_hT(t + 1, 1)
                wait(dve, x1_squared, t)
                mean(ss_f, ms_f, D).then_inc(f_mean.sem, 1)
                wait(dve, f_rstd, t)
                nc.vector.scalar_tensor_tensor(out=h2[:], in0=x1[:], scalar=rstd_f, in1=norm_ffn_row[:],
                                               op0=ALU.mult, op1=ALU.mult).then_inc(h2_ready.sem, 1)
                read_qkv(t + 1)
                norm_qk(t + 1)
                wait(dve, routed, t)
                nc.vector.tensor_tensor(route_sc[:], ps_route, b_router_row[:], ALU.add).then_inc(logits_read.sem, 1)
                wait(dve, logits_read, t)
                nc.vector.tensor_copy(best_f[:, 0:1], route_sc[:, 0:1])
                then_wait(t, nc.vector.max(best, route_sc[:]))
                nc.vector.tensor_scalar(neg_best, best[:, 0:1], -1.0, None, ALU.mult).then_inc(best_ready.sem, 1)
                then_wait(t, nc.vector.max_index(best_i[:], best, route_sc[:]))
                then_wait(t, nc.vector.tensor_copy(best_f, best_i[:]))
                then_wait(t, nc.vector.tensor_tensor(
                    hot[:], cst[:, C_E:C_E + NE].unsqueeze(1).broadcast_to([P, TOP_K, NE]),
                    best_f[:, 0:TOP_K].unsqueeze(2).broadcast_to([P, TOP_K, NE]), ALU.is_equal))
                nc.vector.tensor_reduce(picked[:, bass.ds(t, 1), :].rearrange("p o e -> p (o e)"),
                                        hot[:].rearrange("p k e -> p e k"), AX_X, ALU.add)
                wait(dve, best_exped, t)
                then_wait(t, nc.vector.reciprocal(rsum4, sum4))
                then_wait(t, nc.vector.tensor_scalar(gate4, exp4, rsum4, None, ALU.mult))
                then_wait(t, nc.vector.tensor_tensor(hot_g[:], hot[:], gate4.unsqueeze(2).broadcast_to([P, TOP_K, NE]),
                                                     ALU.mult))
                nc.vector.tensor_reduce(gates[:, bass.ds(t, 1), :].rearrange("p o e -> p (o e)"),
                                        hot_g[:].rearrange("p k e -> p e k"), AX_X, ALU.add)
                assert vstep.n == vstep.per, vstep.n

        @block.tensor
        def _(pe):
            def turn_x(n, i):
                for k in range(4 * i, 4 * i + 4):
                    last = pe.transpose(ps_c[:, i, (k % 4) * P:(k % 4 + 1) * P], xn[:, k * P:(k + 1) * P], ident)
                last.then_inc(x_turned[i].sem, 1)

            def project_qkv(n):
                for dst, a, b in ((ps_q[:], QKV0, QKV0 + AW), (ps_kv[:, 0:2 * KVW], QKV0 + AW, IN_W)):
                    for k in range(KD):
                        if a == QKV0 and k % 4 == 0:
                            wait(pe, hT_ready[k // 4], n)
                        last = pe.matmul(dst, hT[:, k, :], w_in_sb[:, k, a:b], start=(k == 0), stop=(k == KD - 1))
                last.then_inc(qkv_done.sem, 1)

            def project_conv(t, c):
                for j in range(3):
                    for k in range(KD):
                        first = j * CW + c * P
                        last = pe.matmul(ps_c[:, c % 2, j * P:(j + 1) * P], w_in_sb[:, k, first:first + P],
                                         hT[:, k, :], start=(k == 0), stop=(k == KD - 1))
                last.then_inc(conv_done[c].sem, 1)

            def turn_p(t, h):
                wait(pe, exped[h], t)
                if h >= 2:
                    wait(pe, pT_ready[h - 2], t)
                for j in range(2):
                    last = pe.transpose((ps_q, ps_kv)[h % 2][:, j * P:(j + 1) * P], probs[:, slot(h), j * P:(j + 1) * P], ident)
                last.then_inc(p_turned[h].sem, 1)

            def attend(t, h):
                kv = h // (NH // NKV)
                wait(pe, pT_ready[h], t)
                for j in range(2):
                    last = pe.matmul(ps_c[:, 0, h * HD:(h + 1) * HD], pT[:, h % 2, j * P:(j + 1) * P],
                                     v_keys[:, j, kv * HD:(kv + 1) * HD], start=(j == 0), stop=(j == 1))
                last.then_inc(av_done[h].sem, 1)

            pe.wait_ge(setup_loaded, all_setup)
            pe.wait_ge(slots_made, 2)
            pe.matmul(ps_s[0:NH, 0:REL_W], rel_bias_slots[:], rel_const[0:NBUCKET, 0:REL_W],
                      start=True, stop=True).then_inc(rel_summed, 1)
            pe.transpose(ps_s[:, 512:554], vector_rows, ident[0:42, 0:42]).then_inc(vectors_turned, 1)
            pe.wait_ge(bias_loaded, 16)
            pe.wait_ge(vectors_ready, 1)
            for i in range(4):
                last = pe.matmul(ps_s[:, i * 512:(i + 1) * 512], rel_const[:, 2 * REL_W:], probs[:, 2 * i:2 * i + 2, :].rearrange(
                    "p h k -> p (h k)"), start=True, stop=True)
            last.then_inc(bias_turned, 1)
            wait(pe, x_normed, 0)
            turn_x(0, 0)
            turn_x(0, 1)
            pe.wait_ge(qkv_w_loaded, 16)
            project_qkv(0)
            pe.wait_ge(conv_w_loaded, 48)
            pe.wait_ge(bias_flipped, 2)
            pe.wait_ge(out_w_loaded, 16)
            with pe.Fori(0, NB) as t:
                project_conv(t, 0)
                project_conv(t, 1)
                wait(pe, qk_normed, t)
                for i in range(NH // 2):
                    pe.transpose(ps_s[:, i * P:(i + 1) * P], qn[:, i * P:(i + 1) * P], ident)
                for i in range(NKV):
                    last = pe.transpose(ps_s[:, 512 + i * P:512 + (i + 1) * P],
                                        kn[:, i, :, :].rearrange("p j d -> p (j d)"), ident)
                last.then_inc(qk_turned.sem, 1)
                wait(pe, conv_out[0], t)
                project_conv(t, 2)
                wait(pe, qT_ready, t)
                wait(pe, logits_read, t - 1)
                for h in range(NH):
                    a = HD * (h % 2)
                    last = pe.matmul(ps_heads[:, slot(h), :], qT[a:a + HD, h // 2, :],
                                     kT[a:a + HD, h // (NH // NKV), :, :].rearrange("p j k -> p (j k)"),
                                     start=True, stop=True)
                last.then_inc(scored.sem, 1)
                wait(pe, conv_out[1], t)
                project_conv(t, 3)
                wait(pe, conv_out[2], t)
                wait(pe, v_ready, t)
                turn_p(t, 0)
                for h in range(NH):
                    if h + 1 < NH:
                        turn_p(t, h + 1)
                    attend(t, h)
                wait(pe, conv_squared, t)
                for c in range(CC):
                    last = pe.matmul(ps_kv[:, 2 * P + c:2 * P + c + 1], conv_sq[:, c, :], cst[:, C_ONES:C_ONES + 1],
                                     start=True, stop=True)
                last.then_inc(conv_summed.sem, 1)
                wait(pe, conv_scaled, t)
                wait(pe, biased, t)
                for n in range(2):
                    for k in range(CC):
                        last = pe.matmul(ps_s[:, n * 512:(n + 1) * 512], conv_s[:, k, :],
                                         w_out_sb[:, k, n * 512:(n + 1) * 512], start=(k == 0), stop=(k == CC - 1))
                last.then_inc(conv_mixed.sem, 1)
                wait(pe, attn_ready, t)
                for c in range(CC):
                    last = pe.transpose(ps_c[:, 1, c * P:(c + 1) * P], attn[:, c * P:(c + 1) * P], ident)
                last.then_inc(attn_turned.sem, 1)
                wait(pe, x_normed, t + 1)
                turn_x(t + 1, 0)
                wait(pe, attnT_ready, t)
                for n in range(2):
                    for k in range(CC):
                        last = pe.matmul(ps_s[:, D + n * 512:D + (n + 1) * 512], attnT[:, k, :],
                                         w_out_sb[:, CC + k, n * 512:(n + 1) * 512], start=(k == 0), stop=(k == CC - 1))
                last.then_inc(attn_mixed.sem, 1)
                turn_x(t + 1, 1)
                project_qkv(t + 1)
                wait(pe, h2_ready, t)
                for i in range(2):
                    for k in range(4 * i, 4 * i + 4):
                        last = pe.transpose(ps_s[:, k * P:(k + 1) * P], h2[:, k * P:(k + 1) * P], ident)
                    last.then_inc(h2_turned[i].sem, 1)
                for k in range(KD):
                    if k % 4 == 0:
                        wait(pe, h2T_ready[k // 4], t)
                    last = pe.matmul(ps_route, h2T[:, k, :], w_router_sb[:, k, :], start=(k == 0), stop=(k == KD - 1))
                last.then_inc(routed.sem, 1)


def experts(nc, h2_rows, out_rows, w1, b1, w2, b2, cst, picked, gates):
    ident = cst[:, C_ID:C_ID + P]
    ones = cst[:, C_ONES:C_ONES + P]
    last_size = len(SIZES) - 1
    second_rows = ((SIZES.index(144), 16), (SIZES.index(192), 64), (last_size, P))
    with ExitStack() as ctx:
        def sb(name, shape, dt=F32):
            return ctx.enter_context(nc.sbuf_tensor(name, shape, dt))

        def ps(name, shape):
            return ctx.enter_context(nc.psum_tensor(name, shape, F32))

        def sem(name):
            return ctx.enter_context(nc.semaphore(name))

        credited = []

        def event(name, unit=1, credit=0):
            e = Event(sem(name), unit, credit)
            if credit:
                credited.append(e)
            return e

        def wait(eng, e, t):
            eng.wait_ge(e.sem, e.of(t))

        w_slot = sb("w_slot", [P, PIECES, KD, PW])
        b1T = sb("b1T", [P, 2 * P1, NE])
        b2T = sb("b2T", [P, KD, NE])
        b1_cur = sb("b1_cur", [P, 2 * P1])
        b2_cur = sb("b2_cur", [P, KD])
        place = sb("place", [P, NB, NE])
        gate_parts = sb("gate_parts", [P, NB, 3, NE], BF16)
        base_row = sb("base_row", [P, P])
        job_row = sb("job_row", [1, 2 * P], I32)
        jobs = sb("jobs", [1, 2], I32)
        iota_b = sb("iota_b", [P, CAP], BF16)
        place_cur = sb("place_cur", [P, NB])
        token = sb("token", [P, NB])
        match = sb("match", [P, NB, CAP], BF16)
        entry = sb("entry", [P, NB, 5], BF16)
        list_sb = sb("list_sb", [P, 2, 5])
        gate_next = sb("gate_next", [P, 2])
        idx_next = sb("idx_next", [P, 2], I32)
        gate_cur = sb("gate_cur", [P, 2])
        idx_cur = sb("idx_cur", [P, 2], I32)
        x_got = sb("x_got", [P, 2, D])
        xT = sb("xT", [P, KD, CAP])
        glu = sb("glu", [P, 3, CAP])
        lin = sb("lin", [P, 3, CAP])
        sig = sb("sig", [P, 3, CAP])
        act_T = sb("act_T", [P, P1, CAP])
        yT = sb("yT", [P, KD, CAP])
        y_rows = sb("y_rows", [P, 2, D])
        carrier = sb("carrier", [P, 3])
        before = sb("before", [P, NB + 1, NE])
        counts = sb("counts", [P, NE])
        rank = sb("rank", [P, NB, NE])
        other = sb("other", [P, NB, NE])
        n_jobs = sb("n_jobs", [P, NE])
        over = sb("over", [P, 2, NE])
        last_job = sb("last_job", [P, NE])
        ended = sb("ended", [P, NE])
        pick_e = sb("pick_e", [P, 2, NE])
        limits = sb("limits", [P, 2, last_size])
        fields = sb("fields", [P, 3])
        narrow = sb("narrow", [P, 8])

        ps_unit = [ps(f"ps_unit{i}", [P, 2, CAP]) for i in range(3)]
        ps_list = ps("ps_list", [P, 512])
        ps_x = [ps(f"ps_x{i}", [P, 2, CAP]) for i in range(2)]
        ps_y = [ps(f"ps_y{i}", [P, 2, 2, P]) for i in range(2)]

        biases_turned = sem("biases_turned")
        biases_read = sem("biases_read")
        carrier_cleared = sem("carrier_cleared")
        buffers = sem("expert_buffers_cleared")
        sums_ready = sem("sums_ready")
        ranked = sem("ranked")
        fields_ready = sem("fields_ready")
        fields_spread = sem("fields_spread")
        table_ready = sem("table_ready")
        rstep = Steps(sem("routing_step"), 0)
        units_cleared = sem("units_cleared")
        place_taken = event("place_taken")
        entry_ready = event("entry_ready")
        matched = event("matched")
        gate_summed = event("gate_summed")
        listed = event("listed")
        list_read = event("list_read")
        idx_ready = event("idx_ready")
        gathered_a = event("gathered_a", 16)
        gathered_b = event("gathered_b", 16)
        x_turned = [event(f"x_rows_turned{i}") for i in range(4)]
        xT_ready = [event(f"xT_ready{i}") for i in range(4)]
        w_loaded = [event(f"w_loaded{p}", 16) for p in range(PIECES)]
        unit_done = [event(f"unit_done{p}", 1, 1) for p in range(PIECES)]
        unit_read = [event(f"unit_read{p}", 1, 1) for p in range(PIECES)]
        b1_ready = event("b1_ready")
        cur_ready = event("cur_ready")
        b2_ready = event("b2_ready")
        sig_ready = [event(f"sig_ready{p}") for p in range(P1)]
        scaled = [event(f"scaled{p}") for p in range(P1)]
        act_ready = [event(f"act_ready{p}") for p in range(P1)]
        y_turned = [event(f"y_turned{i}") for i in range(4)]
        y_read = [event(f"y_read{i}", 1, 1) for i in range(4)]
        pool_moved = Event(sem("pool_moved"), 32, 1)
        carried = [event(f"carried{i}", 1, 1) for i in range(2)]

        block = ctx.enter_context(nc.Block())

        def job_loop(eng):
            eng.wait_ge(table_ready, 3)
            n = eng.value_load(jobs[0:1, 0:1], min_val=1, max_val=NE + S * TOP_K // CAP)
            return eng.Fori(0, n)

        def expert_of(eng, q):
            return eng.value_load(job_row[0:1, bass.ds(q, 1)], min_val=0, max_val=NE - 1)

        def size_of(eng, q):
            return eng.value_load(job_row[0:1, bass.ds(q + P, 1)], min_val=0, max_val=last_size)


        @block.sync
        def _(sp):
            with job_loop(sp) as q:
                e = expert_of(sp, q)
                for p in range(PIECES):
                    wait(sp, unit_done[p], q - 1)
                    w, first = (w1, p * PW) if p < P1 else (w2, (p - P1) * PW)
                    src = w[0, bass.ds(e, 1), :, first:first + PW].rearrange("o (k p) f -> p (o k) f", p=P)
                    sp.dma_start(w_slot[:, p, :, :], src).then_inc(w_loaded[p].sem, 16)

        @block.gpsimd
        def _(pool):
            for e in credited:
                pool.sem_inc(e.sem, e.unit * e.credit)
            nc.gpsimd.memset(carrier[:], 0.0).then_inc(carrier_cleared, 1)
            nc.gpsimd.memset(x_got[:], 0.0).then_inc(buffers, 1)
            pool.wait_ge(carrier_cleared, 1)

            def second_block(size, move):
                (small, a), (middle, b), (_, c) = second_rows
                with pool.If(size > small):
                    with pool.If(size > middle):
                        move(c)
                    with pool.Else():
                        move(b)
                with pool.Else():
                    move(a)

            pool.wait_ge(buffers, 1)
            pool.dma_start(y_rows[0:NE, :, :].rearrange("e h f -> e (h f)"), b1[0]).then_inc(pool_moved.sem, 16)
            pool.dma_start(x_got[0:NE, 0, :], b2[0]).then_inc(pool_moved.sem, 16)

            def carry_wait(q, i):
                wait(pool, carried[i], q - 1)
                nc.gpsimd.tensor_tensor(carrier[:, i:i + 1], carrier[:, 2:3], carrier[:, 2:3],
                                        ALU.add).then_inc(carried[i].sem, 1)

            def gather(t):
                def get(done, i, n):
                    nc.gpsimd.indirect_dma_start(
                        out=x_got[0:n, i, :], out_offset=None, in_=h2_rows,
                        in_offset=bass.IndirectOffsetOnAxis(ap=idx_next[0:n, i:i + 1], axis=0)).then_inc(done.sem, 16)

                get(gathered_a, 0, P)
                second_block(size_of(pool, t), lambda n: get(gathered_b, 1, n))

            def scatter(t):
                def put(i, n):
                    nc.gpsimd.indirect_dma_start(
                        out=out_rows, out_offset=bass.IndirectOffsetOnAxis(ap=idx_cur[0:n, i:i + 1], axis=0),
                        in_=y_rows[0:n, i, :], in_offset=None, compute_op=ALU.add).then_inc(pool_moved.sem, 16)

                put(0, P)
                second_block(size_of(pool, t), lambda n: put(1, n))

            pool.wait_ge(table_ready, 3)
            wait(pool, idx_ready, 0)
            gather(0)
            with job_loop(pool) as q:
                wait(pool, x_turned[3], q)
                wait(pool, idx_ready, q + 1)
                carry_wait(q, 0)
                gather(q + 1)
                wait(pool, pool_moved, q - 1)
                wait(pool, y_read[3], q)
                carry_wait(q, 1)
                scatter(q)
            pool.wait_ge(gathered_a.sem, 16)
            n = pool.value_load(jobs[0:1, 0:1], min_val=1, max_val=NE + S * TOP_K // CAP)
            wait(pool, pool_moved, n - 1)

        @block.scalar
        def _(act):
            act.wait_ge(biases_read, 3)
            with job_loop(act) as q:
                e = expert_of(act, q)
                wait(act, unit_read[PIECES - 1], q - 1)
                nc.scalar.copy(b2_cur[:], b2T[:, :, bass.ds(e, 1)].rearrange("p m o -> p (m o)")).then_inc(b2_ready.sem, 1)
                for p in range(P1):
                    wait(act, unit_read[p], q)
                    nc.scalar.activation(sig[:, p % 3, :], glu[:, p % 3, :], ACT.Sigmoid,
                                         scale=ALPHA).then_inc(sig_ready[p].sem, 1)
                wait(act, b2_ready, q)
                for p in range(P1, PIECES):
                    wait(act, unit_done[p], q)
                    for u in range(2):
                        m = 2 * (p - P1) + u
                        last = nc.scalar.activation(yT[:, m, :], ps_unit[p % 3][:, u, :], ACT.Identity,
                                                    bias=b2_cur[:, m:m + 1])
                    last.then_inc(unit_read[p].sem, 1)

        @block.vector
        def _(dve):
            v = nc.vector

            def then_wait(ins):
                rstep.did(ins)
                dve.wait_ge(rstep.sem, rstep.n)

            for i in range(3):
                last = v.memset(ps_unit[i][:], 0.0)
            last.then_inc(units_cleared, 1)
            then_wait(v.memset(before[:, 0, :], 0.0))
            for b in range(NB):
                then_wait(v.tensor_tensor(before[:, b + 1, :], before[:, b, :], picked[:, b, :], ALU.add))
            v.tensor_copy(iota_b[:], cst[:, C_IOTA:C_IOTA + CAP])
            v.tensor_copy(entry[:, :, 0], cst[:, C_TOK:C_TOK + NB])
            v.tensor_copy(entry[:, :, 1], cst[:, C_TOK + NB:C_TOK + 2 * NB]).then_inc(sums_ready, 1)
            then_wait(v.scalar_tensor_tensor(out=token[:], in0=cst[:, C_TOK:C_TOK + NB], scalar=32.0,
                                             in1=cst[:, C_TOK + NB:C_TOK + 2 * NB], op0=ALU.mult, op1=ALU.add))
            then_wait(v.tensor_copy(gate_parts[:, :, 0, :], gates[:]))
            then_wait(v.tensor_tensor(other[:], gates[:], gate_parts[:, :, 0, :], ALU.subtract))
            then_wait(v.tensor_copy(gate_parts[:, :, 1, :], other[:]))
            then_wait(v.tensor_tensor(gates[:], other[:], gate_parts[:, :, 1, :], ALU.subtract))
            then_wait(v.tensor_copy(gate_parts[:, :, 2, :], gates[:]))
            dve.wait_ge(ranked, 1)
            v.tensor_copy(rank[:], ps_list[:, 0:NB * NE].rearrange("p (b e) -> p b e", b=NB))
            then_wait(v.tensor_copy(counts[:], ps_list[:, NB * NE:NB * NE + NE]))
            then_wait(v.tensor_tensor(other[:], counts[:].unsqueeze(1).broadcast_to([P, NB, NE]), rank[:], ALU.subtract))
            then_wait(v.tensor_tensor(other[:], other[:], token[:].unsqueeze(2).broadcast_to([P, NB, NE]), ALU.add))
            then_wait(v.tensor_tensor(rank[:], rank[:], other[:], ALU.subtract))
            then_wait(v.tensor_tensor(rank[:], rank[:], picked[:], ALU.mult))
            then_wait(v.tensor_tensor(place[:], rank[:], other[:], ALU.add))
            then_wait(v.tensor_scalar(over[:, 0, :], counts[:], float(CAP), 1.0, ALU.is_gt, ALU.add))
            for i in range(2, S // CAP):
                then_wait(v.tensor_scalar(over[:, 1, :], counts[:], float(CAP * i), None, ALU.is_gt))
                then_wait(v.tensor_tensor(over[:, 0, :], over[:, 0, :], over[:, 1, :], ALU.add))
            then_wait(v.tensor_tensor_scan(last_job[:], cst[:, C_ONES:C_ONES + NE], over[:, 0, :], 0.0, ALU.mult, ALU.add))
            job = cst[:, C_PART:C_PART + 1]
            then_wait(v.tensor_scalar(ended[:], last_job[:], job, None, ALU.is_le))
            then_wait(v.tensor_tensor(pick_e[:, 0, :], ended[:], over[:, 0, :], ALU.mult))
            v.tensor_reduce(narrow[:, 0:1], ended[:], AX_X, ALU.add)
            then_wait(v.tensor_reduce(narrow[:, 1:2], pick_e[:, 0, :], AX_X, ALU.add))
            then_wait(v.tensor_scalar(fields[:, 0:1], narrow[:, 0:1], NE - 1.0, None, ALU.min))
            then_wait(v.tensor_tensor(narrow[:, 2:3], job, narrow[:, 1:2], ALU.subtract))
            then_wait(v.tensor_scalar(fields[:, 2:3], narrow[:, 2:3], float(CAP), None, ALU.mult))
            then_wait(v.tensor_scalar(pick_e[:, 1, :], cst[:, C_E:C_E + NE], fields[:, 0:1], None, ALU.is_equal))
            then_wait(v.tensor_tensor(pick_e[:, 0, :], pick_e[:, 1, :], counts[:], ALU.mult))
            then_wait(v.tensor_reduce(narrow[:, 3:4], pick_e[:, 0, :], AX_X, ALU.add))
            then_wait(v.tensor_tensor(narrow[:, 4:5], narrow[:, 3:4], fields[:, 2:3], ALU.subtract))
            assert SIZES[:-1] == tuple(SIZES[0] + 16 * i for i in range(last_size))
            then_wait(v.tensor_scalar(limits[:, 0, :], cst[:, C_IOTA:C_IOTA + last_size], 16.0, float(SIZES[0]),
                                      ALU.mult, ALU.add))
            then_wait(v.tensor_scalar(limits[:, 1, :], limits[:, 0, :], narrow[:, 4:5], None, ALU.is_lt))
            v.tensor_reduce(fields[:, 1:2], limits[:, 1, :], AX_X, ALU.add).then_inc(fields_ready, 1)
            dve.wait_ge(fields_spread, 1)
            v.tensor_copy(jobs[0:1, 0:1], last_job[0:1, NE - 1:NE]).then_inc(table_ready, 1)
            v.tensor_copy(job_row[:], ps_list[0:1, 0:2 * P]).then_inc(table_ready, 1)
            v.tensor_copy(base_row[:], ps_list[:, 2 * P:3 * P]).then_inc(table_ready, 1)
            dve.wait_ge(biases_turned, 1)
            turned = ps_x[0][:].rearrange("p a b -> p (a b)").rearrange("p (j u e) -> p j u e", u=2, e=NE)
            b1_units = b1T[:].rearrange("p (j u) e -> p j u e", u=2)
            v.tensor_copy(b1_units[:, :, 0, :], turned[:, :, 0, :]).then_inc(biases_read, 1)
            v.tensor_scalar(b1_units[:, :, 1, :], turned[:, :, 1, :], 1.0, None, ALU.add).then_inc(biases_read, 1)
            v.tensor_copy(b2T[:], ps_x[1][:].rearrange("p a b -> p (a b)")[:, 0:KD * NE].rearrange(
                "p (m e) -> p m e", e=NE)).then_inc(biases_read, 1)

            def match_tokens(t, e):
                v.tensor_scalar(place_cur[:], place[:, :, bass.ds(e, 1)].rearrange("p b o -> p (b o)"),
                                base_row[:, bass.ds(t, 1)], None, ALU.subtract).then_inc(place_taken.sem, 1)
                v.tensor_copy(entry[:, :, 2:5], gate_parts[:, :, :, bass.ds(e, 1)].rearrange("p b g o -> p b (g o)"))
                wait(dve, place_taken, t)
                for b in range(NB):
                    last = v.tensor_scalar(match[:, b, :], iota_b[:], place_cur[:, b:b + 1], None, ALU.is_equal)
                last.then_inc(matched.sem, 1)

            def read_list(t):
                wait(dve, listed, t)
                lists = ps_list[:, 0:10].rearrange("p (h f) -> p h f", h=2)
                v.tensor_copy(list_sb[:], lists).then_inc(list_read.sem, 1)
                wait(dve, list_read, t)
                v.scalar_tensor_tensor(out=idx_next[:], in0=list_sb[:, :, 0], scalar=32.0, in1=list_sb[:, :, 1],
                                       op0=ALU.mult, op1=ALU.add).then_inc(idx_ready.sem, 1)
                v.tensor_reduce(gate_next[:], list_sb[:, :, 2:5], AX_X, ALU.add).then_inc(gate_summed.sem, 1)

            def read_xT(t, i):
                wait(dve, x_turned[i], t)
                v.tensor_copy(xT[:, 2 * i:2 * i + 2, :], ps_x[i % 2][:]).then_inc(xT_ready[i].sem, 1)

            def clip(q, p):
                wait(dve, unit_done[p], q)
                v.tensor_scalar(glu[:, p % 3, :], ps_unit[p % 3][:, 0, :], b1_cur[:, 2 * p:2 * p + 1], LIMIT,
                                ALU.add, ALU.min)
                v.tensor_scalar(lin[:, p % 3, :], ps_unit[p % 3][:, 1, :], b1_cur[:, 2 * p + 1:2 * p + 2], LIMIT + 1.0,
                                ALU.add, ALU.min).then_inc(unit_read[p].sem, 1)

            def finish(q, p):
                wait(dve, sig_ready[p], q)
                v.tensor_tensor(sig[:, p % 3, :], sig[:, p % 3, :], glu[:, p % 3, :], ALU.mult).then_inc(scaled[p].sem, 1)
                wait(dve, scaled[p], q)
                v.scalar_tensor_tensor(out=act_T[:, p, :], in0=lin[:, p % 3, :], scalar=1.0 - LIMIT, in1=sig[:, p % 3, :],
                                       op0=ALU.max, op1=ALU.mult).then_inc(act_ready[p].sem, 1)

            def read_y(q, i):
                wait(dve, y_turned[i], q)
                for h in range(2):
                    last = v.tensor_scalar(y_rows[:, h, i * PW:(i + 1) * PW],
                                           ps_y[i % 2][:, h, :, :].rearrange("p u c -> p (u c)"),
                                           gate_cur[:, h:h + 1], None, ALU.mult)
                last.then_inc(y_read[i].sem, 1)

            dve.wait_ge(table_ready, 3)
            match_tokens(0, expert_of(dve, 0))
            read_list(0)
            for i in range(4):
                read_xT(0, i)
            dve.wait_ge(biases_read, 3)
            with job_loop(dve) as q:
                e = expert_of(dve, q)
                e_next = expert_of(dve, q + 1)
                v.tensor_copy(b1_cur[:], b1T[:, :, bass.ds(e, 1)].rearrange("p m o -> p (m o)")).then_inc(b1_ready.sem, 1)
                wait(dve, b1_ready, q)
                for p in range(P1):
                    clip(q, p)
                    if p >= 1:
                        finish(q, p - 1)
                    if p == 1:
                        match_tokens(q + 1, e_next)
                    if p == 4:
                        wait(dve, gate_summed, q)
                        wait(dve, pool_moved, q - 1)
                        v.tensor_copy(idx_cur[:], idx_next[:])
                        v.tensor_copy(gate_cur[:], gate_next[:]).then_inc(cur_ready.sem, 1)
                        wait(dve, cur_ready, q)
                        read_list(q + 1)
                finish(q, P1 - 1)
                for i in range(4):
                    if i >= 1:
                        read_y(q, i - 1)
                    read_xT(q + 1, i)
                read_y(q, 3)

        @block.tensor
        def _(pe):
            def list_tokens(t):
                wait(pe, matched, t)
                for h in range(2):
                    for b in range(NB):
                        last = pe.matmul(ps_list[:, 5 * h:5 * h + 5], match[:, b, h * P:(h + 1) * P], entry[:, b, :],
                                         start=(b == 0), stop=(b == NB - 1))
                last.then_inc(listed.sem, 1)

            def turn_x(t, i):
                if i == 0:
                    wait(pe, gathered_a, t)
                    wait(pe, gathered_b, t)
                if i >= 2:
                    wait(pe, xT_ready[i - 2], t)
                for c in range(2):
                    for h in range(2):
                        k = 2 * i + c
                        last = pe.transpose(ps_x[i % 2][:, c, h * P:(h + 1) * P], x_got[:, h, k * P:(k + 1) * P], ident)
                last.then_inc(x_turned[i].sem, 1)

            def turn_y(q, i):
                wait(pe, unit_read[P1 + i], q)
                wait(pe, y_read[(i + 2) % 4], q - 1 if i < 2 else q)
                for u in range(2):
                    for h in range(2):
                        last = pe.transpose(ps_y[i % 2][:, h, u, :], yT[:, 2 * i + u, h * P:(h + 1) * P], ident)
                last.then_inc(y_turned[i].sem, 1)

            def piece(q, p, n):
                wait(pe, w_loaded[p], q)
                wait(pe, unit_read[(p + 9) % PIECES], q - 1 if p < 3 else q)
                for u in range(2):
                    for k in range(KD):
                        if p == 0 and u == 0 and k % 2 == 0:
                            wait(pe, xT_ready[k // 2], q)
                        if p == P1 and u == 0 and k in (0, 6, 7):
                            wait(pe, act_ready[max(k, 5)], q)
                        if p < P1:
                            w, moving = w_slot[:, p, k, u::2], xT
                        else:
                            w, moving = w_slot[:, p, k, u * P:(u + 1) * P], act_T
                        last = pe.matmul(ps_unit[p % 3][:, u, 0:n], w, moving[:, k, 0:n],
                                         start=(k == 0), stop=(k == KD - 1))
                last.then_inc(unit_done[p].sem, 1)

            def run_job(q, n):
                for p in range(PIECES):
                    piece(q, p, n)
                    if p == 3:
                        list_tokens(q + 1)
                    if p >= P1:
                        if p > P1:
                            turn_y(q, p - P1 - 1)
                        turn_x(q + 1, p - P1)
                turn_y(q, 3)

            def pick_size(q, size, lo, hi):
                if hi - lo == 1:
                    run_job(q, SIZES[lo])
                    return
                mid = (lo + hi) // 2
                with pe.If(size < mid):
                    pick_size(q, size, lo, mid)
                with pe.Else():
                    pick_size(q, size, mid, hi)

            pe.wait_ge(units_cleared, 1)
            pe.wait_ge(sums_ready, 1)
            pe.matmul(ps_list[:, 0:NB * NE], cst[:, C_TRI:C_TRI + P], picked[:].rearrange("p b e -> p (b e)"),
                      start=True, stop=False)
            pe.matmul(ps_list[:, 0:NB * NE], ones, before[:, 0:NB, :].rearrange("p b e -> p (b e)"),
                      start=False, stop=True)
            pe.matmul(ps_list[:, NB * NE:NB * NE + NE], ones, before[:, NB, :], start=True, stop=True).then_inc(ranked, 1)
            pe.wait_ge(pool_moved.sem, 32)
            for m in range(2 * P1):
                first = (m // 2) * PW + m % 2
                pe.transpose(ps_x[0][:].rearrange("p a b -> p (a b)")[:, m * NE:(m + 1) * NE],
                             y_rows[0:NE, :, :].rearrange("e h f -> e (h f)")[:, first:first + PW - 1:2], ident[0:NE, 0:NE])
            for m in range(KD):
                last = pe.transpose(ps_x[1][:].rearrange("p a b -> p (a b)")[:, m * NE:(m + 1) * NE],
                                    x_got[0:NE, 0, m * P:(m + 1) * P], ident[0:NE, 0:NE])
            last.then_inc(biases_turned, 1)
            pe.wait_ge(fields_ready, 1)
            for f in range(3):
                last = pe.matmul(ps_list[:, f * P:(f + 1) * P], fields[:, f:f + 1].broadcast_to([P, P]), ident,
                                 start=True, stop=True)
            last.then_inc(fields_spread, 1)
            pe.wait_ge(table_ready, 3)
            list_tokens(0)
            pe.wait_ge(biases_read, 3)
            for i in range(4):
                turn_x(0, i)
            with job_loop(pe) as q:
                pick_size(q, size_of(pe, q), 0, len(SIZES))


def program(nc, x, norm_mix, w_in, b_in, conv_w, q_norm, k_norm, sinks, rel_bias, out_norm_conv,
            out_norm_attn, w_out, b_out, norm_ffn, w_router, b_router, w1, b1, w2, b2, const, out):
    x_rows = x.rearrange("o s d -> (o s) d")
    out_rows = out.rearrange("o s d -> (o s) d")
    h2_rows = nc.dram_tensor("h2_rows", (S, D), F32, kind="Internal").ap()
    rel_rows = nc.dram_tensor("rel_rows", (NH, REL_W), F32, kind="Internal").ap()
    with ExitStack() as ctx:
        cst = ctx.enter_context(nc.sbuf_tensor("cst", [P, C_HOT], F32))
        picked = ctx.enter_context(nc.sbuf_tensor("picked", [P, NB, NE], F32))
        gates = ctx.enter_context(nc.sbuf_tensor("gates", [P, NB, NE], F32))
        mixer(nc, x_rows, out_rows, h2_rows, rel_rows, norm_mix, w_in, b_in, conv_w, q_norm, k_norm, sinks,
              rel_bias, out_norm_conv, out_norm_attn, w_out, b_out, norm_ffn, w_router, b_router, const,
              cst, picked, gates)
        experts(nc, h2_rows, out_rows, w1, b1, w2, b2, cst, picked, gates)


_INS = ["x", "norm_mix", "w_in", "b_in", "conv_w", "q_norm", "k_norm", "sinks", "rel_bias", "out_norm_conv",
        "out_norm_attn", "w_out", "b_out", "norm_ffn", "w_router", "b_router", "w1", "b1", "w2", "b2"]


def kernel(**inputs):
    import numpy as _np
    import concourse.bacc as _bacc
    from concourse import mybir as _mybir
    from concourse.bass_utils import run_bass_kernel_spmd as _run

    nc = _bacc.Bacc("TRN2", target_bir_lowering=False, num_devices=1)
    arrays, args = {}, []
    for name in _INS:
        a = _np.ascontiguousarray(inputs[name])
        arrays[f"in_{name}_dram"] = a
        args.append(nc.dram_tensor(f"in_{name}_dram", a.shape, _mybir.dt.from_np(a.dtype), kind="ExternalInput").ap())
    const = constants()
    arrays["const_dram"] = const
    args.append(nc.dram_tensor("const_dram", const.shape, F32, kind="ExternalInput").ap())
    args.append(nc.dram_tensor("out_dram", (1, S, D), F32, kind="ExternalOutput").ap())
    program(nc, *args)
    r = _run(nc, [arrays], core_ids=[0])
    return r.results[0]["out_dram"]
```

```python
from contextlib import ExitStack

import numpy as np
import concourse.bass as bass
from concourse import mybir

ALU = mybir.AluOpType
ACT = mybir.ActivationFunctionType
F32 = mybir.dt.float32
BF16 = mybir.dt.bfloat16
I32 = mybir.dt.int32
U32 = mybir.dt.uint32
AX_X = mybir.AxisListType.X

P = 128
D = 1024
S = 1024
NB = S // P
KD = D // P
CW = 512
CC = CW // P
HD = 64
NH = 8
HALF = NH // 2
NKV = 2
AW = NH * HD
KVW = NKV * HD
QKV0 = 3 * CW
IN_W = 3 * CW + AW + 2 * KVW
NBUCKET = 32
MAX_DISTANCE = 128
NE = 32
TOP_K = 4
FF = 1024
LIMIT = 7.0
ALPHA = 1.702
EPS = 1e-5
MASKED = -1e30

CAP = 256
SIZE_STEP = 8
SIZES = tuple(range(P, 209, SIZE_STEP)) + (CAP,)
PIECES = 12
P1 = 8
EARLY_PIECES = 4
PW = 256
REL_W = 384

C_ID, C_TRI, C_IOTA, C_ONES, C_E, C_PART, C_TOK, C_HOT = 0, 128, 256, 512, 640, 672, 673, 689
C_MASK = C_HOT + REL_W
C_FLIP = C_MASK + REL_W
C_W = C_FLIP + P


def constants():
    c = np.zeros((P, C_W), np.float32)
    p = np.arange(P)
    c[:, C_ID:C_ID + P] = np.eye(P)
    c[:, C_TRI:C_TRI + P] = p[:, None] < p[None, :]
    c[:, C_IOTA:C_IOTA + CAP] = np.arange(CAP)
    c[:, C_ONES:C_ONES + P] = 1.0
    c[:, C_E:C_E + NE] = np.arange(NE)
    c[:, C_PART] = p
    tok = p[:, None] + P * np.arange(NB)[None, :]
    c[:, C_TOK:C_TOK + NB] = tok // 32
    c[:, C_TOK + NB:C_TOK + 2 * NB] = tok % 32
    half = NBUCKET // 2
    rel = 255 - np.arange(REL_W)
    n = np.maximum(rel, 1).astype(np.float32)
    large = half + (np.log(n / half) / np.log(MAX_DISTANCE / half) * (NBUCKET - half)).astype(np.int32)
    bucket = np.where(rel < half, np.maximum(rel, 0), np.minimum(large, NBUCKET - 1))
    c[:NBUCKET, C_HOT:C_HOT + REL_W] = bucket[None, :] == np.arange(NBUCKET)[:, None]
    c[:, C_MASK:C_MASK + REL_W] = np.where((rel >= 0) & (rel < P), 0.0, MASKED)[None, :]
    c[:, C_FLIP:C_FLIP + P] = np.eye(P)[::-1]
    return c


class Event:

    def __init__(self, sem, unit=1, credit=0):
        self.sem, self.unit, self.credit = sem, unit, credit

    def of(self, t):
        n = t + (1 + self.credit)
        return n if self.unit == 1 else n * self.unit


class Steps:

    def __init__(self, sem, per):
        self.sem, self.per, self.n = sem, per, 0

    def did(self, ins):
        ins.then_inc(self.sem, 1)
        self.n += 1

    def value(self, t):
        return t * self.per + self.n


def clear_sems(nc, sems):
    numbers = sorted(s.num for s in sems)
    assert numbers == list(range(numbers[0], numbers[-1] + 1))
    nc.all_engine_barrier(sems_to_clear=range(numbers[0], numbers[-1] + 1))


def head_of(s):
    return 2 * (s % HALF) + s // HALF


def mixer(nc, x_rows, out_rows, h2_rows, rel_rows, norm_mix, w_in, b_in, conv_w, q_norm, k_norm, sinks,
          rel_bias, out_norm_conv, out_norm_attn, w_out, b_out, norm_ffn, w_router, b_router, const,
          cst, picked, gates):
    ident = cst[:, C_ID:C_ID + P]
    with ExitStack() as ctx:
        def sb(name, shape, dt=F32):
            return ctx.enter_context(nc.sbuf_tensor(name, shape, dt))

        def ps(name, shape):
            return ctx.enter_context(nc.psum_tensor(name, shape, F32))

        all_sems = []

        def sem(name):
            all_sems.append(ctx.enter_context(nc.semaphore(name)))
            return all_sems[-1]

        credited = []

        def event(name, unit=1, credit=0):
            e = Event(sem(name), unit, credit)
            if credit:
                credited.append(e)
            return e

        w_in_sb = sb("w_in_sb", [P, KD, IN_W])
        w_out_sb = sb("w_out_sb", [P, KD, D])
        w_router_sb = sb("w_router_sb", [P, KD, NE])
        norm_ffn_row = sb("norm_ffn_row", [P, D])
        vectors = sb("vectors", [P, 42])
        norm_mix_col = vectors[:, 0:8]
        b_in_col = vectors[:, 8:20]
        conv_w_col = vectors[:, 20:32].rearrange("p (j c) -> p j c", j=3)
        conv_g_col = vectors[:, 32:36]
        attn_g_col = vectors[:, 36:40]
        q_norm_col = vectors[:, 40:41]
        k_norm_col = vectors[:, 41:42]
        b_qkv_row = sb("b_qkv_row", [P, AW + 2 * KVW])
        b_out_row = sb("b_out_row", [P, D])
        b_router_row = sb("b_router_row", [P, NE])
        q_scale_col = sb("q_scale_col", [P, 1])
        sink_row = sb("sink_row", [P, NH])
        rel_bias_sb = sb("rel_bias_sb", [NBUCKET, NH])
        rel_bias_slots = sb("rel_bias_slots", [NBUCKET, NH])
        sink_slots = sb("sink_slots", [P, NH])
        minus_half = sb("minus_half", [P, NH + NKV])
        bias_prev = sb("bias_prev", [P, NH, P])
        bias_all = sb("bias_all", [P, NH, 2 * P])

        x_in = sb("x_in", [P, D])
        x_res = sb("x_res", [P, D])
        junk = sb("junk", [P, D])
        xn = sb("xn", [P, D])
        hT = sb("hT", [P, KD, P])
        qk = sb("qk", [P, AW + KVW])
        qk_sq = sb("qk_sq", [P, AW + KVW])
        qn = sb("qn", [P, AW])
        kn = sb("kn", [P, NKV, 2, HD])
        qT = sb("qT", [P, NH // 2, P])
        kT = sb("kT", [P, NKV, 2, P])
        v_keys = sb("v_keys", [P, 2, KVW])
        conv_u = sb("conv_u", [P, 2, P])
        conv_x = sb("conv_x", [P, CC, P + 2])
        conv_t = sb("conv_t", [P, 3, P])
        conv_y = sb("conv_y", [P, CC, P])
        conv_sq = sb("conv_sq", [P, CC, P])
        conv_s = sb("conv_s", [P, CC, P])
        probs = sb("probs", [P, NH, 2 * P])
        pT = sb("pT", [P, 2, 2 * P])
        attn = sb("attn", [P, AW])
        attnT = sb("attnT", [P, CC, P])
        x1 = sb("x1", [P, D])
        h2 = sb("h2", [P, D])
        h2T = sb("h2T", [P, KD, P])
        small = sb("small", [P, 160])
        rel_const = x1[:, 0:2 * REL_W + P]
        vector_rows = h2[0:42, 0:P]
        rel_row = h2T[:].rearrange("p k q -> p (k q)")[0:NH, 0:REL_W]
        best_i = sb("best_i", [P, 8], U32)
        hot = sb("hot", [P, TOP_K, NE])
        hot_g = sb("hot_g", [P, TOP_K, NE])
        used = [0]

        def cols(n):
            used[0] += n
            return small[:, used[0] - n:used[0]]

        ss_x, ms_x, rstd_x = cols(1), cols(1), cols(1)
        ss_qk, ms_qk, rstd_qk = cols(NH + NKV), cols(NH + NKV), cols(NH + NKV)
        top, neg_top, sink_gap, sink_exp = cols(NH), cols(NH), cols(NH), cols(NH)
        row_sum, denom, rdenom = cols(NH), cols(NH), cols(NH)
        ss_ca, ms_ca, rstd_ca = cols(2), cols(2), cols(2)
        ss_f, ms_f, rstd_f = cols(1), cols(1), cols(1)
        best, neg_best, best_f = cols(8), cols(1), cols(8)
        exp4, sum4, rsum4, gate4 = cols(TOP_K), cols(1), cols(1), cols(TOP_K)
        route_sc = sb("route_sc", [P, NE])

        ps_q = ps("ps_q", [P, 512])
        ps_kv = ps("ps_kv", [P, 512])
        ps_c = ps("ps_c", [P, 2, 512])
        ps_s = ps("ps_s", [P, 2048])
        ps_heads = ps_s[:].rearrange("p (h k) -> p h k", h=NH)
        ps_route = ps_s[:, 1024:1024 + NE]

        early_loaded = sem("early_loaded")
        late_loaded = sem("late_loaded")
        qkv_w_loaded = sem("qkv_w_loaded")
        conv_w_loaded = [sem(f"conv_w_loaded{c}") for c in range(CC)]
        out_w_loaded = sem("out_w_loaded")
        cleared = sem("buffers_cleared")
        scale_made = sem("scale_made")
        slots_made = sem("slots_made")
        rel_summed = sem("rel_summed")
        vectors_turned = sem("vectors_turned")
        vectors_ready = sem("vectors_ready")
        rel_made = sem("rel_made")
        rel_stored = sem("rel_stored")
        bias_loaded = sem("bias_loaded")
        bias_turned = sem("bias_turned")
        bias_flipped = sem("bias_flipped")
        x_loaded = event("x_loaded", 16)
        x_squared = event("x_squared")
        x_mean = event("x_mean")
        x_rstd = event("x_rstd")
        x_normed = event("x_normed")
        x_turned = [event("x_turned_a"), event("x_turned_b")]
        hT_ready = [event("hT_ready_a"), event("hT_ready_b")]
        qkv_done = event("qkv_done")
        qk_ready = event("qk_ready")
        v_shifted = event("v_shifted")
        v_ready = event("v_ready")
        qk_squared = event("qk_squared")
        qk_summed = event("qk_summed")
        qk_mean = event("qk_mean")
        qk_rstd = event("qk_rstd")
        qk_normed = event("qk_normed")
        conv_done = [event(f"conv_done{c}") for c in range(CC)]
        u_ready = [event(f"u_ready{c}") for c in range(CC)]
        conv_out = [event(f"conv_out{c}", 1, 1) for c in range(CC)]
        conv_squared = event("conv_squared")
        conv_scaled = event("conv_scaled")
        conv_summed = event("conv_summed")
        qk_turned = event("qk_turned")
        k_shifted = event("k_shifted")
        qT_ready = event("qT_ready")
        scored = [event(f"scored_{i}") for i in ("even", "odd")]
        biased = [event(f"biased_{i}") for i in ("even", "odd")]
        bias_switched = event("bias_switched", 1, 1)
        neg_ready = [event(f"neg_ready_{i}") for i in ("even", "odd")]
        exped = [event(f"exped{h}") for h in range(NH)]
        sink_exped = event("sink_exped")
        p_turned = [event(f"p_turned{h}") for h in range(NH)]
        pT_ready = [event(f"pT_ready{h}") for h in range(NH)]
        av_done = [event(f"av_done{h}", 1, 1) for h in range(NH)]
        attn_ready = event("attn_ready")
        attn_squared = event("attn_squared")
        attn_turned = event("attn_turned")
        attnT_ready = event("attnT_ready")
        ca_mean = event("conv_attn_mean")
        ca_rstd = event("conv_attn_rstd")
        res_loaded = event("res_loaded", 16)
        res_biased = event("res_biased")
        conv_mixed = event("conv_mixed")
        attn_mixed = event("attn_mixed")
        x1_ready = event("x1_ready", 1, 1)
        x1_squared = event("x1_squared")
        f_mean = event("ffn_mean")
        f_rstd = event("ffn_rstd")
        h2_ready = event("h2_ready")
        h2_turned = [event("h2_turned_a"), event("h2_turned_b")]
        h2T_ready = [event("h2T_ready_a"), event("h2T_ready_b")]
        routed = event("routed")
        logits_read = event("logits_read", 1, 1)
        stored = event("rows_stored", 32, 1)
        best_ready = event("best_ready")
        best_exped = event("best_exped")
        vstep = Steps(sem("vector_step"), 32)

        ctx.callback(clear_sems, nc, all_sems)
        block = ctx.enter_context(nc.Block())

        early = [
            (rel_const, const[:, C_HOT:C_W]),
            (rel_bias_sb[:], rel_bias),
            (sink_row[:], sinks[0].partition_broadcast(P)),
            (cst[:], const[:, 0:C_HOT]),
            (vector_rows[0:8, :], norm_mix.rearrange("o (k p) -> (o k) p", p=P)),
            (vector_rows[8:20, :], b_in[:, 0:QKV0].rearrange("o (k p) -> (o k) p", p=P)),
            (vector_rows[20:32, :], conv_w.rearrange("o j (c p) -> (o j c) p", p=P)),
            (vector_rows[32:36, :], out_norm_conv.rearrange("o (k p) -> (o k) p", p=P)),
            (vector_rows[36:40, :], out_norm_attn.rearrange("o (k p) -> (o k) p", p=P)),
            (vector_rows[40:41, 0:HD], q_norm),
            (vector_rows[40:41, HD:P], q_norm),
            (vector_rows[41:42, 0:HD], k_norm),
            (vector_rows[41:42, HD:P], k_norm),
            (b_qkv_row[:], b_in[0, QKV0:IN_W].partition_broadcast(P)),
        ]
        late = [
            (b_out_row[:], b_out[0].partition_broadcast(P)),
            (norm_ffn_row[:], norm_ffn[0].partition_broadcast(P)),
            (b_router_row[:], b_router[0].partition_broadcast(P)),
            (w_router_sb[:], w_router[0].rearrange("(k p) e -> p k e", p=P)),
        ]
        all_early, all_late = 16 * len(early), 16 * len(late)

        def wait(eng, e, t):
            eng.wait_ge(e.sem, e.of(t))

        @block.sync
        def _(sp):
            w_rows = w_in[0].rearrange("(k p) n -> p k n", p=P)
            sp.dma_start(x_in[:], x_rows[0:P, :]).then_inc(x_loaded.sem, 16)
            for dst, src in early:
                sp.dma_start(dst, src).then_inc(early_loaded, 16)
            sp.dma_start(w_in_sb[:, :, QKV0:IN_W], w_rows[:, :, QKV0:IN_W]).then_inc(qkv_w_loaded, 16)
            sp.wait_ge(rel_made, 1)
            sp.dma_start(rel_rows, rel_row).then_inc(rel_stored, 16)

            def load_conv_w(c):
                for j in range(3):
                    first = j * CW + c * P
                    sp.dma_start(w_in_sb[:, :, first:first + P], w_rows[:, :, first:first + P]).then_inc(conv_w_loaded[c], 16)

            load_conv_w(0)
            sp.wait_ge(rel_stored, 16)
            slanted = bass.AP(tensor=rel_rows.tensor, offset=0, ap=[[1, P], [REL_W, NH], [1, 2 * P]])
            sp.dma_start(probs[:], slanted).then_inc(bias_loaded, 16)
            for c in range(1, CC):
                load_conv_w(c)
            for dst, src in late:
                sp.dma_start(dst, src).then_inc(late_loaded, 16)
            sp.dma_start(w_out_sb[:], w_out[0].rearrange("(k p) n -> p k n", p=P)).then_inc(out_w_loaded, 16)

            def load_block(n, rows):
                wait(sp, x_normed, n)
                sp.dma_start(x_in[:], rows).then_inc(x_loaded.sem, 16)

            def load_residual(t):
                wait(sp, x1_ready, t - 1)
                sp.dma_start(x_res[:], x_rows[bass.ds(t * P, P), :]).then_inc(res_loaded.sem, 16)

            with sp.Fori(0, NB - 1) as t:
                load_block(t, x_rows[bass.ds((t + 1) * P, P), :])
                load_residual(t)
            load_block(NB - 1, x_rows[(NB - 1) * P:NB * P, :])
            load_residual(NB - 1)

        @block.gpsimd
        def _(pool):
            for e in credited:
                pool.sem_inc(e.sem, e.unit * e.credit)
            nc.gpsimd.memset(minus_half[:], -0.5).then_inc(cleared, 1)
            nc.gpsimd.memset(v_keys[:], 0.0).then_inc(cleared, 1)
            nc.gpsimd.memset(kT[:], 0.0).then_inc(cleared, 1)
            nc.gpsimd.memset(conv_x[:], 0.0).then_inc(cleared, 1)
            nc.gpsimd.memset(bias_all[:, :, 0:P], MASKED).then_inc(cleared, 1)
            pool.wait_ge(cleared, 5)

            def rsqrt(mean, t, src, dst, done):
                wait(pool, mean, t)
                nc.gpsimd.tensor_tensor(dst, src, minus_half[:, 0:src.shape[1]], ALU.pow).then_inc(done.sem, 1)

            rsqrt(x_mean, 0, ms_x, rstd_x, x_rstd)
            rsqrt(qk_mean, 0, ms_qk, rstd_qk, qk_rstd)
            pool.wait_ge(early_loaded, all_early)
            pool.wait_ge(late_loaded, all_late)
            pool.wait_ge(bias_flipped, 2)
            with pool.Fori(0, NB) as t:
                wait(pool, res_loaded, t)
                nc.gpsimd.tensor_tensor(x_res[:], x_res[:], b_out_row[:], ALU.add).then_inc(res_biased.sem, 1)
                wait(pool, biased[1], t)
                nc.gpsimd.tensor_tensor(bias_all[:, :, 0:P], bias_prev[:],
                                        cst[:, C_ONES:C_ONES + P].unsqueeze(1).broadcast_to([P, NH, P]),
                                        ALU.mult).then_inc(bias_switched.sem, 1)
                rsqrt(x_mean, t + 1, ms_x, rstd_x, x_rstd)
                rsqrt(ca_mean, t, ms_ca, rstd_ca, ca_rstd)
                rsqrt(f_mean, t, ms_f, rstd_f, f_rstd)
                rsqrt(qk_mean, t + 1, ms_qk, rstd_qk, qk_rstd)

        @block.scalar
        def _(act):
            def prepare(n):
                wait(act, x_loaded, n)
                nc.scalar.activation(junk[:], x_in[:], ACT.Square, accum_out=ss_x).then_inc(x_squared.sem, 1)
                wait(act, x_rstd, n)
                nc.scalar.activation(xn[:], x_in[:], ACT.Copy, scale=rstd_x).then_inc(x_normed.sem, 1)

            def square_qk(n):
                wait(act, qk_ready, n)
                nc.scalar.activation(qk_sq[:], qk[:], ACT.Square).then_inc(qk_squared.sem, 1)

            def add_u_bias(t, c):
                wait(act, conv_done[c], t)
                if c < 2:
                    wait(act, conv_out[c + 2], t - 1)
                else:
                    wait(act, conv_out[c - 2], t)
                nc.scalar.activation(conv_u[:, c % 2, :], ps_c[:, c % 2, 2 * P:3 * P], ACT.Identity,
                                     bias=b_in_col[:, 2 * CC + c:2 * CC + c + 1]).then_inc(u_ready[c].sem, 1)

            prepare(0)
            act.wait_ge(vectors_ready, 1)
            nc.scalar.activation(q_scale_col[:], q_norm_col, ACT.Copy, scale=HD ** -0.5).then_inc(scale_made, 1)
            square_qk(0)
            act.wait_ge(scale_made, 1)
            act.wait_ge(cleared, 5)
            with act.Fori(0, NB) as t:
                add_u_bias(t, 0)
                add_u_bias(t, 1)
                wait(act, qk_turned, t)
                nc.scalar.copy(kT[:, :, 0, :], kT[:, :, 1, :]).then_inc(k_shifted.sem, 1)
                wait(act, k_shifted, t)
                nc.scalar.activation(kT[:, :, 1, :], ps_s[:, 512:512 + 2 * P].rearrange("p (v k) -> p v k", v=2),
                                     ACT.Copy, scale=k_norm_col)
                nc.scalar.activation(qT[:].rearrange("p h q -> p (h q)"), ps_s[:, 0:512],
                                     ACT.Copy, scale=q_scale_col[:]).then_inc(qT_ready.sem, 1)
                add_u_bias(t, 2)
                for s in range(NH):
                    if s % HALF == 0:
                        wait(act, neg_ready[s // HALF], t)
                    nc.scalar.activation(probs[:, s, :], probs[:, s, :], ACT.Exp, bias=neg_top[:, s:s + 1],
                                         accum_out=row_sum[:, s:s + 1]).then_inc(exped[s].sem, 1)
                add_u_bias(t, 3)
                nc.scalar.activation(sink_exp, sink_gap, ACT.Exp).then_inc(sink_exped.sem, 1)
                wait(act, conv_out[3], t)
                nc.scalar.activation(conv_sq[:], conv_y[:], ACT.Square).then_inc(conv_squared.sem, 1)
                prepare(t + 1)
                wait(act, attn_ready, t)
                nc.scalar.activation(junk[:, 0:AW], attn[:], ACT.Square, accum_out=ss_ca[:, 1:2]).then_inc(attn_squared.sem, 1)
                wait(act, x1_ready, t)
                nc.scalar.activation(junk[:], x1[:], ACT.Square, accum_out=ss_f).then_inc(x1_squared.sem, 1)
                act.dma_start(out_rows[bass.ds(t * P, P), :], x1[:]).then_inc(stored.sem, 16)
                wait(act, h2_ready, t)
                act.dma_start(h2_rows[bass.ds(t * P, P), :], h2[:]).then_inc(stored.sem, 16)
                for i in range(2):
                    wait(act, h2_turned[i], t)
                    nc.scalar.copy(h2T[:, 4 * i:4 * i + 4, :], ps_s[:, 512 * i:512 * i + 512].rearrange(
                        "p (k q) -> p k q", k=4)).then_inc(h2T_ready[i].sem, 1)
                square_qk(t + 1)
                wait(act, best_ready, t)
                nc.scalar.activation(exp4, best[:, 0:TOP_K], ACT.Exp, bias=neg_best,
                                     accum_out=sum4).then_inc(best_exped.sem, 1)
            wait(act, stored, NB - 1)

        @block.vector
        def _(dve):
            def mean(ss, ms, width):
                return nc.vector.tensor_scalar(ms, ss, 1.0 / width, EPS, ALU.mult, ALU.add)

            def x_to_mean(n):
                wait(dve, x_squared, n)
                mean(ss_x, ms_x, D).then_inc(x_mean.sem, 1)

            def read_hT(n, i):
                wait(dve, x_turned[i], n)
                nc.vector.tensor_tensor(hT[:, 4 * i:4 * i + 4, :],
                                        ps_c[:, i, :].rearrange("p (k q) -> p k q", k=4),
                                        norm_mix_col[:, 4 * i:4 * i + 4].unsqueeze(2).broadcast_to([P, 4, P]),
                                        ALU.mult).then_inc(hT_ready[i].sem, 1)

            def read_qkv(n):
                wait(dve, qkv_done, n)
                nc.vector.tensor_tensor(qk[:, 0:AW], ps_q[:], b_qkv_row[:, 0:AW], ALU.add)
                nc.vector.tensor_tensor(qk[:, AW:AW + KVW], ps_kv[:, 0:KVW], b_qkv_row[:, AW:AW + KVW],
                                        ALU.add).then_inc(qk_ready.sem, 1)
                nc.vector.tensor_copy(v_keys[:, 0, :], v_keys[:, 1, :]).then_inc(v_shifted.sem, 1)
                wait(dve, v_shifted, n)
                nc.vector.tensor_tensor(v_keys[:, 1, :], ps_kv[:, KVW:2 * KVW], b_qkv_row[:, AW + KVW:],
                                        ALU.add).then_inc(v_ready.sem, 1)

            def norm_qk(n):
                wait(dve, qk_squared, n)
                nc.vector.tensor_reduce(ss_qk, qk_sq[:].rearrange("p (h d) -> p h d", d=HD), AX_X,
                                        ALU.add).then_inc(qk_summed.sem, 1)
                wait(dve, qk_summed, n)
                mean(ss_qk, ms_qk, HD).then_inc(qk_mean.sem, 1)
                wait(dve, qk_rstd, n)
                nc.vector.tensor_tensor(qn[:].rearrange("p (h d) -> p h d", d=HD),
                                        qk[:, 0:AW].rearrange("p (h d) -> p h d", d=HD),
                                        rstd_qk[:, 0:NH].unsqueeze(2).broadcast_to([P, NH, HD]), ALU.mult)
                for j in range(2):
                    last = nc.vector.tensor_tensor(kn[:, :, j, :],
                                                   qk[:, AW:].rearrange("p (h d) -> p h d", d=HD),
                                                   rstd_qk[:, NH:].unsqueeze(2).broadcast_to([P, NKV, HD]), ALU.mult)
                last.then_inc(qk_normed.sem, 1)

            def convolve(t, c, steps=range(5)):
                gate_b, gate_c = ps_c[:, c % 2, 0:P], ps_c[:, c % 2, P:2 * P]
                for step in steps:
                    if step == 0:
                        wait(dve, conv_done[c], t)
                        wait(dve, u_ready[c], t)
                        vstep.did(nc.vector.scalar_tensor_tensor(
                            out=conv_x[:, c, 2:], in0=gate_c, scalar=b_in_col[:, CC + c:CC + c + 1],
                            in1=conv_u[:, c % 2, :], op0=ALU.add, op1=ALU.mult))
                        continue
                    dve.wait_ge(vstep.sem, vstep.value(t))
                    if step == 1:
                        vstep.did(nc.vector.tensor_scalar(conv_t[:, 0, :], conv_x[:, c, 2:],
                                                          conv_w_col[:, 2, c:c + 1], None, ALU.mult))
                    elif step == 2:
                        vstep.did(nc.vector.scalar_tensor_tensor(
                            out=conv_t[:, 1, :], in0=conv_x[:, c, 1:P + 1], scalar=conv_w_col[:, 1, c:c + 1],
                            in1=conv_t[:, 0, :], op0=ALU.mult, op1=ALU.add))
                    elif step == 3:
                        vstep.did(nc.vector.scalar_tensor_tensor(
                            out=conv_t[:, 2, :], in0=conv_x[:, c, 0:P], scalar=conv_w_col[:, 0, c:c + 1],
                            in1=conv_t[:, 1, :], op0=ALU.mult, op1=ALU.add))
                    else:
                        nc.vector.scalar_tensor_tensor(
                            out=conv_y[:, c, :], in0=gate_b, scalar=b_in_col[:, c:c + 1], in1=conv_t[:, 2, :],
                            op0=ALU.add, op1=ALU.mult).then_inc(conv_out[c].sem, 1)

            def then_wait(t, ins):
                vstep.did(ins)
                dve.wait_ge(vstep.sem, vstep.value(t))

            def add_bias(t, i):
                part = slice(i * HALF, (i + 1) * HALF)
                nc.vector.tensor_tensor(probs[:, part, :], ps_heads[:, part, :], bias_all[:, part, :],
                                        ALU.add).then_inc(biased[i].sem, 1)

            def find_top(t, i):
                part = slice(i * HALF, (i + 1) * HALF)
                then_wait(t, nc.vector.tensor_tensor(top[:, part], denom[:, part], sink_slots[:, part], ALU.max))
                nc.vector.tensor_tensor(sink_gap[:, part], sink_slots[:, part], top[:, part], ALU.subtract)
                nc.vector.tensor_scalar(neg_top[:, part], top[:, part], -1.0, None,
                                        ALU.mult).then_inc(neg_ready[i].sem, 1)

            dve.wait_ge(early_loaded, all_early)
            nc.vector.tensor_copy(sink_slots[:].rearrange("p (b a) -> p b a", b=2),
                                  sink_row[:].rearrange("p (a b) -> p b a", b=2)).then_inc(slots_made, 1)
            nc.vector.tensor_copy(rel_bias_slots[:].rearrange("p (b a) -> p b a", b=2),
                                  rel_bias_sb[:].rearrange("p (a b) -> p b a", b=2)).then_inc(slots_made, 1)
            dve.wait_ge(rel_summed, 1)
            nc.vector.tensor_tensor(rel_row, ps_s[0:NH, 0:REL_W], rel_const[0:NH, REL_W:2 * REL_W],
                                    ALU.add).then_inc(rel_made, 1)
            dve.wait_ge(vectors_turned, 1)
            nc.vector.tensor_copy(vectors[:], ps_s[:, 512:554]).then_inc(vectors_ready, 1)
            dve.wait_ge(vectors_ready, 1)
            dve.wait_ge(slots_made, 2)
            dve.wait_ge(cleared, 5)
            x_to_mean(0)
            read_hT(0, 0)
            read_hT(0, 1)
            read_qkv(0)
            norm_qk(0)
            dve.wait_ge(bias_turned, 1)
            nc.vector.tensor_copy(bias_prev[:], ps_heads[:, :, 0:P]).then_inc(bias_flipped, 1)
            nc.vector.tensor_copy(bias_all[:, :, P:2 * P], ps_heads[:, :, P:2 * P]).then_inc(bias_flipped, 1)
            dve.wait_ge(bias_flipped, 2)
            with dve.Fori(0, NB) as t:
                vstep.n = 0
                then_wait(t, nc.vector.tensor_copy(conv_x[:, :, 0:2], conv_x[:, :, P:P + 2]))
                convolve(t, 0)
                convolve(t, 1)
                convolve(t, 2)
                wait(dve, scored[0], t)
                wait(dve, bias_switched, t - 1)
                wait(dve, av_done[NH - 1], t - 1)
                add_bias(t, 0)
                wait(dve, biased[0], t)
                then_wait(t, nc.vector.tensor_reduce(denom[:, 0:HALF], probs[:, 0:HALF, :], AX_X, ALU.max))
                wait(dve, scored[1], t)
                add_bias(t, 1)
                find_top(t, 0)
                wait(dve, biased[1], t)
                then_wait(t, nc.vector.tensor_reduce(denom[:, HALF:NH], probs[:, HALF:NH, :], AX_X, ALU.max))
                find_top(t, 1)
                for s in range(NH):
                    wait(dve, p_turned[s], t)
                    if s >= 2:
                        wait(dve, av_done[s - 2], t)
                    nc.vector.tensor_copy(pT[:, s % 2, :], (ps_q, ps_kv)[s % 2][:, 0:2 * P]).then_inc(pT_ready[s].sem, 1)
                    if s == 2:
                        convolve(t, 3, range(0, 2))
                    elif s == 3:
                        convolve(t, 3, range(2, 4))
                    elif s == 4:
                        convolve(t, 3, range(4, 5))
                    elif s == 5:
                        wait(dve, conv_out[3], t)
                        nc.vector.tensor_tensor(conv_s[:], conv_y[:], conv_g_col.unsqueeze(2).broadcast_to([P, CC, P]),
                                                ALU.mult).then_inc(conv_scaled.sem, 1)
                wait(dve, sink_exped, t)
                then_wait(t, nc.vector.tensor_tensor(denom, row_sum, sink_exp, ALU.add))
                then_wait(t, nc.vector.reciprocal(rdenom, denom))
                x_to_mean(t + 1)
                wait(dve, av_done[NH - 1], t)
                nc.vector.tensor_tensor(attn[:].rearrange("p (a b d) -> p b a d", b=2, d=HD),
                                        ps_c[:, 0, :].rearrange("p (a b d) -> p b a d", b=2, d=HD),
                                        rdenom.rearrange("p (b a) -> p b a", b=2).unsqueeze(3).broadcast_to(
                                            [P, 2, NH // 2, HD]), ALU.mult).then_inc(attn_ready.sem, 1)
                wait(dve, conv_summed, t)
                nc.vector.tensor_reduce(ss_ca[:, 0:1], ps_kv[:, 2 * P:2 * P + CC], AX_X, ALU.add).then_inc(vstep.sem, 1)
                vstep.n += 1
                wait(dve, attn_turned, t)
                nc.vector.tensor_tensor(attnT[:], ps_c[:, 1, :].rearrange("p (c q) -> p c q", c=CC),
                                        attn_g_col.unsqueeze(2).broadcast_to([P, CC, P]),
                                        ALU.mult).then_inc(attnT_ready.sem, 1)
                dve.wait_ge(vstep.sem, vstep.value(t))
                wait(dve, attn_squared, t)
                mean(ss_ca, ms_ca, CW).then_inc(ca_mean.sem, 1)
                read_hT(t + 1, 0)
                wait(dve, conv_mixed, t)
                wait(dve, ca_rstd, t)
                wait(dve, res_biased, t)
                wait(dve, stored, t - 1)
                dve.wait_ge(late_loaded, all_late)
                then_wait(t, nc.vector.scalar_tensor_tensor(out=x1[:], in0=ps_s[:, 0:D], scalar=rstd_ca[:, 0:1],
                                                            in1=x_res[:], op0=ALU.mult, op1=ALU.add))
                wait(dve, attn_mixed, t)
                nc.vector.scalar_tensor_tensor(out=x1[:], in0=ps_s[:, D:2 * D], scalar=rstd_ca[:, 1:2],
                                               in1=x1[:], op0=ALU.mult, op1=ALU.add).then_inc(x1_ready.sem, 1)
                read_hT(t + 1, 1)
                wait(dve, x1_squared, t)
                mean(ss_f, ms_f, D).then_inc(f_mean.sem, 1)
                wait(dve, f_rstd, t)
                nc.vector.scalar_tensor_tensor(out=h2[:], in0=x1[:], scalar=rstd_f, in1=norm_ffn_row[:],
                                               op0=ALU.mult, op1=ALU.mult).then_inc(h2_ready.sem, 1)
                read_qkv(t + 1)
                norm_qk(t + 1)
                wait(dve, routed, t)
                nc.vector.tensor_tensor(route_sc[:], ps_route, b_router_row[:], ALU.add).then_inc(logits_read.sem, 1)
                wait(dve, logits_read, t)
                nc.vector.tensor_copy(best_f[:, 0:1], route_sc[:, 0:1])
                then_wait(t, nc.vector.max(best, route_sc[:]))
                nc.vector.tensor_scalar(neg_best, best[:, 0:1], -1.0, None, ALU.mult).then_inc(best_ready.sem, 1)
                then_wait(t, nc.vector.max_index(best_i[:], best, route_sc[:]))
                then_wait(t, nc.vector.tensor_copy(best_f, best_i[:]))
                then_wait(t, nc.vector.tensor_tensor(
                    hot[:], cst[:, C_E:C_E + NE].unsqueeze(1).broadcast_to([P, TOP_K, NE]),
                    best_f[:, 0:TOP_K].unsqueeze(2).broadcast_to([P, TOP_K, NE]), ALU.is_equal))
                nc.vector.tensor_reduce(picked[:, bass.ds(t, 1), :].rearrange("p o e -> p (o e)"),
                                        hot[:].rearrange("p k e -> p e k"), AX_X, ALU.add)
                wait(dve, best_exped, t)
                then_wait(t, nc.vector.reciprocal(rsum4, sum4))
                then_wait(t, nc.vector.tensor_scalar(gate4, exp4, rsum4, None, ALU.mult))
                then_wait(t, nc.vector.tensor_tensor(hot_g[:], hot[:], gate4.unsqueeze(2).broadcast_to([P, TOP_K, NE]),
                                                     ALU.mult))
                nc.vector.tensor_reduce(gates[:, bass.ds(t, 1), :].rearrange("p o e -> p (o e)"),
                                        hot_g[:].rearrange("p k e -> p e k"), AX_X, ALU.add)
                assert vstep.n == vstep.per, vstep.n

        @block.tensor
        def _(pe):
            def turn_x(n, i):
                for k in range(4 * i, 4 * i + 4):
                    last = pe.transpose(ps_c[:, i, (k % 4) * P:(k % 4 + 1) * P], xn[:, k * P:(k + 1) * P], ident)
                last.then_inc(x_turned[i].sem, 1)

            def project_q(n):
                for k in range(KD):
                    if k % 4 == 0:
                        wait(pe, hT_ready[k // 4], n)
                    pe.matmul(ps_q[:], hT[:, k, :], w_in_sb[:, k, QKV0:QKV0 + AW], start=(k == 0), stop=(k == KD - 1))

            def project_kv(n):
                for k in range(KD):
                    last = pe.matmul(ps_kv[:, 0:2 * KVW], hT[:, k, :], w_in_sb[:, k, QKV0 + AW:IN_W],
                                     start=(k == 0), stop=(k == KD - 1))
                last.then_inc(qkv_done.sem, 1)

            def project_conv(t, c):
                pe.wait_ge(conv_w_loaded[c], 48)
                for j in range(3):
                    for k in range(KD):
                        first = j * CW + c * P
                        last = pe.matmul(ps_c[:, c % 2, j * P:(j + 1) * P], w_in_sb[:, k, first:first + P],
                                         hT[:, k, :], start=(k == 0), stop=(k == KD - 1))
                last.then_inc(conv_done[c].sem, 1)

            def turn_p(t, s):
                wait(pe, exped[s], t)
                if s >= 2:
                    wait(pe, pT_ready[s - 2], t)
                for j in range(2):
                    last = pe.transpose((ps_q, ps_kv)[s % 2][:, j * P:(j + 1) * P], probs[:, s, j * P:(j + 1) * P], ident)
                last.then_inc(p_turned[s].sem, 1)

            def attend(t, s):
                h = head_of(s)
                kv = h // (NH // NKV)
                wait(pe, pT_ready[s], t)
                for j in range(2):
                    last = pe.matmul(ps_c[:, 0, h * HD:(h + 1) * HD], pT[:, s % 2, j * P:(j + 1) * P],
                                     v_keys[:, j, kv * HD:(kv + 1) * HD], start=(j == 0), stop=(j == 1))
                last.then_inc(av_done[s].sem, 1)

            pe.wait_ge(early_loaded, all_early)
            pe.wait_ge(slots_made, 2)
            pe.matmul(ps_s[0:NH, 0:REL_W], rel_bias_slots[:], rel_const[0:NBUCKET, 0:REL_W],
                      start=True, stop=True).then_inc(rel_summed, 1)
            pe.transpose(ps_s[:, 512:554], vector_rows, ident[0:42, 0:42]).then_inc(vectors_turned, 1)
            wait(pe, x_normed, 0)
            turn_x(0, 0)
            turn_x(0, 1)
            pe.wait_ge(qkv_w_loaded, 16)
            project_q(0)
            project_kv(0)
            pe.wait_ge(bias_loaded, 16)
            pe.wait_ge(vectors_ready, 1)
            for i in range(4):
                last = pe.matmul(ps_s[:, i * 512:(i + 1) * 512], rel_const[:, 2 * REL_W:], probs[:, 2 * i:2 * i + 2, :].rearrange(
                    "p h k -> p (h k)"), start=True, stop=True)
            last.then_inc(bias_turned, 1)
            with pe.Fori(0, NB) as t:
                project_conv(t, 0)
                project_conv(t, 1)
                wait(pe, qk_normed, t)
                pe.wait_ge(bias_flipped, 2)
                for i in range(NH // 2):
                    pe.transpose(ps_s[:, i * P:(i + 1) * P], qn[:, i * P:(i + 1) * P], ident)
                for i in range(NKV):
                    last = pe.transpose(ps_s[:, 512 + i * P:512 + (i + 1) * P],
                                        kn[:, i, :, :].rearrange("p j d -> p (j d)"), ident)
                last.then_inc(qk_turned.sem, 1)
                wait(pe, conv_out[0], t)
                project_conv(t, 2)
                wait(pe, qT_ready, t)
                wait(pe, logits_read, t - 1)
                for s in range(NH):
                    h = head_of(s)
                    a = HD * (h % 2)
                    last = pe.matmul(ps_heads[:, s, :], qT[a:a + HD, h // 2, :],
                                     kT[a:a + HD, h // (NH // NKV), :, :].rearrange("p j k -> p (j k)"),
                                     start=True, stop=True)
                    if s % HALF == HALF - 1:
                        last.then_inc(scored[s // HALF].sem, 1)
                wait(pe, conv_out[1], t)
                project_conv(t, 3)
                turn_p(t, 0)
                for s in range(NH):
                    if s + 1 < NH:
                        turn_p(t, s + 1)
                    if s == 0:
                        wait(pe, conv_out[2], t)
                        wait(pe, v_ready, t)
                    attend(t, s)
                wait(pe, conv_squared, t)
                for c in range(CC):
                    last = pe.matmul(ps_kv[:, 2 * P + c:2 * P + c + 1], conv_sq[:, c, :], cst[:, C_ONES:C_ONES + 1],
                                     start=True, stop=True)
                last.then_inc(conv_summed.sem, 1)
                wait(pe, conv_scaled, t)
                wait(pe, biased[1], t)
                pe.wait_ge(out_w_loaded, 16)
                for n in range(2):
                    for k in range(CC):
                        last = pe.matmul(ps_s[:, n * 512:(n + 1) * 512], conv_s[:, k, :],
                                         w_out_sb[:, k, n * 512:(n + 1) * 512], start=(k == 0), stop=(k == CC - 1))
                    if n == 0:
                        wait(pe, attn_ready, t)
                        wait(pe, conv_out[3], t)
                        for c in range(CC):
                            turned = pe.transpose(ps_c[:, 1, c * P:(c + 1) * P], attn[:, c * P:(c + 1) * P], ident)
                        turned.then_inc(attn_turned.sem, 1)
                last.then_inc(conv_mixed.sem, 1)
                wait(pe, x_normed, t + 1)
                turn_x(t + 1, 0)
                wait(pe, attnT_ready, t)
                for n in range(2):
                    for k in range(CC):
                        last = pe.matmul(ps_s[:, D + n * 512:D + (n + 1) * 512], attnT[:, k, :],
                                         w_out_sb[:, CC + k, n * 512:(n + 1) * 512], start=(k == 0), stop=(k == CC - 1))
                last.then_inc(attn_mixed.sem, 1)
                turn_x(t + 1, 1)
                project_q(t + 1)
                wait(pe, h2_ready, t)
                for i in range(2):
                    for k in range(4 * i, 4 * i + 4):
                        last = pe.transpose(ps_s[:, k * P:(k + 1) * P], h2[:, k * P:(k + 1) * P], ident)
                    last.then_inc(h2_turned[i].sem, 1)
                project_kv(t + 1)
                pe.wait_ge(late_loaded, all_late)
                for k in range(KD):
                    if k % 4 == 0:
                        wait(pe, h2T_ready[k // 4], t)
                    last = pe.matmul(ps_route, h2T[:, k, :], w_router_sb[:, k, :], start=(k == 0), stop=(k == KD - 1))
                last.then_inc(routed.sem, 1)


def experts(nc, h2_rows, out_rows, w1, b1, w2, b2, cst, picked, gates):
    ident = cst[:, C_ID:C_ID + P]
    ones = cst[:, C_ONES:C_ONES + P]
    last_size = len(SIZES) - 1
    second_rows = ((SIZES.index(144), 16), (SIZES.index(192), 64), (last_size, P))
    with ExitStack() as ctx:
        def sb(name, shape, dt=F32):
            return ctx.enter_context(nc.sbuf_tensor(name, shape, dt))

        def ps(name, shape):
            return ctx.enter_context(nc.psum_tensor(name, shape, F32))

        def sem(name):
            return ctx.enter_context(nc.semaphore(name))

        credited = []

        def event(name, unit=1, credit=0):
            e = Event(sem(name), unit, credit)
            if credit:
                credited.append(e)
            return e

        def wait(eng, e, t):
            eng.wait_ge(e.sem, e.of(t))

        w_slot = sb("w_slot", [P, PIECES, KD, PW])
        b1T = sb("b1T", [P, 2 * P1, NE])
        b2T = sb("b2T", [P, KD, NE])
        b1_cur = sb("b1_cur", [P, 2 * P1])
        b2_cur = sb("b2_cur", [P, KD])
        place = sb("place", [P, NB, NE])
        gate_parts = sb("gate_parts", [P, NB, 3, NE], BF16)
        base_row = sb("base_row", [P, P])
        job_row = sb("job_row", [1, 2 * P], I32)
        jobs = sb("jobs", [1, 2], I32)
        iota_b = sb("iota_b", [P, CAP], BF16)
        place_cur = sb("place_cur", [P, NB])
        token = sb("token", [P, NB])
        match = sb("match", [P, NB, CAP], BF16)
        entry = sb("entry", [P, NB, 5], BF16)
        list_sb = sb("list_sb", [P, 2, 5])
        gate_next = sb("gate_next", [P, 2])
        idx_next = sb("idx_next", [P, 2], I32)
        gate_cur = sb("gate_cur", [P, 2])
        idx_cur = sb("idx_cur", [P, 2], I32)
        x_got = sb("x_got", [P, 2, D])
        xT = sb("xT", [P, KD, CAP])
        glu = sb("glu", [P, 3, CAP])
        lin = sb("lin", [P, 3, CAP])
        sig = sb("sig", [P, 3, CAP])
        act_T = sb("act_T", [P, P1, CAP])
        yT = sb("yT", [P, KD, CAP])
        b2_rows = yT[:].rearrange("p m n -> p (m n)")[:, 0:D]
        y_rows = sb("y_rows", [P, 2, D])
        carrier = sb("carrier", [P, 3])
        before = sb("before", [P, NB + 1, NE])
        counts = sb("counts", [P, NE])
        rank = sb("rank", [P, NB, NE])
        other = sb("other", [P, NB, NE])
        n_jobs = sb("n_jobs", [P, NE])
        over = sb("over", [P, 2, NE])
        last_job = sb("last_job", [P, NE])
        ended = sb("ended", [P, NE])
        pick_e = sb("pick_e", [P, 2, NE])
        limits = sb("limits", [P, 2, last_size])
        fields = sb("fields", [P, 3])
        narrow = sb("narrow", [P, 8])

        ps_unit = [ps(f"ps_unit{i}", [P, 2, CAP]) for i in range(3)]
        ps_list = ps("ps_list", [P, 512])
        ps_x = [ps(f"ps_x{i}", [P, 2, CAP]) for i in range(2)]
        ps_y = [ps(f"ps_y{i}", [P, 2, 2, P]) for i in range(2)]

        biases_turned = sem("biases_turned")
        biases_read = sem("biases_read")
        carrier_cleared = sem("carrier_cleared")
        buffers = sem("expert_buffers_cleared")
        sums_ready = sem("sums_ready")
        ranked = sem("ranked")
        fields_ready = sem("fields_ready")
        fields_spread = sem("fields_spread")
        table_ready = sem("table_ready")
        rstep = Steps(sem("routing_step"), 0)
        units_cleared = sem("units_cleared")
        place_taken = event("place_taken")
        entry_ready = event("entry_ready")
        matched = event("matched")
        gate_summed = event("gate_summed")
        listed = event("listed")
        list_read = event("list_read")
        idx_ready = event("idx_ready")
        gathered_a = event("gathered_a", 16)
        gathered_b = event("gathered_b", 16)
        x_turned = [event(f"x_rows_turned{i}") for i in range(4)]
        xT_ready = [event(f"xT_ready{i}") for i in range(4)]
        w_loaded = [event(f"w_loaded{p}", 16) for p in range(PIECES)]
        unit_done = [event(f"unit_done{p}", 1, 1) for p in range(PIECES)]
        unit_read = [event(f"unit_read{p}", 1, 1) for p in range(PIECES)]
        b1_ready = event("b1_ready")
        cur_ready = event("cur_ready")
        b2_ready = event("b2_ready")
        sig_ready = [event(f"sig_ready{p}") for p in range(P1)]
        scaled = [event(f"scaled{p}") for p in range(P1)]
        act_ready = [event(f"act_ready{p}") for p in range(P1)]
        y_turned = [event(f"y_turned{i}") for i in range(4)]
        y_read = [event(f"y_read{i}", 1, 1) for i in range(4)]
        pool_moved = Event(sem("pool_moved"), 32, 1)
        carried = [event(f"carried{i}", 1, 1) for i in range(2)]

        block = ctx.enter_context(nc.Block())

        def job_loop(eng):
            eng.wait_ge(table_ready, 3)
            n = eng.value_load(jobs[0:1, 0:1], min_val=1, max_val=NE + S * TOP_K // CAP)
            return eng.Fori(0, n)

        def expert_of(eng, q):
            return eng.value_load(job_row[0:1, bass.ds(q, 1)], min_val=0, max_val=NE - 1)

        def size_at(q):
            return job_row[0:1, bass.ds(q + P, 1)]

        def size_of(eng, q):
            return eng.value_load(size_at(q), min_val=0, max_val=last_size)


        @block.sync
        def _(sp):
            def load_piece(p, e):
                w, first = (w1, p * PW) if p < P1 else (w2, (p - P1) * PW)
                src = w[0, e, :, first:first + PW].rearrange("o (k p) f -> p (o k) f", p=P)
                sp.dma_start(w_slot[:, p, :, :], src).then_inc(w_loaded[p].sem, 16)

            sp.wait_ge(pool_moved.sem, 32)
            for p in range(EARLY_PIECES):
                load_piece(p, slice(0, 1))
            wait(sp, gathered_b, 0)
            for p in range(EARLY_PIECES, PIECES):
                load_piece(p, slice(0, 1))
            sp.wait_ge(table_ready, 3)
            n = sp.value_load(jobs[0:1, 0:1], min_val=1, max_val=NE + S * TOP_K // CAP)
            with sp.Fori(1, n) as q:
                e = expert_of(sp, q)
                for p in range(PIECES):
                    wait(sp, unit_done[p], q - 1)
                    load_piece(p, bass.ds(e, 1))

        @block.gpsimd
        def _(pool):
            for e in credited:
                pool.sem_inc(e.sem, e.unit * e.credit)
            pool.dma_start(y_rows[0:NE, :, :].rearrange("e h f -> e (h f)"), b1[0]).then_inc(pool_moved.sem, 16)
            pool.dma_start(b2_rows[0:NE, :], b2[0]).then_inc(pool_moved.sem, 16)
            nc.gpsimd.memset(carrier[:], 0.0).then_inc(carrier_cleared, 1)
            nc.gpsimd.memset(x_got[:], 0.0).then_inc(buffers, 1)
            pool.wait_ge(carrier_cleared, 1)

            def second_block(size, move):
                (small, a), (middle, b), (_, c) = second_rows
                with pool.If(size > small):
                    with pool.If(size > middle):
                        move(c)
                    with pool.Else():
                        move(b)
                with pool.Else():
                    move(a)


            def carry_wait(q, i):
                wait(pool, carried[i], q - 1)
                nc.gpsimd.tensor_tensor(carrier[:, i:i + 1], carrier[:, 2:3], carrier[:, 2:3],
                                        ALU.add).then_inc(carried[i].sem, 1)

            def gather(t):
                def get(done, i, n):
                    nc.gpsimd.indirect_dma_start(
                        out=x_got[0:n, i, :], out_offset=None, in_=h2_rows,
                        in_offset=bass.IndirectOffsetOnAxis(ap=idx_next[0:n, i:i + 1], axis=0)).then_inc(done.sem, 16)

                get(gathered_a, 0, P)
                second_block(size_of(pool, t), lambda n: get(gathered_b, 1, n))

            def scatter(t):
                def put(i, n):
                    nc.gpsimd.indirect_dma_start(
                        out=out_rows, out_offset=bass.IndirectOffsetOnAxis(ap=idx_cur[0:n, i:i + 1], axis=0),
                        in_=y_rows[0:n, i, :], in_offset=None, compute_op=ALU.add).then_inc(pool_moved.sem, 16)

                put(0, P)
                second_block(size_of(pool, t), lambda n: put(1, n))

            pool.wait_ge(buffers, 1)
            pool.wait_ge(table_ready, 3)
            wait(pool, idx_ready, 0)
            gather(0)
            with job_loop(pool) as q:
                wait(pool, x_turned[3], q)
                wait(pool, idx_ready, q + 1)
                carry_wait(q, 0)
                gather(q + 1)
                wait(pool, pool_moved, q - 1)
                wait(pool, y_read[3], q)
                carry_wait(q, 1)
                scatter(q)
            pool.wait_ge(gathered_a.sem, 16)
            n = pool.value_load(jobs[0:1, 0:1], min_val=1, max_val=NE + S * TOP_K // CAP)
            wait(pool, pool_moved, n - 1)

        @block.scalar
        def _(act):
            for bank in (*(u[:].rearrange("p u n -> p (u n)") for u in ps_unit),
                         *(y[:].rearrange("p h u n -> p (h u n)") for y in ps_y)):
                nc.scalar.activation(bank, cst[:, 0:2 * CAP], ACT.Copy, scale=0.0).then_inc(units_cleared, 1)
            act.wait_ge(biases_read, 3)
            with job_loop(act) as q:
                e = expert_of(act, q)
                wait(act, unit_read[PIECES - 1], q - 1)
                nc.scalar.copy(b2_cur[:], b2T[:, :, bass.ds(e, 1)].rearrange("p m o -> p (m o)")).then_inc(b2_ready.sem, 1)
                for p in range(P1):
                    wait(act, unit_read[p], q)
                    nc.scalar.activation(sig[:, p % 3, :], glu[:, p % 3, :], ACT.Sigmoid,
                                         scale=ALPHA).then_inc(sig_ready[p].sem, 1)
                wait(act, b2_ready, q)
                for p in range(P1, PIECES):
                    wait(act, unit_done[p], q)
                    for u in range(2):
                        m = 2 * (p - P1) + u
                        last = nc.scalar.activation(yT[:, m, :], ps_unit[p % 3][:, u, :], ACT.Identity,
                                                    bias=b2_cur[:, m:m + 1])
                    last.then_inc(unit_read[p].sem, 1)

        @block.vector
        def _(dve):
            v = nc.vector

            def then_wait(ins):
                rstep.did(ins)
                dve.wait_ge(rstep.sem, rstep.n)

            then_wait(v.memset(before[:, 0, :], 0.0))
            for b in range(NB):
                then_wait(v.tensor_tensor(before[:, b + 1, :], before[:, b, :], picked[:, b, :], ALU.add))
            v.tensor_copy(iota_b[:], cst[:, C_IOTA:C_IOTA + CAP])
            v.tensor_copy(entry[:, :, 0], cst[:, C_TOK:C_TOK + NB])
            v.tensor_copy(entry[:, :, 1], cst[:, C_TOK + NB:C_TOK + 2 * NB]).then_inc(sums_ready, 1)
            then_wait(v.scalar_tensor_tensor(out=token[:], in0=cst[:, C_TOK:C_TOK + NB], scalar=32.0,
                                             in1=cst[:, C_TOK + NB:C_TOK + 2 * NB], op0=ALU.mult, op1=ALU.add))
            then_wait(v.tensor_copy(gate_parts[:, :, 0, :], gates[:]))
            then_wait(v.tensor_tensor(other[:], gates[:], gate_parts[:, :, 0, :], ALU.subtract))
            then_wait(v.tensor_copy(gate_parts[:, :, 1, :], other[:]))
            then_wait(v.tensor_tensor(gates[:], other[:], gate_parts[:, :, 1, :], ALU.subtract))
            then_wait(v.tensor_copy(gate_parts[:, :, 2, :], gates[:]))
            dve.wait_ge(ranked, 1)
            v.tensor_copy(rank[:], ps_list[:, 0:NB * NE].rearrange("p (b e) -> p b e", b=NB))
            then_wait(v.tensor_copy(counts[:], ps_list[:, NB * NE:NB * NE + NE]))
            then_wait(v.tensor_tensor(other[:], counts[:].unsqueeze(1).broadcast_to([P, NB, NE]), rank[:], ALU.subtract))
            then_wait(v.tensor_tensor(other[:], other[:], token[:].unsqueeze(2).broadcast_to([P, NB, NE]), ALU.add))
            then_wait(v.tensor_tensor(rank[:], rank[:], other[:], ALU.subtract))
            then_wait(v.tensor_tensor(rank[:], rank[:], picked[:], ALU.mult))
            then_wait(v.tensor_tensor(place[:], rank[:], other[:], ALU.add))
            then_wait(v.tensor_scalar(over[:, 0, :], counts[:], float(CAP), 1.0, ALU.is_gt, ALU.add))
            for i in range(2, S // CAP):
                then_wait(v.tensor_scalar(over[:, 1, :], counts[:], float(CAP * i), None, ALU.is_gt))
                then_wait(v.tensor_tensor(over[:, 0, :], over[:, 0, :], over[:, 1, :], ALU.add))
            then_wait(v.tensor_tensor_scan(last_job[:], cst[:, C_ONES:C_ONES + NE], over[:, 0, :], 0.0, ALU.mult, ALU.add))
            job = cst[:, C_PART:C_PART + 1]
            then_wait(v.tensor_scalar(ended[:], last_job[:], job, None, ALU.is_le))
            then_wait(v.tensor_tensor(pick_e[:, 0, :], ended[:], over[:, 0, :], ALU.mult))
            v.tensor_reduce(narrow[:, 0:1], ended[:], AX_X, ALU.add)
            then_wait(v.tensor_reduce(narrow[:, 1:2], pick_e[:, 0, :], AX_X, ALU.add))
            then_wait(v.tensor_scalar(fields[:, 0:1], narrow[:, 0:1], NE - 1.0, None, ALU.min))
            then_wait(v.tensor_tensor(narrow[:, 2:3], job, narrow[:, 1:2], ALU.subtract))
            then_wait(v.tensor_scalar(fields[:, 2:3], narrow[:, 2:3], float(CAP), None, ALU.mult))
            then_wait(v.tensor_scalar(pick_e[:, 1, :], cst[:, C_E:C_E + NE], fields[:, 0:1], None, ALU.is_equal))
            then_wait(v.tensor_tensor(pick_e[:, 0, :], pick_e[:, 1, :], counts[:], ALU.mult))
            then_wait(v.tensor_reduce(narrow[:, 3:4], pick_e[:, 0, :], AX_X, ALU.add))
            then_wait(v.tensor_tensor(narrow[:, 4:5], narrow[:, 3:4], fields[:, 2:3], ALU.subtract))
            assert SIZES[:-1] == tuple(SIZES[0] + SIZE_STEP * i for i in range(last_size))
            then_wait(v.tensor_scalar(limits[:, 0, :], cst[:, C_IOTA:C_IOTA + last_size], float(SIZE_STEP), float(SIZES[0]),
                                      ALU.mult, ALU.add))
            then_wait(v.tensor_scalar(limits[:, 1, :], limits[:, 0, :], narrow[:, 4:5], None, ALU.is_lt))
            v.tensor_reduce(fields[:, 1:2], limits[:, 1, :], AX_X, ALU.add).then_inc(fields_ready, 1)
            dve.wait_ge(fields_spread, 1)
            v.tensor_copy(jobs[0:1, 0:1], last_job[0:1, NE - 1:NE]).then_inc(table_ready, 1)
            v.tensor_copy(job_row[:], ps_list[0:1, 0:2 * P]).then_inc(table_ready, 1)
            v.tensor_copy(base_row[:], ps_list[:, 2 * P:3 * P]).then_inc(table_ready, 1)
            def match_tokens(t, e):
                v.tensor_scalar(place_cur[:], place[:, :, bass.ds(e, 1)].rearrange("p b o -> p (b o)"),
                                base_row[:, bass.ds(t, 1)], None, ALU.subtract).then_inc(place_taken.sem, 1)
                v.tensor_copy(entry[:, :, 2:5], gate_parts[:, :, :, bass.ds(e, 1)].rearrange("p b g o -> p b (g o)"))
                wait(dve, place_taken, t)
                for b in range(NB):
                    last = v.tensor_scalar(match[:, b, :], iota_b[:], place_cur[:, b:b + 1], None, ALU.is_equal)
                last.then_inc(matched.sem, 1)

            def read_list(t):
                wait(dve, listed, t)
                lists = ps_list[:, 0:10].rearrange("p (h f) -> p h f", h=2)
                v.tensor_copy(list_sb[:], lists).then_inc(list_read.sem, 1)
                wait(dve, list_read, t)
                v.scalar_tensor_tensor(out=idx_next[:], in0=list_sb[:, :, 0], scalar=32.0, in1=list_sb[:, :, 1],
                                       op0=ALU.mult, op1=ALU.add).then_inc(idx_ready.sem, 1)
                v.tensor_reduce(gate_next[:], list_sb[:, :, 2:5], AX_X, ALU.add).then_inc(gate_summed.sem, 1)

            def read_xT(t, i):
                wait(dve, x_turned[i], t)
                v.tensor_copy(xT[:, 2 * i:2 * i + 2, :], ps_x[i % 2][:]).then_inc(xT_ready[i].sem, 1)

            def clip(q, p):
                wait(dve, unit_done[p], q)
                v.tensor_scalar(glu[:, p % 3, :], ps_unit[p % 3][:, 0, :], b1_cur[:, 2 * p:2 * p + 1], LIMIT,
                                ALU.add, ALU.min)
                v.tensor_scalar(lin[:, p % 3, :], ps_unit[p % 3][:, 1, :], b1_cur[:, 2 * p + 1:2 * p + 2], LIMIT + 1.0,
                                ALU.add, ALU.min).then_inc(unit_read[p].sem, 1)

            def finish(q, p):
                wait(dve, sig_ready[p], q)
                v.tensor_tensor(sig[:, p % 3, :], sig[:, p % 3, :], glu[:, p % 3, :], ALU.mult).then_inc(scaled[p].sem, 1)
                wait(dve, scaled[p], q)
                v.scalar_tensor_tensor(out=act_T[:, p, :], in0=lin[:, p % 3, :], scalar=1.0 - LIMIT, in1=sig[:, p % 3, :],
                                       op0=ALU.max, op1=ALU.mult).then_inc(act_ready[p].sem, 1)

            def read_y(q, i):
                wait(dve, y_turned[i], q)
                for h in range(2):
                    last = v.tensor_scalar(y_rows[:, h, i * PW:(i + 1) * PW],
                                           ps_y[i % 2][:, h, :, :].rearrange("p u c -> p (u c)"),
                                           gate_cur[:, h:h + 1], None, ALU.mult)
                last.then_inc(y_read[i].sem, 1)

            dve.wait_ge(table_ready, 3)
            match_tokens(0, expert_of(dve, 0))
            read_list(0)
            dve.wait_ge(biases_turned, 1)
            turned = ps_x[0][:].rearrange("p a b -> p (a b)").rearrange("p (j u e) -> p j u e", u=2, e=NE)
            b1_units = b1T[:].rearrange("p (j u) e -> p j u e", u=2)
            v.tensor_copy(b1_units[:, :, 0, :], turned[:, :, 0, :]).then_inc(biases_read, 1)
            v.tensor_scalar(b1_units[:, :, 1, :], turned[:, :, 1, :], 1.0, None, ALU.add).then_inc(biases_read, 1)
            v.tensor_copy(b2T[:], ps_x[1][:].rearrange("p a b -> p (a b)")[:, 0:KD * NE].rearrange(
                "p (m e) -> p m e", e=NE)).then_inc(biases_read, 1)
            for i in range(4):
                read_xT(0, i)
            dve.wait_ge(biases_read, 3)
            with job_loop(dve) as q:
                e = expert_of(dve, q)
                e_next = expert_of(dve, q + 1)
                v.tensor_copy(b1_cur[:], b1T[:, :, bass.ds(e, 1)].rearrange("p m o -> p (m o)")).then_inc(b1_ready.sem, 1)
                wait(dve, b1_ready, q)
                for p in range(P1):
                    clip(q, p)
                    if p >= 1:
                        finish(q, p - 1)
                    if p == 1:
                        match_tokens(q + 1, e_next)
                    if p == 4:
                        wait(dve, gate_summed, q)
                        wait(dve, pool_moved, q - 1)
                        v.tensor_copy(idx_cur[:], idx_next[:])
                        v.tensor_copy(gate_cur[:], gate_next[:]).then_inc(cur_ready.sem, 1)
                        wait(dve, cur_ready, q)
                        read_list(q + 1)
                finish(q, P1 - 1)
                for i in range(4):
                    if i >= 1:
                        read_y(q, i - 1)
                    read_xT(q + 1, i)
                read_y(q, 3)

        @block.tensor
        def _(pe):
            def list_tokens(t):
                wait(pe, matched, t)
                for h in range(2):
                    for b in range(NB):
                        last = pe.matmul(ps_list[:, 5 * h:5 * h + 5], match[:, b, h * P:(h + 1) * P], entry[:, b, :],
                                         start=(b == 0), stop=(b == NB - 1))
                last.then_inc(listed.sem, 1)

            def turn_x(t, i):
                if i == 0:
                    wait(pe, gathered_a, t)
                    wait(pe, gathered_b, t)
                if i >= 2:
                    wait(pe, xT_ready[i - 2], t)
                for c in range(2):
                    for h in range(2):
                        k = 2 * i + c
                        last = pe.transpose(ps_x[i % 2][:, c, h * P:(h + 1) * P], x_got[:, h, k * P:(k + 1) * P], ident)
                last.then_inc(x_turned[i].sem, 1)

            def turn_y(q, i, n):
                wait(pe, unit_read[P1 + i], q)
                wait(pe, y_read[(i + 2) % 4], q - 1 if i < 2 else q)
                for u in range(2):
                    for h in range(1 if n <= P else 2):
                        last = pe.transpose(ps_y[i % 2][:, h, u, :], yT[:, 2 * i + u, h * P:(h + 1) * P], ident)
                last.then_inc(y_turned[i].sem, 1)

            def piece(q, p, n):
                wait(pe, w_loaded[p], q)
                wait(pe, unit_read[(p + 9) % PIECES], q - 1 if p < 3 else q)
                for u in range(2):
                    for k in range(KD):
                        if p == 0 and u == 0 and k % 2 == 0:
                            wait(pe, xT_ready[k // 2], q)
                        if p == P1 and u == 0 and k in (0, 6, 7):
                            wait(pe, act_ready[max(k, 5)], q)
                        if p < P1:
                            w, moving = w_slot[:, p, k, u::2], xT
                        else:
                            w, moving = w_slot[:, p, k, u * P:(u + 1) * P], act_T
                        last = pe.matmul(ps_unit[p % 3][:, u, 0:n], w, moving[:, k, 0:n],
                                         start=(k == 0), stop=(k == KD - 1))
                last.then_inc(unit_done[p].sem, 1)

            def run_job(q, n):
                for p in range(PIECES):
                    piece(q, p, n)
                    if p == 3:
                        list_tokens(q + 1)
                    if p == P1 - 1:
                        turn_x(q + 1, 0)
                        turn_x(q + 1, 1)
                        pe.reg_load(next_size, size_at(q + 1))
                    if p > P1:
                        if p == PIECES - 1:
                            turn_x(q + 1, 2)
                        turn_y(q, p - P1 - 1, n)
                turn_x(q + 1, 3)
                turn_y(q, 3, n)

            def pick_size(q, size, lo, hi):
                if hi - lo == 1:
                    run_job(q, SIZES[lo])
                    return
                mid = (lo + hi) // 2
                with pe.If(size < mid):
                    pick_size(q, size, lo, mid)
                with pe.Else():
                    pick_size(q, size, mid, hi)

            pe.wait_ge(sums_ready, 1)
            pe.matmul(ps_list[:, 0:NB * NE], cst[:, C_TRI:C_TRI + P], picked[:].rearrange("p b e -> p (b e)"),
                      start=True, stop=False)
            pe.matmul(ps_list[:, 0:NB * NE], ones, before[:, 0:NB, :].rearrange("p b e -> p (b e)"),
                      start=False, stop=True)
            pe.matmul(ps_list[:, NB * NE:NB * NE + NE], ones, before[:, NB, :], start=True, stop=True).then_inc(ranked, 1)
            pe.wait_ge(pool_moved.sem, 32)
            for m in range(2 * P1):
                first = (m // 2) * PW + m % 2
                pe.transpose(ps_x[0][:].rearrange("p a b -> p (a b)")[:, m * NE:(m + 1) * NE],
                             y_rows[0:NE, :, :].rearrange("e h f -> e (h f)")[:, first:first + PW - 1:2], ident[0:NE, 0:NE])
            for m in range(KD):
                last = pe.transpose(ps_x[1][:].rearrange("p a b -> p (a b)")[:, m * NE:(m + 1) * NE],
                                    b2_rows[0:NE, m * P:(m + 1) * P], ident[0:NE, 0:NE])
            last.then_inc(biases_turned, 1)
            pe.wait_ge(fields_ready, 1)
            for f in range(3):
                last = pe.matmul(ps_list[:, f * P:(f + 1) * P], fields[:, f:f + 1].broadcast_to([P, P]), ident,
                                 start=True, stop=True)
            last.then_inc(fields_spread, 1)
            pe.wait_ge(table_ready, 3)
            list_tokens(0)
            pe.wait_ge(biases_read, 3)
            pe.wait_ge(units_cleared, 5)
            for i in range(4):
                turn_x(0, i)
            next_size = pe.alloc_register("next_size")
            pe.reg_load(next_size, size_at(0))
            with job_loop(pe) as q:
                pick_size(q, pe.snap(next_size, min_val=0, max_val=last_size), 0, len(SIZES))


def program(nc, x, norm_mix, w_in, b_in, conv_w, q_norm, k_norm, sinks, rel_bias, out_norm_conv,
            out_norm_attn, w_out, b_out, norm_ffn, w_router, b_router, w1, b1, w2, b2, const, out):
    x_rows = x.rearrange("o s d -> (o s) d")
    out_rows = out.rearrange("o s d -> (o s) d")
    h2_rows = nc.dram_tensor("h2_rows", (S, D), F32, kind="Internal").ap()
    rel_rows = nc.dram_tensor("rel_rows", (NH, REL_W), F32, kind="Internal").ap()
    with ExitStack() as ctx:
        cst = ctx.enter_context(nc.sbuf_tensor("cst", [P, C_HOT], F32))
        picked = ctx.enter_context(nc.sbuf_tensor("picked", [P, NB, NE], F32))
        gates = ctx.enter_context(nc.sbuf_tensor("gates", [P, NB, NE], F32))
        mixer(nc, x_rows, out_rows, h2_rows, rel_rows, norm_mix, w_in, b_in, conv_w, q_norm, k_norm, sinks,
              rel_bias, out_norm_conv, out_norm_attn, w_out, b_out, norm_ffn, w_router, b_router, const,
              cst, picked, gates)
        experts(nc, h2_rows, out_rows, w1, b1, w2, b2, cst, picked, gates)


_INS = ["x", "norm_mix", "w_in", "b_in", "conv_w", "q_norm", "k_norm", "sinks", "rel_bias", "out_norm_conv",
        "out_norm_attn", "w_out", "b_out", "norm_ffn", "w_router", "b_router", "w1", "b1", "w2", "b2"]


def kernel(**inputs):
    import numpy as _np
    import concourse.bacc as _bacc
    from concourse import mybir as _mybir
    from concourse.bass_utils import run_bass_kernel_spmd as _run

    nc = _bacc.Bacc("TRN2", target_bir_lowering=False, num_devices=1)
    arrays, args = {}, []
    for name in _INS:
        a = _np.ascontiguousarray(inputs[name])
        arrays[f"in_{name}_dram"] = a
        args.append(nc.dram_tensor(f"in_{name}_dram", a.shape, _mybir.dt.from_np(a.dtype), kind="ExternalInput").ap())
    const = constants()
    arrays["const_dram"] = const
    args.append(nc.dram_tensor("const_dram", const.shape, F32, kind="ExternalInput").ap())
    args.append(nc.dram_tensor("out_dram", (1, S, D), F32, kind="ExternalOutput").ap())
    program(nc, *args)
    r = _run(nc, [arrays], core_ids=[0])
    return r.results[0]["out_dram"]
```

```python
from contextlib import ExitStack

import numpy as np
import concourse.bass as bass
from concourse import mybir

ALU = mybir.AluOpType
ACT = mybir.ActivationFunctionType
F32 = mybir.dt.float32
BF16 = mybir.dt.bfloat16
I32 = mybir.dt.int32
U32 = mybir.dt.uint32
AX_X = mybir.AxisListType.X

P = 128
D = 1024
S = 1024
NB = S // P
KD = D // P
CW = 512
CC = CW // P
HD = 64
NH = 8
HALF = NH // 2
NKV = 2
AW = NH * HD
KVW = NKV * HD
QKV0 = 3 * CW
IN_W = 3 * CW + AW + 2 * KVW
NBUCKET = 32
MAX_DISTANCE = 128
NE = 32
TOP_K = 4
LIMIT = 7.0
ALPHA = 1.702
EPS = 1e-5
MASKED = -1e30

CAP = 256
SIZE_STEP = 8
SIZES = tuple(range(P, 209, SIZE_STEP)) + (CAP,)
PIECES = 12
P1 = 8
LOADS = PIECES // 2
EARLY_LOADS = 1
PW = 256
REL_W = 384

C_ID, C_TRI, C_IOTA, C_ONES, C_E, C_PART, C_TOK, C_HOT = 0, 128, 256, 512, 640, 672, 673, 689
C_MASK = C_HOT + REL_W
C_FLIP = C_MASK + REL_W
C_W = C_FLIP + P


def constants():
    c = np.zeros((P, C_W), np.float32)
    p = np.arange(P)
    c[:, C_ID:C_ID + P] = np.eye(P)
    c[:, C_TRI:C_TRI + P] = p[:, None] < p[None, :]
    c[:, C_IOTA:C_IOTA + CAP] = np.arange(CAP)
    c[:, C_ONES:C_ONES + P] = 1.0
    c[:, C_E:C_E + NE] = np.arange(NE)
    c[:, C_PART] = p
    tok = p[:, None] + P * np.arange(NB)[None, :]
    c[:, C_TOK:C_TOK + NB] = tok // 32
    c[:, C_TOK + NB:C_TOK + 2 * NB] = tok % 32
    half = NBUCKET // 2
    rel = 255 - np.arange(REL_W)
    n = np.maximum(rel, 1).astype(np.float32)
    large = half + (np.log(n / half) / np.log(MAX_DISTANCE / half) * (NBUCKET - half)).astype(np.int32)
    bucket = np.where(rel < half, np.maximum(rel, 0), np.minimum(large, NBUCKET - 1))
    c[:NBUCKET, C_HOT:C_HOT + REL_W] = bucket[None, :] == np.arange(NBUCKET)[:, None]
    c[:, C_MASK:C_MASK + REL_W] = np.where((rel >= 0) & (rel < P), 0.0, MASKED)[None, :]
    c[:, C_FLIP:C_FLIP + P] = np.eye(P)[::-1]
    return c


class Event:

    def __init__(self, sem, unit=1, credit=0):
        self.sem, self.unit, self.credit = sem, unit, credit

    def of(self, t):
        n = t + (1 + self.credit)
        return n if self.unit == 1 else n * self.unit


class Steps:

    def __init__(self, sem, per):
        self.sem, self.per, self.n = sem, per, 0

    def did(self, ins):
        ins.then_inc(self.sem, 1)
        self.n += 1

    def value(self, t):
        return t * self.per + self.n


def clear_sems(nc, sems):
    numbers = sorted(s.num for s in sems)
    assert numbers == list(range(numbers[0], numbers[-1] + 1))
    nc.all_engine_barrier(sems_to_clear=range(numbers[0], numbers[-1] + 1))


def head_of(s):
    return HALF * (s // HALF) + 2 * (s % 2) + s % HALF // 2


def mixer(nc, x_rows, out_rows, h2_rows, rel_rows, norm_mix, w_in, b_in, conv_w, q_norm, k_norm, sinks,
          rel_bias, out_norm_conv, out_norm_attn, w_out, b_out, norm_ffn, w_router, b_router, const,
          cst, picked, gates, before):
    ident = cst[:, C_ID:C_ID + P]
    with ExitStack() as ctx:
        def sb(name, shape, dt=F32):
            return ctx.enter_context(nc.sbuf_tensor(name, shape, dt))

        def ps(name, shape):
            return ctx.enter_context(nc.psum_tensor(name, shape, F32))

        all_sems = []

        def sem(name):
            all_sems.append(ctx.enter_context(nc.semaphore(name)))
            return all_sems[-1]

        credited = []

        def event(name, unit=1, credit=0):
            e = Event(sem(name), unit, credit)
            if credit:
                credited.append(e)
            return e

        w_in_sb = sb("w_in_sb", [P, KD, IN_W])
        w_out_sb = sb("w_out_sb", [P, KD, D])
        w_router_sb = sb("w_router_sb", [P, KD, NE])
        norm_ffn_row = sb("norm_ffn_row", [P, D])
        vectors = sb("vectors", [P, 42])
        norm_mix_col = vectors[:, 0:8]
        b_in_col = vectors[:, 8:20]
        conv_w_col = vectors[:, 20:32].rearrange("p (j c) -> p j c", j=3)
        conv_g_col = vectors[:, 32:36]
        attn_g_col = vectors[:, 36:40]
        q_norm_col = vectors[:, 40:41]
        k_norm_col = vectors[:, 41:42]
        b_qkv_row = sb("b_qkv_row", [P, AW + 2 * KVW])
        b_out_row = sb("b_out_row", [P, D])
        b_router_row = sb("b_router_row", [P, NE])
        q_scale_col = sb("q_scale_col", [P, 1])
        sink_row = sb("sink_row", [P, NH])
        rel_bias_sb = sb("rel_bias_sb", [NBUCKET, NH])
        rel_bias_slots = sb("rel_bias_slots", [NBUCKET, NH])
        sink_slots = sb("sink_slots", [P, NH])
        minus_half = sb("minus_half", [P, NH + NKV])
        bias_prev = sb("bias_prev", [P, NH, P])
        bias_all = sb("bias_all", [P, NH, 2 * P])

        x_in = sb("x_in", [P, D])
        x_res = sb("x_res", [P, D])
        junk = sb("junk", [P, D])
        xn = sb("xn", [P, D])
        hT = sb("hT", [P, KD, P])
        qk = sb("qk", [P, AW + KVW])
        qk_sq = sb("qk_sq", [P, AW + KVW])
        qn = sb("qn", [P, AW])
        kn = sb("kn", [P, NKV, 2, HD])
        qT = sb("qT", [P, NH // 2, P])
        kT = sb("kT", [P, NKV, 2, P])
        v_keys = sb("v_keys", [P, 2, KVW])
        conv_u = sb("conv_u", [P, 2, P])
        conv_x = sb("conv_x", [P, CC, P + 2])
        conv_t = sb("conv_t", [P, 3, P])
        conv_y = sb("conv_y", [P, CC, P])
        conv_sq = sb("conv_sq", [P, CC, P])
        conv_s = sb("conv_s", [P, CC, P])
        probs = sb("probs", [P, NH, 2 * P])
        pT = sb("pT", [P, 2, 2 * P])
        attn = sb("attn", [P, AW])
        attnT = sb("attnT", [P, CC, P])
        x1 = sb("x1", [P, D])
        h2 = sb("h2", [P, D])
        h2T = sb("h2T", [P, KD, P])
        small = sb("small", [P, 160])
        rel_const = x1[:, 0:2 * REL_W + P]
        vector_rows = h2[0:42, 0:P]
        rel_row = h2T[:].rearrange("p k q -> p (k q)")[0:NH, 0:REL_W]
        best_i = sb("best_i", [P, 8], U32)
        hot = sb("hot", [P, TOP_K, NE])
        hot_g = sb("hot_g", [P, TOP_K, NE])
        used = [0]

        def cols(n):
            used[0] += n
            return small[:, used[0] - n:used[0]]

        ss_x, ms_x, rstd_x = cols(1), cols(1), cols(1)
        ss_qk, ms_qk, rstd_qk = cols(NH + NKV), cols(NH + NKV), cols(NH + NKV)
        top, neg_top, sink_gap, sink_exp = cols(NH), cols(NH), cols(NH), cols(NH)
        row_sum, denom, rdenom = cols(NH), cols(NH), cols(NH)
        ss_ca, ms_ca, rstd_ca = cols(2), cols(2), cols(2)
        ss_f, ms_f, rstd_f = cols(1), cols(1), cols(1)
        best, neg_best, best_f = cols(8), cols(1), cols(8)
        exp4, sum4, rsum4, gate4 = cols(TOP_K), cols(1), cols(1), cols(TOP_K)
        route_sc = sb("route_sc", [P, NE])

        ps_q = ps("ps_q", [P, 512])
        ps_kv = ps("ps_kv", [P, 512])
        ps_c = ps("ps_c", [P, 2, 512])
        ps_s = ps("ps_s", [P, 2048])
        ps_heads = ps_s[:].rearrange("p (h k) -> p h k", h=NH)
        ps_route = ps_s[:, 1024:1024 + NE]

        early_loaded = sem("early_loaded")
        late_loaded = sem("late_loaded")
        qkv_b_loaded = sem("qkv_b_loaded")
        qkv_w_loaded = [sem(f"qkv_w_loaded{i}") for i in range(2)]
        conv_w_loaded = [sem(f"conv_w_loaded{c}") for c in range(CC)]
        out_w_loaded = sem("out_w_loaded")
        cleared = sem("buffers_cleared")
        scale_made = sem("scale_made")
        slots_made = sem("slots_made")
        rel_summed = sem("rel_summed")
        vectors_turned = sem("vectors_turned")
        vectors_ready = sem("vectors_ready")
        rel_made = sem("rel_made")
        rel_stored = sem("rel_stored")
        bias_loaded = sem("bias_loaded")
        bias_turned = sem("bias_turned")
        bias_flipped = sem("bias_flipped")
        x_loaded = event("x_loaded", 16)
        x_squared = event("x_squared")
        x_mean = event("x_mean")
        x_rstd = event("x_rstd")
        x_normed = event("x_normed")
        x_turned = [event("x_turned_a"), event("x_turned_b")]
        hT_ready = [event("hT_ready_a"), event("hT_ready_b")]
        qkv_done = event("qkv_done")
        qk_ready = event("qk_ready")
        v_shifted = event("v_shifted")
        v_ready = event("v_ready")
        qk_squared = event("qk_squared")
        qk_summed = event("qk_summed")
        qk_mean = event("qk_mean")
        qk_rstd = event("qk_rstd")
        qk_normed = event("qk_normed")
        conv_done = [event(f"conv_done{c}") for c in range(CC)]
        u_ready = [event(f"u_ready{c}") for c in range(CC)]
        conv_out = [event(f"conv_out{c}", 1, 1) for c in range(CC)]
        conv_squared = event("conv_squared")
        conv_scaled = event("conv_scaled")
        conv_summed = event("conv_summed")
        qk_turned = event("qk_turned")
        k_shifted = event("k_shifted")
        qT_ready = event("qT_ready")
        scored = [event(f"scored_{i}") for i in ("first", "second")]
        biased = [event(f"biased_{i}") for i in ("first", "second")]
        bias_switched = event("bias_switched", 1, 1)
        neg_ready = [event(f"neg_ready_{i}") for i in ("first", "second")]
        exped = [event(f"exped{h}") for h in range(NH)]
        sink_exped = event("sink_exped")
        p_turned = [event(f"p_turned{h}") for h in range(NH)]
        pT_ready = [event(f"pT_ready{h}") for h in range(NH)]
        av_done = [event(f"av_done{h}", 1, 1) for h in range(NH)]
        attn_ready = event("attn_ready")
        attn_squared = event("attn_squared")
        attn_turned = event("attn_turned")
        attnT_ready = event("attnT_ready")
        ca_mean = event("conv_attn_mean")
        ca_rstd = event("conv_attn_rstd")
        res_loaded = event("res_loaded", 16)
        res_biased = event("res_biased")
        conv_mixed = event("conv_mixed")
        attn_mixed = event("attn_mixed")
        x1_ready = event("x1_ready", 1, 1)
        x1_squared = event("x1_squared")
        f_mean = event("ffn_mean")
        f_rstd = event("ffn_rstd")
        h2_ready = event("h2_ready")
        h2_turned = [event("h2_turned_a"), event("h2_turned_b")]
        h2T_ready = [event("h2T_ready_a"), event("h2T_ready_b")]
        routed = event("routed")
        logits_read = event("logits_read", 1, 1)
        stored = event("rows_stored", 32, 1)
        best_ready = event("best_ready")
        best_exped = event("best_exped")
        vstep = Steps(sem("vector_step"), 21)
        pstep = Steps(sem("pool_step"), 8)
        gated = [event(f"gated{c}") for c in range(CC)]
        tapped = [event(f"tapped{c}") for c in range(CC)]

        ctx.callback(clear_sems, nc, all_sems)
        block = ctx.enter_context(nc.Block())

        early = [
            (rel_const, const[:, C_HOT:C_W]),
            (rel_bias_sb[:], rel_bias),
            (sink_row[:], sinks[0].partition_broadcast(P)),
            (cst[:], const[:, 0:C_HOT]),
            (vector_rows[0:8, :], norm_mix.rearrange("o (k p) -> (o k) p", p=P)),
            (vector_rows[8:20, :], b_in[:, 0:QKV0].rearrange("o (k p) -> (o k) p", p=P)),
            (vector_rows[20:32, :], conv_w.rearrange("o j (c p) -> (o j c) p", p=P)),
            (vector_rows[32:36, :], out_norm_conv.rearrange("o (k p) -> (o k) p", p=P)),
            (vector_rows[36:40, :], out_norm_attn.rearrange("o (k p) -> (o k) p", p=P)),
            (vector_rows[40:41, 0:HD], q_norm),
            (vector_rows[40:41, HD:P], q_norm),
            (vector_rows[41:42, 0:HD], k_norm),
            (vector_rows[41:42, HD:P], k_norm),
        ]
        late = [
            (b_out_row[:], b_out[0].partition_broadcast(P)),
            (norm_ffn_row[:], norm_ffn[0].partition_broadcast(P)),
            (b_router_row[:], b_router[0].partition_broadcast(P)),
            (w_router_sb[:], w_router[0].rearrange("(k p) e -> p k e", p=P)),
        ]
        all_early, all_late = 16 * len(early), 16 * len(late)

        def wait(eng, e, t):
            eng.wait_ge(e.sem, e.of(t))

        @block.sync
        def _(sp):
            w_rows = w_in[0].rearrange("(k p) n -> p k n", p=P)
            sp.dma_start(x_in[:], x_rows[0:P, :]).then_inc(x_loaded.sem, 16)
            for dst, src in early:
                sp.dma_start(dst, src).then_inc(early_loaded, 16)
            for i in range(2):
                part = slice(i * KD // 2, (i + 1) * KD // 2)
                sp.dma_start(w_in_sb[:, part, QKV0:IN_W], w_rows[:, part, QKV0:IN_W]).then_inc(qkv_w_loaded[i], 16)
            sp.dma_start(b_qkv_row[:], b_in[0, QKV0:IN_W].partition_broadcast(P)).then_inc(qkv_b_loaded, 16)
            sp.wait_ge(rel_made, 1)
            sp.dma_start(rel_rows, rel_row).then_inc(rel_stored, 16)

            def load_conv_w(c):
                for j in range(3):
                    first = j * CW + c * P
                    sp.dma_start(w_in_sb[:, :, first:first + P], w_rows[:, :, first:first + P]).then_inc(conv_w_loaded[c], 16)

            load_conv_w(0)
            sp.wait_ge(rel_stored, 16)
            slanted = bass.AP(tensor=rel_rows.tensor, offset=0, ap=[[1, P], [REL_W, NH], [1, 2 * P]])
            sp.dma_start(probs[:], slanted).then_inc(bias_loaded, 16)
            for c in range(1, CC):
                load_conv_w(c)
            for dst, src in late:
                sp.dma_start(dst, src).then_inc(late_loaded, 16)
            sp.dma_start(w_out_sb[:], w_out[0].rearrange("(k p) n -> p k n", p=P)).then_inc(out_w_loaded, 16)

            def load_block(n, rows):
                wait(sp, x_normed, n)
                sp.dma_start(x_in[:], rows).then_inc(x_loaded.sem, 16)

            def load_residual(t):
                wait(sp, x1_ready, t - 1)
                sp.dma_start(x_res[:], x_rows[bass.ds(t * P, P), :]).then_inc(res_loaded.sem, 16)

            with sp.Fori(0, NB - 1) as t:
                load_block(t, x_rows[bass.ds((t + 1) * P, P), :])
                load_residual(t)
            load_residual(NB - 1)

        @block.gpsimd
        def _(pool):
            for e in credited:
                pool.sem_inc(e.sem, e.unit * e.credit)
            nc.gpsimd.memset(minus_half[:], -0.5).then_inc(cleared, 1)
            nc.gpsimd.memset(before[:, 0, :], 0.0).then_inc(cleared, 1)
            nc.gpsimd.memset(v_keys[:], 0.0).then_inc(cleared, 1)
            nc.gpsimd.memset(kT[:], 0.0).then_inc(cleared, 1)
            nc.gpsimd.memset(conv_x[:], 0.0).then_inc(cleared, 1)
            nc.gpsimd.memset(bias_all[:, :, 0:P], MASKED).then_inc(cleared, 1)
            pool.wait_ge(cleared, 6)

            def rsqrt(mean, t, src, dst, done):
                wait(pool, mean, t)
                nc.gpsimd.tensor_tensor(dst, src, minus_half[:, 0:src.shape[1]], ALU.pow).then_inc(done.sem, 1)

            rsqrt(x_mean, 0, ms_x, rstd_x, x_rstd)
            rsqrt(qk_mean, 0, ms_qk, rstd_qk, qk_rstd)
            pool.wait_ge(early_loaded, all_early)
            pool.wait_ge(bias_flipped, 2)
            def add_taps_pool(t, c):
                wait(pool, gated[c], t)
                for j in range(3):
                    last = nc.gpsimd.tensor_tensor(conv_t[:, j, :], conv_x[:, c, j:j + P],
                                                   conv_w_col[:, j, c:c + 1].broadcast_to([P, P]), ALU.mult)
                    pstep.did(last)
                pool.wait_ge(pstep.sem, pstep.value(t))
                pstep.did(nc.gpsimd.tensor_tensor(conv_t[:, 1, :], conv_t[:, 2, :], conv_t[:, 1, :], ALU.add))
                pool.wait_ge(pstep.sem, pstep.value(t))
                nc.gpsimd.tensor_tensor(conv_t[:, 2, :], conv_t[:, 1, :], conv_t[:, 0, :], ALU.add).then_inc(tapped[c].sem, 1)

            def one_block(t, more):
                pstep.n = 0
                add_taps_pool(t, 2)
                assert pstep.n == 4
                wait(pool, biased[1], t)
                nc.gpsimd.tensor_tensor(bias_all[:, :, 0:P], bias_prev[:],
                                        cst[:, C_ONES:C_ONES + P].unsqueeze(1).broadcast_to([P, NH, P]),
                                        ALU.mult).then_inc(bias_switched.sem, 1)
                add_taps_pool(t, 3)
                for i in range(CC):
                    wait(pool, conv_out[i], t)
                wait(pool, conv_mixed, t - 1)
                nc.gpsimd.tensor_tensor(conv_s[:], conv_y[:], conv_g_col.unsqueeze(2).broadcast_to([P, CC, P]),
                                        ALU.mult).then_inc(conv_scaled.sem, 1)
                if more:
                    rsqrt(x_mean, t + 1, ms_x, rstd_x, x_rstd)
                pool.wait_ge(late_loaded, all_late)
                wait(pool, res_loaded, t)
                nc.gpsimd.tensor_tensor(x_res[:], x_res[:], b_out_row[:], ALU.add).then_inc(res_biased.sem, 1)
                rsqrt(ca_mean, t, ms_ca, rstd_ca, ca_rstd)
                rsqrt(f_mean, t, ms_f, rstd_f, f_rstd)
                if more:
                    rsqrt(qk_mean, t + 1, ms_qk, rstd_qk, qk_rstd)

            with pool.Fori(0, NB - 1) as t:
                one_block(t, True)
            one_block(NB - 1, False)

        @block.scalar
        def _(act):
            def prepare(n):
                wait(act, x_loaded, n)
                nc.scalar.activation(junk[:], x_in[:], ACT.Square, accum_out=ss_x).then_inc(x_squared.sem, 1)
                wait(act, x_rstd, n)
                nc.scalar.activation(xn[:], x_in[:], ACT.Copy, scale=rstd_x).then_inc(x_normed.sem, 1)

            def square_qk(n):
                wait(act, qk_ready, n)
                nc.scalar.activation(qk_sq[:], qk[:], ACT.Square).then_inc(qk_squared.sem, 1)

            def add_u_bias(t, c):
                wait(act, conv_done[c], t)
                if c < 2:
                    wait(act, conv_out[c + 2], t - 1)
                else:
                    wait(act, conv_out[c - 2], t)
                nc.scalar.activation(conv_u[:, c % 2, :], ps_c[:, c % 2, 2 * P:3 * P], ACT.Identity,
                                     bias=b_in_col[:, 2 * CC + c:2 * CC + c + 1]).then_inc(u_ready[c].sem, 1)

            prepare(0)
            act.wait_ge(vectors_ready, 1)
            nc.scalar.activation(q_scale_col[:], q_norm_col, ACT.Copy, scale=HD ** -0.5).then_inc(scale_made, 1)
            square_qk(0)
            act.wait_ge(scale_made, 1)
            act.wait_ge(cleared, 6)
            def one_block(t, more):
                add_u_bias(t, 0)
                add_u_bias(t, 1)
                wait(act, qk_turned, t)
                nc.scalar.copy(kT[:, :, 0, :], kT[:, :, 1, :]).then_inc(k_shifted.sem, 1)
                wait(act, k_shifted, t)
                nc.scalar.activation(kT[:, :, 1, :], ps_s[:, 512:512 + 2 * P].rearrange("p (v k) -> p v k", v=2),
                                     ACT.Copy, scale=k_norm_col)
                nc.scalar.activation(qT[:].rearrange("p h q -> p (h q)"), ps_s[:, 0:512],
                                     ACT.Copy, scale=q_scale_col[:]).then_inc(qT_ready.sem, 1)
                add_u_bias(t, 2)
                for s in range(NH):
                    if s % HALF == 0:
                        wait(act, neg_ready[s // HALF], t)
                    nc.scalar.activation(probs[:, s, :], probs[:, s, :], ACT.Exp, bias=neg_top[:, s:s + 1],
                                         accum_out=row_sum[:, s:s + 1]).then_inc(exped[s].sem, 1)
                add_u_bias(t, 3)
                nc.scalar.activation(sink_exp, sink_gap, ACT.Exp).then_inc(sink_exped.sem, 1)
                wait(act, conv_out[3], t)
                nc.scalar.activation(conv_sq[:], conv_y[:], ACT.Square).then_inc(conv_squared.sem, 1)
                if more:
                    prepare(t + 1)
                wait(act, attn_ready, t)
                nc.scalar.activation(junk[:, 0:AW], attn[:], ACT.Square, accum_out=ss_ca[:, 1:2]).then_inc(attn_squared.sem, 1)
                wait(act, x1_ready, t)
                nc.scalar.activation(junk[:], x1[:], ACT.Square, accum_out=ss_f).then_inc(x1_squared.sem, 1)
                act.dma_start(out_rows[bass.ds(t * P, P), :], x1[:]).then_inc(stored.sem, 16)
                wait(act, h2_ready, t)
                act.dma_start(h2_rows[bass.ds(t * P, P), :], h2[:]).then_inc(stored.sem, 16)
                for i in range(2):
                    wait(act, h2_turned[i], t)
                    nc.scalar.copy(h2T[:, 4 * i:4 * i + 4, :], ps_s[:, 512 * i:512 * i + 512].rearrange(
                        "p (k q) -> p k q", k=4)).then_inc(h2T_ready[i].sem, 1)
                if more:
                    square_qk(t + 1)
                wait(act, best_ready, t)
                nc.scalar.activation(exp4, best[:, 0:TOP_K], ACT.Exp, bias=neg_best,
                                     accum_out=sum4).then_inc(best_exped.sem, 1)

            with act.Fori(0, NB - 1) as t:
                one_block(t, True)
            one_block(NB - 1, False)
            wait(act, stored, NB - 1)

        @block.vector
        def _(dve):
            def mean(ss, ms, width):
                return nc.vector.tensor_scalar(ms, ss, 1.0 / width, EPS, ALU.mult, ALU.add)

            def x_to_mean(n):
                wait(dve, x_squared, n)
                mean(ss_x, ms_x, D).then_inc(x_mean.sem, 1)

            def read_hT(n, i):
                wait(dve, x_turned[i], n)
                nc.vector.tensor_tensor(hT[:, 4 * i:4 * i + 4, :],
                                        ps_c[:, i, :].rearrange("p (k q) -> p k q", k=4),
                                        norm_mix_col[:, 4 * i:4 * i + 4].unsqueeze(2).broadcast_to([P, 4, P]),
                                        ALU.mult).then_inc(hT_ready[i].sem, 1)

            def read_qkv(n):
                wait(dve, qkv_done, n)
                dve.wait_ge(qkv_b_loaded, 16)
                nc.vector.tensor_tensor(qk[:, 0:AW], ps_q[:], b_qkv_row[:, 0:AW], ALU.add)
                nc.vector.tensor_tensor(qk[:, AW:AW + KVW], ps_kv[:, 0:KVW], b_qkv_row[:, AW:AW + KVW],
                                        ALU.add).then_inc(qk_ready.sem, 1)
                nc.vector.tensor_copy(v_keys[:, 0, :], v_keys[:, 1, :]).then_inc(v_shifted.sem, 1)
                wait(dve, v_shifted, n)
                nc.vector.tensor_tensor(v_keys[:, 1, :], ps_kv[:, KVW:2 * KVW], b_qkv_row[:, AW + KVW:],
                                        ALU.add).then_inc(v_ready.sem, 1)

            def norm_qk(n):
                wait(dve, qk_squared, n)
                nc.vector.tensor_reduce(ss_qk, qk_sq[:].rearrange("p (h d) -> p h d", d=HD), AX_X,
                                        ALU.add).then_inc(qk_summed.sem, 1)
                wait(dve, qk_summed, n)
                mean(ss_qk, ms_qk, HD).then_inc(qk_mean.sem, 1)
                wait(dve, qk_rstd, n)
                nc.vector.tensor_tensor(qn[:].rearrange("p (h d) -> p h d", d=HD),
                                        qk[:, 0:AW].rearrange("p (h d) -> p h d", d=HD),
                                        rstd_qk[:, 0:NH].unsqueeze(2).broadcast_to([P, NH, HD]), ALU.mult)
                for j in range(2):
                    last = nc.vector.tensor_tensor(kn[:, :, j, :],
                                                   qk[:, AW:].rearrange("p (h d) -> p h d", d=HD),
                                                   rstd_qk[:, NH:].unsqueeze(2).broadcast_to([P, NKV, HD]), ALU.mult)
                last.then_inc(qk_normed.sem, 1)

            def gate_input(t, c):
                wait(dve, conv_done[c], t)
                wait(dve, u_ready[c], t)
                nc.vector.scalar_tensor_tensor(out=conv_x[:, c, 2:], in0=ps_c[:, c % 2, P:2 * P],
                                               scalar=b_in_col[:, CC + c:CC + c + 1], in1=conv_u[:, c % 2, :],
                                               op0=ALU.add, op1=ALU.mult).then_inc(gated[c].sem, 1)

            def add_taps(t, c):
                wait(dve, gated[c], t)
                then_wait(t, nc.vector.tensor_scalar(conv_t[:, 0, :], conv_x[:, c, 2:], conv_w_col[:, 2, c:c + 1],
                                                     None, ALU.mult))
                then_wait(t, nc.vector.scalar_tensor_tensor(
                    out=conv_t[:, 1, :], in0=conv_x[:, c, 1:P + 1], scalar=conv_w_col[:, 1, c:c + 1],
                    in1=conv_t[:, 0, :], op0=ALU.mult, op1=ALU.add))
                nc.vector.scalar_tensor_tensor(
                    out=conv_t[:, 2, :], in0=conv_x[:, c, 0:P], scalar=conv_w_col[:, 0, c:c + 1],
                    in1=conv_t[:, 1, :], op0=ALU.mult, op1=ALU.add).then_inc(tapped[c].sem, 1)

            def gate_output(t, c):
                wait(dve, tapped[c], t)
                nc.vector.scalar_tensor_tensor(out=conv_y[:, c, :], in0=ps_c[:, c % 2, 0:P], scalar=b_in_col[:, c:c + 1],
                                               in1=conv_t[:, 2, :], op0=ALU.add, op1=ALU.mult).then_inc(conv_out[c].sem, 1)

            def then_wait(t, ins):
                vstep.did(ins)
                dve.wait_ge(vstep.sem, vstep.value(t))

            def add_bias(t, i):
                part = slice(i * HALF, (i + 1) * HALF)
                nc.vector.tensor_tensor(probs[:, part, :], ps_heads[:, part, :], bias_all[:, part, :],
                                        ALU.add).then_inc(biased[i].sem, 1)

            def find_top(t, i):
                part = slice(i * HALF, (i + 1) * HALF)
                then_wait(t, nc.vector.tensor_tensor(top[:, part], denom[:, part], sink_slots[:, part], ALU.max))
                nc.vector.tensor_tensor(sink_gap[:, part], sink_slots[:, part], top[:, part], ALU.subtract)
                nc.vector.tensor_scalar(neg_top[:, part], top[:, part], -1.0, None,
                                        ALU.mult).then_inc(neg_ready[i].sem, 1)

            dve.wait_ge(cleared, 6)
            x_to_mean(0)
            dve.wait_ge(early_loaded, all_early)
            nc.vector.tensor_copy(sink_slots[:].rearrange("p (g b a) -> p g b a", g=2, b=2),
                                  sink_row[:].rearrange("p (g a b) -> p g b a", g=2, b=2)).then_inc(slots_made, 1)
            nc.vector.tensor_copy(rel_bias_slots[:].rearrange("p (g b a) -> p g b a", g=2, b=2),
                                  rel_bias_sb[:].rearrange("p (g a b) -> p g b a", g=2, b=2)).then_inc(slots_made, 1)
            dve.wait_ge(rel_summed, 1)
            nc.vector.tensor_tensor(rel_row, ps_s[0:NH, 0:REL_W], rel_const[0:NH, REL_W:2 * REL_W],
                                    ALU.add).then_inc(rel_made, 1)
            dve.wait_ge(vectors_turned, 1)
            nc.vector.tensor_copy(vectors[:], ps_s[:, 512:554]).then_inc(vectors_ready, 1)
            dve.wait_ge(vectors_ready, 1)
            dve.wait_ge(slots_made, 2)
            read_hT(0, 0)
            read_hT(0, 1)
            read_qkv(0)
            norm_qk(0)
            dve.wait_ge(bias_turned, 1)
            nc.vector.tensor_copy(bias_prev[:], ps_heads[:, :, 0:P]).then_inc(bias_flipped, 1)
            nc.vector.tensor_copy(bias_all[:, :, P:2 * P], ps_heads[:, :, P:2 * P]).then_inc(bias_flipped, 1)
            dve.wait_ge(bias_flipped, 2)
            def one_block(t, more):
                vstep.n = 0
                then_wait(t, nc.vector.tensor_copy(conv_x[:, :, 0:2], conv_x[:, :, P:P + 2]))
                for c in range(2):
                    gate_input(t, c)
                    add_taps(t, c)
                    gate_output(t, c)
                gate_input(t, 2)
                wait(dve, scored[0], t)
                wait(dve, bias_switched, t - 1)
                wait(dve, av_done[NH - 1], t - 1)
                add_bias(t, 0)
                wait(dve, biased[0], t)
                then_wait(t, nc.vector.tensor_reduce(denom[:, 0:HALF], probs[:, 0:HALF, :], AX_X, ALU.max))
                wait(dve, scored[1], t)
                add_bias(t, 1)
                find_top(t, 0)
                wait(dve, biased[1], t)
                then_wait(t, nc.vector.tensor_reduce(denom[:, HALF:NH], probs[:, HALF:NH, :], AX_X, ALU.max))
                find_top(t, 1)
                gate_output(t, 2)
                for s in range(NH):
                    wait(dve, p_turned[s], t)
                    if s >= 2:
                        wait(dve, av_done[s - 2], t)
                    nc.vector.tensor_copy(pT[:, s % 2, :], (ps_q, ps_kv)[s % 2][:, 0:2 * P]).then_inc(pT_ready[s].sem, 1)
                    if s == 2:
                        gate_input(t, 3)
                    elif s == 6:
                        gate_output(t, 3)
                wait(dve, sink_exped, t)
                then_wait(t, nc.vector.tensor_tensor(denom, row_sum, sink_exp, ALU.add))
                then_wait(t, nc.vector.reciprocal(rdenom.rearrange("p (g a b) -> p g b a", g=2, b=2),
                                                   denom.rearrange("p (g b a) -> p g b a", g=2, b=2)))
                if more:
                    x_to_mean(t + 1)
                wait(dve, av_done[NH - 1], t)
                nc.vector.tensor_tensor(attn[:].rearrange("p (h d) -> p h d", d=HD),
                                        ps_c[:, 0, :].rearrange("p (h d) -> p h d", d=HD),
                                        rdenom.unsqueeze(2).broadcast_to([P, NH, HD]), ALU.mult).then_inc(attn_ready.sem, 1)
                wait(dve, conv_summed, t)
                nc.vector.tensor_reduce(ss_ca[:, 0:1], ps_kv[:, 2 * P:2 * P + CC], AX_X, ALU.add).then_inc(vstep.sem, 1)
                vstep.n += 1
                wait(dve, attn_turned, t)
                nc.vector.tensor_tensor(attnT[:], ps_c[:, 1, :].rearrange("p (c q) -> p c q", c=CC),
                                        attn_g_col.unsqueeze(2).broadcast_to([P, CC, P]),
                                        ALU.mult).then_inc(attnT_ready.sem, 1)
                dve.wait_ge(vstep.sem, vstep.value(t))
                wait(dve, attn_squared, t)
                mean(ss_ca, ms_ca, CW).then_inc(ca_mean.sem, 1)
                if more:
                    read_hT(t + 1, 0)
                wait(dve, conv_mixed, t)
                wait(dve, ca_rstd, t)
                wait(dve, res_biased, t)
                wait(dve, stored, t - 1)
                dve.wait_ge(late_loaded, all_late)
                then_wait(t, nc.vector.scalar_tensor_tensor(out=x1[:], in0=ps_s[:, 0:D], scalar=rstd_ca[:, 0:1],
                                                            in1=x_res[:], op0=ALU.mult, op1=ALU.add))
                wait(dve, attn_mixed, t)
                nc.vector.scalar_tensor_tensor(out=x1[:], in0=ps_s[:, D:2 * D], scalar=rstd_ca[:, 1:2],
                                               in1=x1[:], op0=ALU.mult, op1=ALU.add).then_inc(x1_ready.sem, 1)
                if more:
                    read_hT(t + 1, 1)
                wait(dve, x1_squared, t)
                mean(ss_f, ms_f, D).then_inc(f_mean.sem, 1)
                wait(dve, f_rstd, t)
                nc.vector.scalar_tensor_tensor(out=h2[:], in0=x1[:], scalar=rstd_f, in1=norm_ffn_row[:],
                                               op0=ALU.mult, op1=ALU.mult).then_inc(h2_ready.sem, 1)
                if more:
                    read_qkv(t + 1)
                    norm_qk(t + 1)
                wait(dve, routed, t)
                nc.vector.tensor_tensor(route_sc[:], ps_route, b_router_row[:], ALU.add).then_inc(logits_read.sem, 1)
                wait(dve, logits_read, t)
                nc.vector.tensor_copy(best_f[:, 0:1], route_sc[:, 0:1])
                then_wait(t, nc.vector.max(best, route_sc[:]))
                nc.vector.tensor_scalar(neg_best, best[:, 0:1], -1.0, None, ALU.mult).then_inc(best_ready.sem, 1)
                then_wait(t, nc.vector.max_index(best_i[:], best, route_sc[:]))
                then_wait(t, nc.vector.tensor_copy(best_f, best_i[:]))
                then_wait(t, nc.vector.tensor_tensor(
                    hot[:], cst[:, C_E:C_E + NE].unsqueeze(1).broadcast_to([P, TOP_K, NE]),
                    best_f[:, 0:TOP_K].unsqueeze(2).broadcast_to([P, TOP_K, NE]), ALU.is_equal))
                then_wait(t, nc.vector.tensor_reduce(picked[:, bass.ds(t, 1), :].rearrange("p o e -> p (o e)"),
                                                     hot[:].rearrange("p k e -> p e k"), AX_X, ALU.add))
                nc.vector.tensor_tensor(before[:, bass.ds(t + 1, 1), :].rearrange("p o e -> p (o e)"),
                                        before[:, bass.ds(t, 1), :].rearrange("p o e -> p (o e)"),
                                        picked[:, bass.ds(t, 1), :].rearrange("p o e -> p (o e)"), ALU.add)
                wait(dve, best_exped, t)
                then_wait(t, nc.vector.reciprocal(rsum4, sum4))
                then_wait(t, nc.vector.tensor_scalar(gate4, exp4, rsum4, None, ALU.mult))
                then_wait(t, nc.vector.tensor_tensor(hot_g[:], hot[:], gate4.unsqueeze(2).broadcast_to([P, TOP_K, NE]),
                                                     ALU.mult))
                nc.vector.tensor_reduce(gates[:, bass.ds(t, 1), :].rearrange("p o e -> p (o e)"),
                                        hot_g[:].rearrange("p k e -> p e k"), AX_X, ALU.add)
                assert vstep.n == vstep.per, vstep.n

            with dve.Fori(0, NB - 1) as t:
                one_block(t, True)
            one_block(NB - 1, False)

        @block.tensor
        def _(pe):
            def turn_x(n, i):
                for k in range(4 * i, 4 * i + 4):
                    last = pe.transpose(ps_c[:, i, (k % 4) * P:(k % 4 + 1) * P], xn[:, k * P:(k + 1) * P], ident)
                last.then_inc(x_turned[i].sem, 1)

            def project_q(n):
                for k in range(KD):
                    if k % 4 == 0:
                        pe.wait_ge(qkv_w_loaded[k // 4], 16)
                        wait(pe, hT_ready[k // 4], n)
                    pe.matmul(ps_q[:], hT[:, k, :], w_in_sb[:, k, QKV0:QKV0 + AW], start=(k == 0), stop=(k == KD - 1))

            def project_kv(n):
                for k in range(KD):
                    last = pe.matmul(ps_kv[:, 0:2 * KVW], hT[:, k, :], w_in_sb[:, k, QKV0 + AW:IN_W],
                                     start=(k == 0), stop=(k == KD - 1))
                last.then_inc(qkv_done.sem, 1)

            def project_conv(t, c, parts=range(3)):
                pe.wait_ge(conv_w_loaded[c], 48)
                for j in parts:
                    for k in range(KD):
                        first = j * CW + c * P
                        last = pe.matmul(ps_c[:, c % 2, j * P:(j + 1) * P], w_in_sb[:, k, first:first + P],
                                         hT[:, k, :], start=(k == 0), stop=(k == KD - 1))
                if parts[-1] == 2:
                    last.then_inc(conv_done[c].sem, 1)

            def turn_p(t, s):
                wait(pe, exped[s], t)
                if s >= 2:
                    wait(pe, pT_ready[s - 2], t)
                for j in range(2):
                    last = pe.transpose((ps_q, ps_kv)[s % 2][:, j * P:(j + 1) * P], probs[:, s, j * P:(j + 1) * P], ident)
                last.then_inc(p_turned[s].sem, 1)

            def attend(t, s):
                h = head_of(s)
                kv = h // (NH // NKV)
                wait(pe, pT_ready[s], t)
                for j in range(2):
                    last = pe.matmul(ps_c[:, 0, h * HD:(h + 1) * HD], pT[:, s % 2, j * P:(j + 1) * P],
                                     v_keys[:, j, kv * HD:(kv + 1) * HD], start=(j == 0), stop=(j == 1))
                last.then_inc(av_done[s].sem, 1)

            pe.wait_ge(early_loaded, all_early)
            pe.wait_ge(slots_made, 2)
            pe.matmul(ps_s[0:NH, 0:REL_W], rel_bias_slots[:], rel_const[0:NBUCKET, 0:REL_W],
                      start=True, stop=True).then_inc(rel_summed, 1)
            pe.transpose(ps_s[:, 512:554], vector_rows, ident[0:42, 0:42]).then_inc(vectors_turned, 1)
            wait(pe, x_normed, 0)
            turn_x(0, 0)
            turn_x(0, 1)
            project_q(0)
            project_kv(0)
            pe.wait_ge(bias_loaded, 16)
            pe.wait_ge(vectors_ready, 1)
            for i in range(4):
                last = pe.matmul(ps_s[:, i * 512:(i + 1) * 512], rel_const[:, 2 * REL_W:], probs[:, 2 * i:2 * i + 2, :].rearrange(
                    "p h k -> p (h k)"), start=True, stop=True)
            last.then_inc(bias_turned, 1)
            def one_block(t, more):
                project_conv(t, 0)
                project_conv(t, 1)
                wait(pe, qk_normed, t)
                pe.wait_ge(bias_flipped, 2)
                for i in range(NH // 2):
                    pe.transpose(ps_s[:, i * P:(i + 1) * P], qn[:, i * P:(i + 1) * P], ident)
                for i in range(NKV):
                    last = pe.transpose(ps_s[:, 512 + i * P:512 + (i + 1) * P],
                                        kn[:, i, :, :].rearrange("p j d -> p (j d)"), ident)
                last.then_inc(qk_turned.sem, 1)
                wait(pe, conv_out[0], t)
                project_conv(t, 2)
                wait(pe, qT_ready, t)
                wait(pe, logits_read, t - 1)
                for s in (0, 2, 1, 3, 4, 6, 5, 7):
                    h = head_of(s)
                    a = HD * (h % 2)
                    last = pe.matmul(ps_heads[:, s, :], qT[a:a + HD, h // 2, :],
                                     kT[a:a + HD, h // (NH // NKV), :, :].rearrange("p j k -> p (j k)"),
                                     start=True, stop=True)
                    if s % HALF == HALF - 1:
                        last.then_inc(scored[s // HALF].sem, 1)
                wait(pe, conv_out[1], t)
                project_conv(t, 3, (0, 1))
                turn_p(t, 0)
                project_conv(t, 3, (2,))
                for s in range(NH):
                    if s + 1 < NH:
                        turn_p(t, s + 1)
                    if s == 0:
                        wait(pe, conv_out[2], t)
                        wait(pe, v_ready, t)
                    attend(t, s)
                wait(pe, conv_squared, t)
                for c in range(CC):
                    last = pe.matmul(ps_kv[:, 2 * P + c:2 * P + c + 1], conv_sq[:, c, :], cst[:, C_ONES:C_ONES + 1],
                                     start=True, stop=True)
                last.then_inc(conv_summed.sem, 1)
                wait(pe, conv_scaled, t)
                wait(pe, biased[1], t)
                pe.wait_ge(out_w_loaded, 16)
                for n in range(2):
                    for k in range(CC):
                        last = pe.matmul(ps_s[:, n * 512:(n + 1) * 512], conv_s[:, k, :],
                                         w_out_sb[:, k, n * 512:(n + 1) * 512], start=(k == 0), stop=(k == CC - 1))
                    if n == 0:
                        wait(pe, attn_ready, t)
                        wait(pe, conv_out[3], t)
                        for c in range(CC):
                            turned = pe.transpose(ps_c[:, 1, c * P:(c + 1) * P], attn[:, c * P:(c + 1) * P], ident)
                        turned.then_inc(attn_turned.sem, 1)
                last.then_inc(conv_mixed.sem, 1)
                if more:
                    wait(pe, x_normed, t + 1)
                    turn_x(t + 1, 0)
                wait(pe, attnT_ready, t)
                for n in range(2):
                    for k in range(CC):
                        last = pe.matmul(ps_s[:, D + n * 512:D + (n + 1) * 512], attnT[:, k, :],
                                         w_out_sb[:, CC + k, n * 512:(n + 1) * 512], start=(k == 0), stop=(k == CC - 1))
                last.then_inc(attn_mixed.sem, 1)
                if more:
                    turn_x(t + 1, 1)
                    project_q(t + 1)
                wait(pe, h2_ready, t)
                for i in range(2):
                    for k in range(4 * i, 4 * i + 4):
                        last = pe.transpose(ps_s[:, k * P:(k + 1) * P], h2[:, k * P:(k + 1) * P], ident)
                    last.then_inc(h2_turned[i].sem, 1)
                if more:
                    project_kv(t + 1)
                pe.wait_ge(late_loaded, all_late)
                for k in range(KD):
                    if k % 4 == 0:
                        wait(pe, h2T_ready[k // 4], t)
                    last = pe.matmul(ps_route, h2T[:, k, :], w_router_sb[:, k, :], start=(k == 0), stop=(k == KD - 1))
                last.then_inc(routed.sem, 1)

            with pe.Fori(0, NB - 1) as t:
                one_block(t, True)
            one_block(NB - 1, False)


def experts(nc, h2_rows, out_rows, w1, b1, w2, b2, cst, picked, gates, before):
    ident = cst[:, C_ID:C_ID + P]
    ones = cst[:, C_ONES:C_ONES + P]
    last_size = len(SIZES) - 1
    second_rows = ((SIZES.index(144), 16), (SIZES.index(192), 64), (last_size, P))
    with ExitStack() as ctx:
        def sb(name, shape, dt=F32):
            return ctx.enter_context(nc.sbuf_tensor(name, shape, dt))

        def ps(name, shape):
            return ctx.enter_context(nc.psum_tensor(name, shape, F32))

        def sem(name):
            return ctx.enter_context(nc.semaphore(name))

        credited = []

        def event(name, unit=1, credit=0):
            e = Event(sem(name), unit, credit)
            if credit:
                credited.append(e)
            return e

        def wait(eng, e, t):
            eng.wait_ge(e.sem, e.of(t))

        w_slot = sb("w_slot", [P, LOADS, KD, 2 * PW])
        b1T = sb("b1T", [P, 2 * P1, NE])
        b2T = sb("b2T", [P, KD, NE])
        b1_cur = sb("b1_cur", [P, 2 * P1])
        b2_cur = sb("b2_cur", [P, KD])
        place = sb("place", [P, NB, NE])
        gate_parts = sb("gate_parts", [P, NB, 3, NE], BF16)
        base_row = sb("base_row", [P, P])
        job_row = sb("job_row", [1, 2 * P], I32)
        jobs = sb("jobs", [1, 2], I32)
        iota_b = sb("iota_b", [P, CAP], BF16)
        place_cur = sb("place_cur", [P, NB])
        token = sb("token", [P, NB])
        match = sb("match", [P, NB, CAP], BF16)
        entry = sb("entry", [P, NB, 5], BF16)
        list_sb = sb("list_sb", [P, 2, 5])
        gate_next = sb("gate_next", [P, 2])
        idx_next = sb("idx_next", [P, 2], I32)
        gate_cur = sb("gate_cur", [P, 2])
        idx_cur = sb("idx_cur", [P, 2], I32)
        x_got = sb("x_got", [P, 2, D])
        xT = sb("xT", [P, KD, CAP])
        glu = sb("glu", [P, 3, CAP])
        lin = sb("lin", [P, 3, CAP])
        sig = sb("sig", [P, 3, CAP])
        act_T = sb("act_T", [P, P1, CAP])
        yT = sb("yT", [P, KD, CAP])
        b2_rows = yT[:].rearrange("p m n -> p (m n)")[:, 0:D]
        y_rows = sb("y_rows", [P, 2, D])
        carrier = sb("carrier", [P, 3])
        counts = sb("counts", [P, NE])
        rank = sb("rank", [P, NB, NE])
        other = sb("other", [P, NB, NE])
        n_jobs = sb("n_jobs", [P, NE])
        over = sb("over", [P, 2, NE])
        last_job = sb("last_job", [P, NE])
        ended = sb("ended", [P, NE])
        pick_e = sb("pick_e", [P, 2, NE])
        limits = sb("limits", [P, 2, last_size])
        fields = sb("fields", [P, 3])
        narrow = sb("narrow", [P, 8])

        ps_unit = [ps(f"ps_unit{i}", [P, 2, CAP]) for i in range(3)]
        ps_list = ps("ps_list", [P, 512])
        ps_x = [ps(f"ps_x{i}", [P, 2, CAP]) for i in range(2)]
        ps_y = [ps(f"ps_y{i}", [P, 2, 2, P]) for i in range(2)]

        biases_turned = sem("biases_turned")
        biases_read = sem("biases_read")
        carrier_cleared = sem("carrier_cleared")
        buffers = sem("expert_buffers_cleared")
        counters_copied = sem("counters_copied")
        ranked = sem("ranked")
        fields_ready = sem("fields_ready")
        fields_spread = sem("fields_spread")
        table_ready = sem("table_ready")
        rstep = Steps(sem("routing_step"), 0)
        units_cleared = sem("units_cleared")
        place_taken = event("place_taken")
        entry_ready = event("entry_ready")
        matched = event("matched")
        gate_summed = event("gate_summed")
        listed = event("listed")
        list_read = event("list_read")
        idx_ready = event("idx_ready")
        gathered_a = event("gathered_a", 16)
        gathered_b = event("gathered_b", 16)
        x_turned = [event(f"x_rows_turned{i}") for i in range(4)]
        xT_ready = [event(f"xT_ready{i}") for i in range(4)]
        w_loaded = [event(f"w_loaded{i}", 16) for i in range(LOADS)]
        unit_done = [event(f"unit_done{p}", 1, 1) for p in range(PIECES)]
        unit_read = [event(f"unit_read{p}", 1, 1) for p in range(PIECES)]
        b1_ready = event("b1_ready")
        cur_ready = event("cur_ready")
        b2_ready = event("b2_ready")
        glu_ready = [event(f"glu_ready{p}") for p in range(P1)]
        sig_ready = [event(f"sig_ready{p}") for p in range(P1)]
        scaled = [event(f"scaled{p}") for p in range(P1)]
        act_ready = [event(f"act_ready{p}") for p in range(P1)]
        y_turned = [event(f"y_turned{i}") for i in range(4)]
        y_read = [event(f"y_read{i}", 1, 1) for i in range(4)]
        pool_moved = Event(sem("pool_moved"), 32, 1)
        carried = [event(f"carried{i}", 1, 1) for i in range(2)]

        block = ctx.enter_context(nc.Block())

        def job_loop(eng):
            eng.wait_ge(table_ready, 3)
            n = eng.value_load(jobs[0:1, 0:1], min_val=1, max_val=NE + S * TOP_K // CAP)
            return eng.Fori(0, n)

        def expert_of(eng, q):
            return eng.value_load(job_row[0:1, bass.ds(q, 1)], min_val=0, max_val=NE - 1)

        def size_at(q):
            return job_row[0:1, bass.ds(q + P, 1)]

        def size_of(eng, q):
            return eng.value_load(size_at(q), min_val=0, max_val=last_size)


        @block.sync
        def _(sp):
            def load_pieces(i, e):
                w, first = (w1, 2 * i * PW) if 2 * i < P1 else (w2, (2 * i - P1) * PW)
                src = w[0, e, :, first:first + 2 * PW].rearrange("o (k p) f -> p (o k) f", p=P)
                sp.dma_start(w_slot[:, i, :, :], src).then_inc(w_loaded[i].sem, 16)

            sp.wait_ge(pool_moved.sem, 32)
            for i in range(EARLY_LOADS):
                load_pieces(i, slice(0, 1))
            wait(sp, gathered_b, 0)
            for i in range(EARLY_LOADS, LOADS):
                load_pieces(i, slice(0, 1))
            sp.wait_ge(table_ready, 3)
            n = sp.value_load(jobs[0:1, 0:1], min_val=1, max_val=NE + S * TOP_K // CAP)
            with sp.Fori(1, n) as q:
                e = expert_of(sp, q)
                for i in range(LOADS):
                    wait(sp, unit_done[2 * i + 1], q - 1)
                    load_pieces(i, bass.ds(e, 1))

        @block.gpsimd
        def _(pool):
            pool.dma_start(y_rows[0:NE, :, :].rearrange("e h f -> e (h f)"), b1[0]).then_inc(pool_moved.sem, 16)
            pool.dma_start(b2_rows[0:NE, :], b2[0]).then_inc(pool_moved.sem, 16)
            for e in credited:
                pool.sem_inc(e.sem, e.unit * e.credit)
            nc.gpsimd.memset(carrier[:], 0.0).then_inc(carrier_cleared, 1)
            nc.gpsimd.memset(x_got[:], 0.0).then_inc(buffers, 1)
            pool.wait_ge(carrier_cleared, 1)

            def second_block(size, move):
                (small, a), (middle, b), (_, c) = second_rows
                with pool.If(size > small):
                    with pool.If(size > middle):
                        move(c)
                    with pool.Else():
                        move(b)
                with pool.Else():
                    move(a)


            def carry_wait(q, i):
                wait(pool, carried[i], q - 1)
                nc.gpsimd.tensor_tensor(carrier[:, i:i + 1], carrier[:, 2:3], carrier[:, 2:3],
                                        ALU.add).then_inc(carried[i].sem, 1)

            def get(done, i, n):
                nc.gpsimd.indirect_dma_start(
                    out=x_got[0:n, i, :], out_offset=None, in_=h2_rows,
                    in_offset=bass.IndirectOffsetOnAxis(ap=idx_next[0:n, i:i + 1], axis=0)).then_inc(done.sem, 16)

            def gather(t):
                get(gathered_a, 0, P)
                second_block(size_of(pool, t), lambda n: get(gathered_b, 1, n))

            def scatter(t):
                def put(i, n):
                    nc.gpsimd.indirect_dma_start(
                        out=out_rows, out_offset=bass.IndirectOffsetOnAxis(ap=idx_cur[0:n, i:i + 1], axis=0),
                        in_=y_rows[0:n, i, :], in_offset=None, compute_op=ALU.add).then_inc(pool_moved.sem, 16)

                put(0, P)
                second_block(size_of(pool, t), lambda n: put(1, n))

            pool.wait_ge(buffers, 1)
            wait(pool, idx_ready, 0)
            get(gathered_a, 0, P)
            get(gathered_b, 1, P)
            with job_loop(pool) as q:
                wait(pool, x_turned[3], q)
                wait(pool, idx_ready, q + 1)
                carry_wait(q, 0)
                gather(q + 1)
                wait(pool, pool_moved, q - 1)
                wait(pool, y_read[3], q)
                carry_wait(q, 1)
                scatter(q)
            pool.wait_ge(gathered_a.sem, 16)
            n = pool.value_load(jobs[0:1, 0:1], min_val=1, max_val=NE + S * TOP_K // CAP)
            wait(pool, pool_moved, n - 1)

        @block.scalar
        def _(act):
            nc.scalar.copy(iota_b[:], cst[:, C_IOTA:C_IOTA + CAP]).then_inc(counters_copied, 1)
            nc.scalar.copy(entry[:, :, 0], cst[:, C_TOK:C_TOK + NB]).then_inc(counters_copied, 1)
            nc.scalar.copy(entry[:, :, 1], cst[:, C_TOK + NB:C_TOK + 2 * NB]).then_inc(counters_copied, 1)
            for bank in (*(u[:].rearrange("p u n -> p (u n)") for u in ps_unit),
                         *(y[:].rearrange("p h u n -> p (h u n)") for y in ps_y)):
                nc.scalar.activation(bank, cst[:, 0:2 * CAP], ACT.Copy, scale=0.0).then_inc(units_cleared, 1)
            act.wait_ge(biases_read, 3)
            with job_loop(act) as q:
                e = expert_of(act, q)
                wait(act, unit_read[PIECES - 1], q - 1)
                nc.scalar.copy(b2_cur[:], b2T[:, :, bass.ds(e, 1)].rearrange("p m o -> p (m o)")).then_inc(b2_ready.sem, 1)
                for p in range(P1):
                    wait(act, glu_ready[p], q)
                    nc.scalar.activation(sig[:, p % 3, :], glu[:, p % 3, :], ACT.Sigmoid,
                                         scale=ALPHA).then_inc(sig_ready[p].sem, 1)
                wait(act, b2_ready, q)
                for p in range(P1, PIECES):
                    wait(act, unit_done[p], q)
                    for u in range(2):
                        m = 2 * (p - P1) + u
                        last = nc.scalar.activation(yT[:, m, :], ps_unit[p % 3][:, u, :], ACT.Identity,
                                                    bias=b2_cur[:, m:m + 1])
                    last.then_inc(unit_read[p].sem, 1)

        @block.vector
        def _(dve):
            v = nc.vector

            def then_wait(ins):
                rstep.did(ins)
                dve.wait_ge(rstep.sem, rstep.n)

            def match_tokens(t, e, base):
                v.tensor_scalar(place_cur[:], place[:, :, e].rearrange("p b o -> p (b o)"),
                                base, None, ALU.subtract).then_inc(place_taken.sem, 1)
                v.tensor_copy(entry[:, :, 2:5], gate_parts[:, :, :, e].rearrange("p b g o -> p b (g o)"))
                wait(dve, place_taken, t)
                for b in range(NB):
                    last = v.tensor_scalar(match[:, b, :], iota_b[:], place_cur[:, b:b + 1], None, ALU.is_equal)
                last.then_inc(matched.sem, 1)

            def read_list(t):
                wait(dve, listed, t)
                lists = ps_list[:, 0:10].rearrange("p (h f) -> p h f", h=2)
                v.tensor_copy(list_sb[:], lists).then_inc(list_read.sem, 1)
                wait(dve, list_read, t)
                v.scalar_tensor_tensor(out=idx_next[:], in0=list_sb[:, :, 0], scalar=32.0, in1=list_sb[:, :, 1],
                                       op0=ALU.mult, op1=ALU.add).then_inc(idx_ready.sem, 1)
                v.tensor_reduce(gate_next[:], list_sb[:, :, 2:5], AX_X, ALU.add).then_inc(gate_summed.sem, 1)

            then_wait(v.scalar_tensor_tensor(out=token[:], in0=cst[:, C_TOK:C_TOK + NB], scalar=32.0,
                                             in1=cst[:, C_TOK + NB:C_TOK + 2 * NB], op0=ALU.mult, op1=ALU.add))
            then_wait(v.tensor_copy(gate_parts[:, :, 0, :], gates[:]))
            then_wait(v.tensor_tensor(other[:], gates[:], gate_parts[:, :, 0, :], ALU.subtract))
            then_wait(v.tensor_copy(gate_parts[:, :, 1, :], other[:]))
            then_wait(v.tensor_tensor(gates[:], other[:], gate_parts[:, :, 1, :], ALU.subtract))
            then_wait(v.tensor_copy(gate_parts[:, :, 2, :], gates[:]))
            dve.wait_ge(ranked, 1)
            v.tensor_copy(rank[:], ps_list[:, 0:NB * NE].rearrange("p (b e) -> p b e", b=NB))
            then_wait(v.tensor_copy(counts[:], ps_list[:, NB * NE:NB * NE + NE]))
            then_wait(v.tensor_tensor(other[:], counts[:].unsqueeze(1).broadcast_to([P, NB, NE]), rank[:], ALU.subtract))
            then_wait(v.tensor_tensor(other[:], other[:], token[:].unsqueeze(2).broadcast_to([P, NB, NE]), ALU.add))
            then_wait(v.tensor_tensor(rank[:], rank[:], other[:], ALU.subtract))
            then_wait(v.tensor_tensor(rank[:], rank[:], picked[:], ALU.mult))
            then_wait(v.tensor_tensor(place[:], rank[:], other[:], ALU.add))
            dve.wait_ge(counters_copied, 3)
            match_tokens(0, slice(0, 1), 0.0)
            then_wait(v.tensor_scalar(over[:, 0, :], counts[:], float(CAP), 1.0, ALU.is_gt, ALU.add))
            for i in range(2, S // CAP):
                then_wait(v.tensor_scalar(over[:, 1, :], counts[:], float(CAP * i), None, ALU.is_gt))
                then_wait(v.tensor_tensor(over[:, 0, :], over[:, 0, :], over[:, 1, :], ALU.add))
            then_wait(v.tensor_tensor_scan(last_job[:], cst[:, C_ONES:C_ONES + NE], over[:, 0, :], 0.0, ALU.mult, ALU.add))
            read_list(0)
            job = cst[:, C_PART:C_PART + 1]
            then_wait(v.tensor_scalar(ended[:], last_job[:], job, None, ALU.is_le))
            then_wait(v.tensor_tensor(pick_e[:, 0, :], ended[:], over[:, 0, :], ALU.mult))
            v.tensor_reduce(narrow[:, 0:1], ended[:], AX_X, ALU.add)
            then_wait(v.tensor_reduce(narrow[:, 1:2], pick_e[:, 0, :], AX_X, ALU.add))
            then_wait(v.tensor_scalar(fields[:, 0:1], narrow[:, 0:1], NE - 1.0, None, ALU.min))
            then_wait(v.tensor_tensor(narrow[:, 2:3], job, narrow[:, 1:2], ALU.subtract))
            then_wait(v.tensor_scalar(fields[:, 2:3], narrow[:, 2:3], float(CAP), None, ALU.mult))
            then_wait(v.tensor_scalar(pick_e[:, 1, :], cst[:, C_E:C_E + NE], fields[:, 0:1], None, ALU.is_equal))
            then_wait(v.tensor_tensor(pick_e[:, 0, :], pick_e[:, 1, :], counts[:], ALU.mult))
            then_wait(v.tensor_reduce(narrow[:, 3:4], pick_e[:, 0, :], AX_X, ALU.add))
            then_wait(v.tensor_tensor(narrow[:, 4:5], narrow[:, 3:4], fields[:, 2:3], ALU.subtract))
            assert SIZES[:-1] == tuple(SIZES[0] + SIZE_STEP * i for i in range(last_size))
            then_wait(v.tensor_scalar(limits[:, 0, :], cst[:, C_IOTA:C_IOTA + last_size], float(SIZE_STEP), float(SIZES[0]),
                                      ALU.mult, ALU.add))
            then_wait(v.tensor_scalar(limits[:, 1, :], limits[:, 0, :], narrow[:, 4:5], None, ALU.is_lt))
            v.tensor_reduce(fields[:, 1:2], limits[:, 1, :], AX_X, ALU.add).then_inc(fields_ready, 1)
            dve.wait_ge(fields_spread, 1)
            v.tensor_copy(jobs[0:1, 0:1], last_job[0:1, NE - 1:NE]).then_inc(table_ready, 1)
            v.tensor_copy(job_row[:], ps_list[0:1, P:3 * P]).then_inc(table_ready, 1)
            v.tensor_copy(base_row[:], ps_list[:, 3 * P:4 * P]).then_inc(table_ready, 1)
            def read_xT(t, i):
                wait(dve, x_turned[i], t)
                v.tensor_copy(xT[:, 2 * i:2 * i + 2, :], ps_x[i % 2][:]).then_inc(xT_ready[i].sem, 1)

            def clip(q, p):
                wait(dve, unit_done[p], q)
                v.tensor_scalar(glu[:, p % 3, :], ps_unit[p % 3][:, 0, :], b1_cur[:, 2 * p:2 * p + 1], LIMIT,
                                ALU.add, ALU.min).then_inc(glu_ready[p].sem, 1)
                v.tensor_scalar(lin[:, p % 3, :], ps_unit[p % 3][:, 1, :], b1_cur[:, 2 * p + 1:2 * p + 2], LIMIT + 1.0,
                                ALU.add, ALU.min).then_inc(unit_read[p].sem, 1)

            def finish(q, p):
                wait(dve, sig_ready[p], q)
                v.tensor_tensor(sig[:, p % 3, :], sig[:, p % 3, :], glu[:, p % 3, :], ALU.mult).then_inc(scaled[p].sem, 1)
                wait(dve, scaled[p], q)
                v.scalar_tensor_tensor(out=act_T[:, p, :], in0=lin[:, p % 3, :], scalar=1.0 - LIMIT, in1=sig[:, p % 3, :],
                                       op0=ALU.max, op1=ALU.mult).then_inc(act_ready[p].sem, 1)

            def read_y(q, i):
                wait(dve, y_turned[i], q)
                for h in range(2):
                    last = v.tensor_scalar(y_rows[:, h, i * PW:(i + 1) * PW],
                                           ps_y[i % 2][:, h, :, :].rearrange("p u c -> p (u c)"),
                                           gate_cur[:, h:h + 1], None, ALU.mult)
                last.then_inc(y_read[i].sem, 1)

            dve.wait_ge(table_ready, 3)
            dve.wait_ge(biases_turned, 1)
            turned = ps_x[0][:].rearrange("p a b -> p (a b)").rearrange("p (j u e) -> p j u e", u=2, e=NE)
            b1_units = b1T[:].rearrange("p (j u) e -> p j u e", u=2)
            v.tensor_copy(b1_units[:, :, 0, :], turned[:, :, 0, :]).then_inc(biases_read, 1)
            v.tensor_scalar(b1_units[:, :, 1, :], turned[:, :, 1, :], 1.0, None, ALU.add).then_inc(biases_read, 1)
            v.tensor_copy(b2T[:], ps_x[1][:].rearrange("p a b -> p (a b)")[:, 0:KD * NE].rearrange(
                "p (m e) -> p m e", e=NE)).then_inc(biases_read, 1)
            for i in range(4):
                read_xT(0, i)
            dve.wait_ge(biases_read, 3)
            with job_loop(dve) as q:
                e = expert_of(dve, q)
                e_next = expert_of(dve, q + 1)
                v.tensor_copy(b1_cur[:], b1T[:, :, bass.ds(e, 1)].rearrange("p m o -> p (m o)")).then_inc(b1_ready.sem, 1)
                wait(dve, b1_ready, q)
                for p in range(P1):
                    if p >= 1:
                        finish(q, p - 1)
                    clip(q, p)
                    if p == 0:
                        match_tokens(q + 1, bass.ds(e_next, 1), base_row[:, bass.ds(q + 1, 1)])
                    if p == 3:
                        wait(dve, gate_summed, q)
                        wait(dve, pool_moved, q - 1)
                        v.tensor_copy(idx_cur[:], idx_next[:])
                        v.tensor_copy(gate_cur[:], gate_next[:]).then_inc(cur_ready.sem, 1)
                        wait(dve, cur_ready, q)
                        read_list(q + 1)
                finish(q, P1 - 1)
                for i in range(4):
                    if i >= 1:
                        read_y(q, i - 1)
                    read_xT(q + 1, i)
                read_y(q, 3)

        @block.tensor
        def _(pe):
            def list_tokens(t):
                wait(pe, matched, t)
                for h in range(2):
                    for b in range(NB):
                        last = pe.matmul(ps_list[:, 5 * h:5 * h + 5], match[:, b, h * P:(h + 1) * P], entry[:, b, :],
                                         start=(b == 0), stop=(b == NB - 1))
                last.then_inc(listed.sem, 1)

            def turn_x(t, i):
                if i == 0:
                    wait(pe, gathered_a, t)
                    wait(pe, gathered_b, t)
                if i >= 2:
                    wait(pe, xT_ready[i - 2], t)
                for c in range(2):
                    for h in range(2):
                        k = 2 * i + c
                        last = pe.transpose(ps_x[i % 2][:, c, h * P:(h + 1) * P], x_got[:, h, k * P:(k + 1) * P], ident)
                last.then_inc(x_turned[i].sem, 1)

            def turn_y(q, i, n):
                wait(pe, unit_read[P1 + i], q)
                wait(pe, y_read[(i + 2) % 4], q - 1 if i < 2 else q)
                for u in range(2):
                    for h in range(1 if n <= P else 2):
                        last = pe.transpose(ps_y[i % 2][:, h, u, :], yT[:, 2 * i + u, h * P:(h + 1) * P], ident)
                last.then_inc(y_turned[i].sem, 1)

            def piece(q, p, n):
                if p % 2 == 0:
                    wait(pe, w_loaded[p // 2], q)
                first = p % 2 * PW
                wait(pe, unit_read[(p + 9) % PIECES], q - 1 if p < 3 else q)
                for u in range(2):
                    for k in range(KD):
                        if p == 0 and u == 0 and k % 2 == 0:
                            wait(pe, xT_ready[k // 2], q)
                        if p == P1 and u == 0 and k in (0, 6, 7):
                            wait(pe, act_ready[max(k, 5)], q)
                        if p < P1:
                            w, moving = w_slot[:, p // 2, k, first + u:first + PW:2], xT
                        else:
                            w, moving = w_slot[:, p // 2, k, first + u * P:first + (u + 1) * P], act_T
                        last = pe.matmul(ps_unit[p % 3][:, u, 0:n], w, moving[:, k, 0:n],
                                         start=(k == 0), stop=(k == KD - 1))
                last.then_inc(unit_done[p].sem, 1)

            def run_job(q, n):
                for p in range(PIECES):
                    piece(q, p, n)
                    if p == 2:
                        list_tokens(q + 1)
                    if p == P1 - 1:
                        turn_x(q + 1, 0)
                        turn_x(q + 1, 1)
                        pe.reg_load(next_size, size_at(q + 1))
                    if p > P1:
                        if p == PIECES - 1:
                            turn_x(q + 1, 2)
                        turn_y(q, p - P1 - 1, n)
                turn_x(q + 1, 3)
                turn_y(q, 3, n)

            def pick_size(q, size, lo, hi):
                if hi - lo == 1:
                    run_job(q, SIZES[lo])
                    return
                mid = 1 if lo == 0 else (lo + hi) // 2
                with pe.If(size < mid):
                    pick_size(q, size, lo, mid)
                with pe.Else():
                    pick_size(q, size, mid, hi)

            pe.matmul(ps_list[:, 0:NB * NE], cst[:, C_TRI:C_TRI + P], picked[:].rearrange("p b e -> p (b e)"),
                      start=True, stop=False)
            pe.matmul(ps_list[:, 0:NB * NE], ones, before[:, 0:NB, :].rearrange("p b e -> p (b e)"),
                      start=False, stop=True)
            pe.matmul(ps_list[:, NB * NE:NB * NE + NE], ones, before[:, NB, :], start=True, stop=True).then_inc(ranked, 1)
            pe.wait_ge(pool_moved.sem, 32)
            for m in range(2 * P1):
                first = (m // 2) * PW + m % 2
                pe.transpose(ps_x[0][:].rearrange("p a b -> p (a b)")[:, m * NE:(m + 1) * NE],
                             y_rows[0:NE, :, :].rearrange("e h f -> e (h f)")[:, first:first + PW - 1:2], ident[0:NE, 0:NE])
            for m in range(KD):
                last = pe.transpose(ps_x[1][:].rearrange("p a b -> p (a b)")[:, m * NE:(m + 1) * NE],
                                    b2_rows[0:NE, m * P:(m + 1) * P], ident[0:NE, 0:NE])
            last.then_inc(biases_turned, 1)
            list_tokens(0)
            pe.wait_ge(fields_ready, 1)
            for f in range(3):
                last = pe.matmul(ps_list[:, (f + 1) * P:(f + 2) * P], fields[:, f:f + 1].broadcast_to([P, P]), ident,
                                 start=True, stop=True)
            last.then_inc(fields_spread, 1)
            pe.wait_ge(biases_read, 3)
            pe.wait_ge(units_cleared, 5)
            for i in range(4):
                turn_x(0, i)
            pe.wait_ge(table_ready, 3)
            next_size = pe.alloc_register("next_size")
            pe.reg_load(next_size, size_at(0))
            with job_loop(pe) as q:
                pick_size(q, pe.snap(next_size, min_val=0, max_val=last_size), 0, len(SIZES))


def program(nc, x, norm_mix, w_in, b_in, conv_w, q_norm, k_norm, sinks, rel_bias, out_norm_conv,
            out_norm_attn, w_out, b_out, norm_ffn, w_router, b_router, w1, b1, w2, b2, const, out):
    x_rows = x.rearrange("o s d -> (o s) d")
    out_rows = out.rearrange("o s d -> (o s) d")
    h2_rows = nc.dram_tensor("h2_rows", (S, D), F32, kind="Internal").ap()
    rel_rows = nc.dram_tensor("rel_rows", (NH, REL_W), F32, kind="Internal").ap()
    with ExitStack() as ctx:
        cst = ctx.enter_context(nc.sbuf_tensor("cst", [P, C_HOT], F32))
        picked = ctx.enter_context(nc.sbuf_tensor("picked", [P, NB, NE], F32))
        gates = ctx.enter_context(nc.sbuf_tensor("gates", [P, NB, NE], F32))
        before = ctx.enter_context(nc.sbuf_tensor("before", [P, NB + 1, NE], F32))
        mixer(nc, x_rows, out_rows, h2_rows, rel_rows, norm_mix, w_in, b_in, conv_w, q_norm, k_norm, sinks,
              rel_bias, out_norm_conv, out_norm_attn, w_out, b_out, norm_ffn, w_router, b_router, const,
              cst, picked, gates, before)
        experts(nc, h2_rows, out_rows, w1, b1, w2, b2, cst, picked, gates, before)


_INS = ["x", "norm_mix", "w_in", "b_in", "conv_w", "q_norm", "k_norm", "sinks", "rel_bias", "out_norm_conv",
        "out_norm_attn", "w_out", "b_out", "norm_ffn", "w_router", "b_router", "w1", "b1", "w2", "b2"]


def kernel(**inputs):
    import numpy as _np
    import concourse.bacc as _bacc
    from concourse import mybir as _mybir
    from concourse.bass_utils import run_bass_kernel_spmd as _run

    nc = _bacc.Bacc("TRN2", target_bir_lowering=False, num_devices=1)
    arrays, args = {}, []
    for name in _INS:
        a = _np.ascontiguousarray(inputs[name])
        arrays[f"in_{name}_dram"] = a
        args.append(nc.dram_tensor(f"in_{name}_dram", a.shape, _mybir.dt.from_np(a.dtype), kind="ExternalInput").ap())
    const = constants()
    arrays["const_dram"] = const
    args.append(nc.dram_tensor("const_dram", const.shape, F32, kind="ExternalInput").ap())
    args.append(nc.dram_tensor("out_dram", (1, S, D), F32, kind="ExternalOutput").ap())
    program(nc, *args)
    r = _run(nc, [arrays], core_ids=[0])
    return r.results[0]["out_dram"]
```
